# Optimizing a Trainium2 kernel written in Bass

```python
import jax, jax.numpy as jnp
from jax import lax
import numpy as np
import math

D_MODEL = 1024
BATCH = 1
SEQ = 256
DEPTH = 1

CTX_LEN = 256
GRID_W = 64
A_CHUNK = 2 * GRID_W
A_WIDTH = D_MODEL
A_GROUPS = 8
A_GROUP_DIM = A_WIDTH // A_GROUPS
GLA_HEADS = 4
GLA_DK = D_MODEL // 2
GLA_DV = D_MODEL
GLA_HEAD_K = GLA_DK // GLA_HEADS
GLA_HEAD_V = GLA_DV // GLA_HEADS
GLA_GATE_RANK = 16
GLA_TAU = 16.0
GLA_CHUNK = 64
N_EXPERTS = 16
N_EXPERT_GROUPS = 4
EXPERTS_PER_GROUP = N_EXPERTS // N_EXPERT_GROUPS
TOP_K = 2
D_EXPERT = 3 * D_MODEL // 2
MOE_BLOCK = 128
EPS = 1e-6
IN_SIZES = (2 * A_WIDTH, GLA_DK, GLA_DK, GLA_DV, GLA_DV, GLA_GATE_RANK, GLA_GATE_RANK, 2 * D_MODEL)
IN_COLS = sum(IN_SIZES)


def rms_norm(x, g):
    xf = x.astype(jnp.float32)
    y = xf * lax.rsqrt(jnp.mean(xf * xf, axis=-1, keepdims=True) + EPS)
    return (y * g.astype(jnp.float32)).astype(x.dtype)

def layer_norm(x, g, b):
    xf = x.astype(jnp.float32)
    mu = jnp.mean(xf, axis=-1, keepdims=True)
    xc = xf - mu
    y = xc * lax.rsqrt(jnp.mean(xc * xc, axis=-1, keepdims=True) + EPS)
    return (y * g.astype(jnp.float32) + b.astype(jnp.float32)).astype(x.dtype)

def split_cols(p):
    idx, acc = [], 0
    for s in IN_SIZES[:-1]:
        acc += s
        idx.append(acc)
    return jnp.split(p, idx, axis=-1)

def spatial_gating(z, ln_g, ln_b, w_s, b_s):
    u, v = jnp.split(z, 2, axis=-1)
    v = layer_norm(v, ln_g, ln_b)
    bsz, length, width = v.shape
    vr = v.reshape(bsz, length // A_CHUNK, A_CHUNK, A_GROUPS, A_GROUP_DIM)
    mixed = jnp.einsum('gts,bnsgc->bntgc', w_s, vr) + b_s.T[:, :, None]
    return u * mixed.reshape(bsz, length, width)

def gla_chunk_scan(q, k, v, log_a, s0):
    bsz, nh, length, _ = q.shape
    dv = v.shape[-1]
    n = length // GLA_CHUNK
    cs = lambda t: t.astype(jnp.float32).reshape(bsz, nh, n, GLA_CHUNK, t.shape[-1])
    q, k, v, log_a = cs(q), cs(k), cs(v), cs(log_a)
    b = jnp.cumsum(log_a, axis=-2)
    b_last = b[..., -1:, :]
    q_in = q * jnp.exp(b)
    k_in = k * jnp.exp(-b)
    k_st = k * jnp.exp(b_last - b)
    mask = jnp.tril(jnp.ones((GLA_CHUNK, GLA_CHUNK), dtype=bool))
    att = jnp.where(mask, jnp.einsum('bhntk,bhnsk->bhnts', q_in, k_in), 0.0)
    o_intra = jnp.einsum('bhnts,bhnsv->bhntv', att, v)

    def step(state, xs):
        qc, kc, vc, dc = xs
        o = jnp.einsum('bhtk,bhkv->bhtv', qc, state)
        state = dc[..., 0, :, None] * state + jnp.einsum('bhsk,bhsv->bhkv', kc, vc)
        return state, o

    xs = tuple(jnp.moveaxis(t, 2, 0) for t in (q_in, k_st, v, jnp.exp(b_last)))
    s_fin, o_inter = lax.scan(step, s0, xs)
    o = o_intra + jnp.moveaxis(o_inter, 0, 2)
    return o.reshape(bsz, nh, length, dv), s_fin

def gla_bidirectional(q, k, v, la_f, la_b, s_f, s_b):
    o_f, s_f = gla_chunk_scan(q, k, v, la_f, s_f)
    flip = lambda t: jnp.flip(t, axis=2)
    o_b, s_b = gla_chunk_scan(flip(q), flip(k), flip(v), flip(la_b), s_b)
    return o_f + flip(o_b), s_f, s_b

def token_mixer(h_x, h_c, w_in, w_gate2, b_gate2, gla_g, sgu_ln_g, sgu_ln_b, sgu_w, sgu_b,
                w_a, w_b, b_branch, w_out, with_ctx):
    parts_x = split_cols(h_x @ w_in)
    parts_c = split_cols(h_c @ w_in)

    def heads(t):
        bsz, length, width = t.shape
        return t.reshape(bsz, length, GLA_HEADS, width // GLA_HEADS).transpose(0, 2, 1, 3)

    def gla_inputs(parts):
        _, q, k, v, _, lr_f, lr_b, _ = parts
        la = [heads(jax.nn.log_sigmoid((lr @ w_gate2[d] + b_gate2[d]).astype(jnp.float32)) / GLA_TAU)
              for d, lr in enumerate((lr_f, lr_b))]
        return heads(q) * GLA_HEAD_K ** -0.5, heads(k), heads(v), la[0], la[1]

    zero = jnp.zeros((h_c.shape[0], GLA_HEADS, GLA_HEAD_K, GLA_HEAD_V), jnp.float32)
    o_c, s_f, s_b = gla_bidirectional(*gla_inputs(parts_c), zero, zero)
    o_x, _, _ = gla_bidirectional(*gla_inputs(parts_x), s_f, s_b)

    def merge(parts, o):
        z_a, _, _, _, r, _, _, gates = parts
        y_a = spatial_gating(jax.nn.gelu(z_a), sgu_ln_g, sgu_ln_b, sgu_w, sgu_b) @ w_a
        o_n = o * lax.rsqrt(jnp.mean(o * o, axis=-1, keepdims=True) + EPS)
        bsz, _, length, _ = o.shape
        o_n = o_n.transpose(0, 2, 1, 3).reshape(bsz, length, GLA_DV) * gla_g
        y_b = (o_n.astype(r.dtype) * jax.nn.silu(r)) @ w_b
        g_a, g_b = jnp.split(jax.nn.sigmoid(gates + b_branch), 2, axis=-1)
        return (g_a * y_a + g_b * y_b) @ w_out

    y_x = merge(parts_x, o_x)
    y_c = merge(parts_c, o_c) if with_ctx else None
    return y_x, y_c

def moe_ffn(h, w_router, b_router, w_g, w_u, w_d):
    n_tok, d = h.shape
    logits = h.astype(jnp.float32) @ w_router.astype(jnp.float32) + b_router.astype(jnp.float32)
    probs = jax.nn.softmax(logits, axis=-1).reshape(n_tok, N_EXPERT_GROUPS, EXPERTS_PER_GROUP)
    group_score = lax.top_k(probs, TOP_K)[0].sum(-1)
    g_sel = jnp.argmax(group_score, axis=-1)
    in_group = jnp.take_along_axis(probs, g_sel[:, None, None], axis=1)[:, 0]
    top_w, top_i = lax.top_k(in_group, TOP_K)
    weight = top_w / jnp.sum(top_w, axis=-1, keepdims=True)
    expert = (g_sel[:, None] * EXPERTS_PER_GROUP + top_i).reshape(-1).astype(jnp.int32)

    n_slot = n_tok * TOP_K
    token = jnp.repeat(jnp.arange(n_tok, dtype=jnp.int32), TOP_K)
    order = jnp.argsort(expert)
    e_sorted = expert[order]
    counts = jnp.bincount(expert, length=N_EXPERTS).astype(jnp.int32)
    starts = jnp.cumsum(counts) - counts
    padded = (counts + MOE_BLOCK - 1) // MOE_BLOCK * MOE_BLOCK
    p_ends = jnp.cumsum(padded)
    p_starts = p_ends - padded
    dest_sorted = p_starts[e_sorted] + jnp.arange(n_slot, dtype=jnp.int32) - starts[e_sorted]
    n_blocks = -(-n_slot // MOE_BLOCK) + N_EXPERTS
    buf_tok = jnp.full((n_blocks * MOE_BLOCK,), n_tok, jnp.int32).at[dest_sorted].set(token[order])
    block_e = jnp.minimum(jnp.searchsorted(p_ends, jnp.arange(n_blocks, dtype=jnp.int32) * MOE_BLOCK,
                                           side='right'), N_EXPERTS - 1)
    h_pad = jnp.concatenate([h, jnp.zeros((1, d), h.dtype)], axis=0)
    x_blk = h_pad[buf_tok].reshape(n_blocks, MOE_BLOCK, d)

    def expert_block(args):
        xb, e = args
        return (jax.nn.silu(xb @ w_g[e]) * (xb @ w_u[e])) @ w_d[e]

    y_blk = lax.map(expert_block, (x_blk, block_e)).reshape(-1, d)
    dest = jnp.zeros((n_slot,), jnp.int32).at[order].set(dest_sorted)
    y = y_blk[dest].reshape(n_tok, TOP_K, d) * weight[..., None].astype(h.dtype)
    return jnp.sum(y, axis=1)

def first_inputs(seed: int = 0) -> dict:
    key = jax.random.key(seed)
    ks = iter(jax.random.split(key, 32))
    nrm = lambda shape, std: jax.random.normal(next(ks), shape, jnp.float32) * std
    L = DEPTH
    return {
        "x": nrm((BATCH, SEQ, D_MODEL), 1.0),
        "c": nrm((BATCH, D_MODEL), 1.0),
        "ctx": nrm((BATCH, CTX_LEN, D_MODEL), 1.0),
        "c_ctx": nrm((D_MODEL,), 1.0),
        "w_mod": nrm((L, D_MODEL, 6 * D_MODEL), 0.5 * D_MODEL ** -0.5),
        "b_mod": nrm((L, 6 * D_MODEL), 0.01),
        "g_norm1": 1.0 + nrm((L, D_MODEL), 0.01),
        "g_norm2": 1.0 + nrm((L, D_MODEL), 0.01),
        "w_in": nrm((L, D_MODEL, IN_COLS), D_MODEL ** -0.5),
        "w_gate2": nrm((L, 2, GLA_GATE_RANK, GLA_DK), GLA_GATE_RANK ** -0.5),
        "b_gate2": nrm((L, 2, GLA_DK), 0.1),
        "gla_norm_g": 1.0 + nrm((L, GLA_DV), 0.01),
        "sgu_ln_g": 1.0 + nrm((L, A_WIDTH), 0.01),
        "sgu_ln_b": nrm((L, A_WIDTH), 0.01),
        "sgu_w": nrm((L, A_GROUPS, A_CHUNK, A_CHUNK), A_CHUNK ** -0.5),
        "sgu_b": 1.0 + nrm((L, A_GROUPS, A_CHUNK), 0.01),
        "w_branch_a": nrm((L, A_WIDTH, D_MODEL), A_WIDTH ** -0.5),
        "w_branch_b": nrm((L, GLA_DV, D_MODEL), GLA_DV ** -0.5),
        "b_branch": nrm((L, 2 * D_MODEL), 0.01),
        "w_out": nrm((L, D_MODEL, D_MODEL), D_MODEL ** -0.5),
        "w_router": nrm((D_MODEL, N_EXPERTS), D_MODEL ** -0.5),
        "b_router": nrm((N_EXPERTS,), 0.01),
        "w_exp_gate": nrm((L, N_EXPERTS, D_MODEL, D_EXPERT), D_MODEL ** -0.5),
        "w_exp_up": nrm((L, N_EXPERTS, D_MODEL, D_EXPERT), D_MODEL ** -0.5),
        "w_exp_down": nrm((L, N_EXPERTS, D_EXPERT, D_MODEL), D_EXPERT ** -0.5),
        "g_final": 1.0 + nrm((D_MODEL,), 0.01),
    }

def first_block(x, c, ctx, c_ctx, w_mod, b_mod, g_norm1, g_norm2, w_in, w_gate2, b_gate2, gla_norm_g,
              sgu_ln_g, sgu_ln_b, sgu_w, sgu_b, w_branch_a, w_branch_b, b_branch, w_out,
              w_router, b_router, w_exp_gate, w_exp_up, w_exp_down, g_final):
    bsz, seq, d = x.shape
    n_lat = bsz * seq
    for layer in range(DEPTH):
        with_ctx = layer < DEPTH - 1
        mod_x = (jax.nn.silu(c) @ w_mod[layer] + b_mod[layer])[:, None, :]
        mod_c = jax.nn.silu(c_ctx) @ w_mod[layer] + b_mod[layer]
        sh1, sc1, gt1, sh2, sc2, gt2 = jnp.split(mod_x, 6, axis=-1)
        csh1, csc1, cgt1, csh2, csc2, cgt2 = jnp.split(mod_c, 6, axis=-1)

        h_x = rms_norm(x, g_norm1[layer]) * (1.0 + sc1) + sh1
        h_c = rms_norm(ctx, g_norm1[layer]) * (1.0 + csc1) + csh1
        y_x, y_c = token_mixer(h_x, h_c, w_in[layer], w_gate2[layer], b_gate2[layer], gla_norm_g[layer],
                               sgu_ln_g[layer], sgu_ln_b[layer], sgu_w[layer], sgu_b[layer],
                               w_branch_a[layer], w_branch_b[layer], b_branch[layer], w_out[layer], with_ctx)
        x = x + gt1 * y_x

        tokens = (rms_norm(x, g_norm2[layer]) * (1.0 + sc2) + sh2).reshape(-1, d)
        if with_ctx:
            ctx = ctx + cgt1 * y_c
            h_c2 = rms_norm(ctx, g_norm2[layer]) * (1.0 + csc2) + csh2
            tokens = jnp.concatenate([tokens, h_c2.reshape(-1, d)], axis=0)
        y = moe_ffn(tokens, w_router, b_router, w_exp_gate[layer], w_exp_up[layer], w_exp_down[layer])
        x = x + gt2 * y[:n_lat].reshape(bsz, seq, d)
        if with_ctx:
            ctx = ctx + cgt2 * y[n_lat:].reshape(ctx.shape)
    return rms_norm(x, g_final)


DEPTH_2 = 2

CHUNK = 64
DN_HEADS = 8
DN_DK = 128
DN_DV = 128
DN_WIDTH = DN_HEADS * DN_DK
CONV_K = 4
SA_HEADS = 8
SA_HD = 128
SA_WIDTH = SA_HEADS * SA_HD
IDX_HEADS = 8
IDX_HD = 64
TOPK_MAX = 256
Q_BLOCK = 128
XA_HEADS = 4
XA_HD = 256
XA_WIDTH = XA_HEADS * XA_HD
N_MEM = 256
ROPE_THETA = 500000.0
ROPE_DIV = 4
D_FF = ((8 * D_MODEL // 3 + 255) // 256) * 256
N_BRANCH = 3
NORM_EPS = 1e-6

IN_SIZES_2 = (DN_WIDTH, DN_WIDTH, DN_HEADS * DN_DV, DN_HEADS * DN_DV, DN_HEADS, DN_HEADS,
            SA_WIDTH, SA_WIDTH, SA_WIDTH, IDX_HEADS * IDX_HD, IDX_HD, IDX_HEADS,
            XA_WIDTH, N_BRANCH * D_MODEL)
N_IN = sum(IN_SIZES_2)


def rmsnorm(x, g):
    xf = x.astype(jnp.float32)
    y = xf * lax.rsqrt(jnp.mean(xf * xf, axis=-1, keepdims=True) + NORM_EPS)
    return (y * g.astype(jnp.float32)).astype(x.dtype)

def l2norm(x):
    return x * lax.rsqrt(jnp.sum(x * x, axis=-1, keepdims=True) + NORM_EPS)

def rope_partial(x, positions):
    rd = x.shape[-1] // ROPE_DIV
    half = rd // 2
    inv_freq = ROPE_THETA ** (-(jnp.arange(half, dtype=jnp.float32) * 2.0 / rd))
    ang = positions.astype(jnp.float32)[..., None] * inv_freq
    cos = jnp.cos(ang)[:, :, None, :]
    sin = jnp.sin(ang)[:, :, None, :]
    xr = x[..., :rd].astype(jnp.float32)
    x1, x2 = xr[..., :half], xr[..., half:]
    rot = jnp.concatenate([x1 * cos - x2 * sin, x2 * cos + x1 * sin], axis=-1)
    return jnp.concatenate([rot.astype(x.dtype), x[..., rd:]], axis=-1)

def causal_conv(x, w):
    c = x.shape[-1]
    return lax.conv_general_dilated(x, w[:, None, :], window_strides=(1,),
                                    padding=[(CONV_K - 1, 0)],
                                    dimension_numbers=('NWC', 'WIO', 'NWC'),
                                    feature_group_count=c)

def gated_delta_rule(q, k, v, beta, g):
    b, s, h, dk = q.shape
    dv = v.shape[-1]
    n = s // CHUNK

    def chunks(t):
        return jnp.moveaxis(t.reshape((b, n, CHUNK) + t.shape[2:]), 2, 3)

    qc, kc, vc, bc, gc = (chunks(t) for t in (q, k, v, beta, g))
    gc = jnp.cumsum(gc, axis=-1)
    pos = jnp.arange(CHUNK)
    incl = pos[:, None] >= pos[None, :]
    strict = pos[:, None] > pos[None, :]
    diff = gc[..., :, None] - gc[..., None, :]
    decay = jnp.where(incl, jnp.exp(jnp.where(incl, diff, 0.0)), 0.0)
    kb = kc * bc[..., None]
    m = jnp.where(strict, jnp.einsum('bnhid,bnhjd->bnhij', kb, kc) * decay, 0.0)
    rhs = jnp.concatenate([vc * bc[..., None], kb * jnp.exp(gc)[..., None]], axis=-1)
    sol = lax.linalg.triangular_solve(m, rhs, left_side=True, lower=True, unit_diagonal=True)
    u, w = sol[..., :dv], sol[..., dv:]
    a_qk = jnp.einsum('bnhid,bnhjd->bnhij', qc, kc) * decay
    q_dec = qc * jnp.exp(gc)[..., None]
    g_last = gc[..., -1]
    k_dec = kc * jnp.exp(g_last[..., None] - gc)[..., None]
    c_dec = jnp.exp(g_last)

    def step(state, xs):
        qd, kd, a, uu, ww, cd = xs
        v_new = uu - jnp.einsum('bhck,bhkv->bhcv', ww, state)
        o = jnp.einsum('bhck,bhkv->bhcv', qd, state) + jnp.einsum('bhij,bhjv->bhiv', a, v_new)
        state = state * cd[..., None, None] + jnp.einsum('bhck,bhcv->bhkv', kd, v_new)
        return state, o

    xs = tuple(jnp.moveaxis(t, 1, 0) for t in (q_dec, k_dec, a_qk, u, w, c_dec))
    s0 = jnp.zeros((b, h, dk, dv), jnp.float32)
    _, o = lax.scan(step, s0, xs)
    return jnp.swapaxes(jnp.moveaxis(o, 0, 1), 2, 3).reshape(b, s, h, dv)

def deltanet_branch(q_in, k_in, v_in, z_in, b_in, a_in, conv_w, a_log, dt_bias, dn_norm):
    b, s, _ = q_in.shape
    f32 = jnp.float32
    qkv = jax.nn.silu(causal_conv(jnp.concatenate([q_in, k_in, v_in], axis=-1), conv_w))
    q, k, v = jnp.split(qkv, [DN_WIDTH, 2 * DN_WIDTH], axis=-1)
    q = l2norm(q.reshape(b, s, DN_HEADS, DN_DK).astype(f32)) * DN_DK ** -0.5
    k = l2norm(k.reshape(b, s, DN_HEADS, DN_DK).astype(f32))
    v = v.reshape(b, s, DN_HEADS, DN_DV).astype(f32)
    beta = jax.nn.sigmoid(b_in.astype(f32))
    g = -jnp.exp(a_log.astype(f32)) * jax.nn.softplus(a_in.astype(f32) + dt_bias.astype(f32))
    o = gated_delta_rule(q, k, v, beta, g)
    z = z_in.reshape(b, s, DN_HEADS, DN_DV).astype(f32)
    o = rmsnorm(o, dn_norm) * jax.nn.silu(z)
    return o.reshape(b, s, DN_WIDTH).astype(q_in.dtype)

def dsa_branch(q_in, k_in, v_in, iq_in, ik_in, iw_in, positions):
    b, s, _ = q_in.shape
    f32 = jnp.float32
    q = rope_partial(q_in.reshape(b, s, SA_HEADS, SA_HD), positions)
    k = rope_partial(k_in.reshape(b, s, SA_HEADS, SA_HD), positions)
    v = v_in.reshape(b, s, SA_HEADS, SA_HD)
    iq = rope_partial(iq_in.reshape(b, s, IDX_HEADS, IDX_HD), positions).astype(f32)
    ik = rope_partial(ik_in.reshape(b, s, 1, IDX_HD), positions)[:, :, 0].astype(f32)
    iw = iw_in.astype(f32) * (IDX_HEADS ** -0.5 * IDX_HD ** -0.5)
    k_sel = min(TOPK_MAX, s // 4)
    nb = s // Q_BLOCK
    key_chunk = jnp.arange(s) // CHUNK

    def blocks(t):
        return jnp.moveaxis(t.reshape((b, nb, Q_BLOCK) + t.shape[2:]), 1, 0)

    def attend(xs):
        qb, iqb, iwb, blk = xs
        q_chunk = (blk * Q_BLOCK + jnp.arange(Q_BLOCK)) // CHUNK
        score = jax.nn.relu(jnp.einsum('bthd,bsd->bths', iqb, ik))
        score = jnp.einsum('bths,bth->bts', score, iwb)
        admissible = key_chunk[None, :] <= q_chunk[:, None]
        score = jnp.where(admissible[None], score, -jnp.inf)
        _, sel = lax.top_k(score, k_sel)
        valid = (sel // CHUNK) <= q_chunk[None, :, None]
        kg = jax.vmap(lambda a, i: a[i])(k, sel)
        vg = jax.vmap(lambda a, i: a[i])(v, sel)
        logits = jnp.einsum('bthd,btkhd->bthk', qb, kg).astype(f32) * SA_HD ** -0.5
        logits = jnp.where(valid[:, :, None, :], logits, -jnp.inf)
        p = jax.nn.softmax(logits, axis=-1).astype(vg.dtype)
        return jnp.einsum('bthk,btkhd->bthd', p, vg)

    o = lax.map(attend, (blocks(q), blocks(iq), blocks(iw), jnp.arange(nb, dtype=jnp.int32)))
    return jnp.moveaxis(o, 0, 1).reshape(b, s, SA_WIDTH)

def memory_branch(q_in, mem_n, w_mem_kv):
    b, s, _ = q_in.shape
    m = mem_n.shape[1]
    mk, mv = jnp.split(mem_n @ w_mem_kv, 2, axis=-1)
    q = q_in.reshape(b, s, XA_HEADS, XA_HD)
    mk = mk.reshape(b, m, XA_HEADS, XA_HD)
    mv = mv.reshape(b, m, XA_HEADS, XA_HD)
    logits = jnp.einsum('bshd,bmhd->bhsm', q, mk).astype(jnp.float32) * XA_HD ** -0.5
    p = jax.nn.softmax(logits, axis=-1).astype(mv.dtype)
    return jnp.einsum('bhsm,bmhd->bshd', p, mv).reshape(b, s, XA_WIDTH)

def second_inputs(seed: int = 0) -> dict:
    key = jax.random.key(seed)
    ks = jax.random.split(key, 20)
    f32 = jnp.float32

    def nrm(k, shape, fan_in):
        return jax.random.normal(k, shape, f32) * fan_in ** -0.5

    def gain(k, shape):
        return 1.0 + 0.02 * jax.random.normal(k, shape, f32)

    x = jax.random.normal(ks[0], (BATCH, SEQ, D_MODEL), f32)
    mem = jax.random.normal(ks[1], (BATCH, N_MEM, D_MODEL), f32)
    offset = jax.random.randint(ks[2], (BATCH, 1), 0, 64, dtype=jnp.int32) * CHUNK
    positions = (offset + jnp.arange(SEQ, dtype=jnp.int32)[None, :]).astype(jnp.int32)
    dt = jnp.exp(jax.random.uniform(ks[3], (DEPTH_2, DN_HEADS), f32, math.log(1e-3), math.log(1e-1)))
    return {
        'x': x,
        'mem': mem,
        'positions': positions,
        'norm_mix': gain(ks[4], (DEPTH_2, D_MODEL)),
        'norm_mem': gain(ks[5], (DEPTH_2, D_MODEL)),
        'w_in': nrm(ks[6], (DEPTH_2, D_MODEL, N_IN), D_MODEL),
        'b_gate': 0.1 * jax.random.normal(ks[7], (DEPTH_2, N_BRANCH, D_MODEL), f32),
        'conv_w': nrm(ks[8], (DEPTH_2, CONV_K, 3 * DN_WIDTH), CONV_K),
        'a_log': jnp.log(jax.random.uniform(ks[9], (DEPTH_2, DN_HEADS), f32, 1.0, 16.0)),
        'dt_bias': jnp.log(jnp.expm1(dt)),
        'dn_norm': gain(ks[10], (DEPTH_2, DN_DV)),
        'w_mem_kv': nrm(ks[11], (DEPTH_2, D_MODEL, 2 * XA_WIDTH), D_MODEL),
        'w_branch': nrm(ks[12], (DEPTH_2, N_BRANCH, DN_WIDTH, D_MODEL), DN_WIDTH),
        'w_out': nrm(ks[13], (DEPTH_2, D_MODEL, D_MODEL), D_MODEL),
        'norm_ffn': gain(ks[14], (DEPTH_2, D_MODEL)),
        'w_ffn_in': nrm(ks[15], (DEPTH_2, D_MODEL, 2 * D_FF), D_MODEL),
        'w_ffn_out': nrm(ks[16], (DEPTH_2, D_FF, D_MODEL), D_FF),
        'norm_final': gain(ks[17], (D_MODEL,)),
    }

def second_block(x, mem, positions, norm_mix, norm_mem, w_in, b_gate, conv_w, a_log, dt_bias,
              dn_norm, w_mem_kv, w_branch, w_out, norm_ffn, w_ffn_in, w_ffn_out, norm_final):
    b, s, d = x.shape
    split_pts = []
    acc = 0
    for size in IN_SIZES_2[:-1]:
        acc += size
        split_pts.append(acc)
    for l in range(DEPTH_2):
        h = rmsnorm(x, norm_mix[l])
        (dq, dk, dv, dz, db, da, sq, sk, sv, iq, ik, iw, xq, gl) = jnp.split(h @ w_in[l], split_pts, axis=-1)
        o_dn = deltanet_branch(dq, dk, dv, dz, db, da, conv_w[l], a_log[l], dt_bias[l], dn_norm[l])
        o_sa = dsa_branch(sq, sk, sv, iq, ik, iw, positions)
        o_xa = memory_branch(xq, rmsnorm(mem, norm_mem[l]), w_mem_kv[l])
        gates = jax.nn.sigmoid((gl.reshape(b, s, N_BRANCH, d) + b_gate[l]).astype(jnp.float32)).astype(x.dtype)
        merged = (gates[:, :, 0] * (o_dn @ w_branch[l, 0])
                  + gates[:, :, 1] * (o_sa @ w_branch[l, 1])
                  + gates[:, :, 2] * (o_xa @ w_branch[l, 2]))
        x = x + merged @ w_out[l]
        h = rmsnorm(x, norm_ffn[l])
        gt, up = jnp.split(h @ w_ffn_in[l], 2, axis=-1)
        x = x + (jax.nn.silu(gt) * up) @ w_ffn_out[l]
    return rmsnorm(x, norm_final)


def setup_inputs(seed=0):
    out = dict(first_inputs(seed))
    for name, value in second_inputs(seed + 1).items():
        if name != "x":
            out[name + "_2"] = value
    return out


def reference(
    x, c, ctx, c_ctx, w_mod, b_mod, g_norm1, g_norm2, w_in, w_gate2, b_gate2, gla_norm_g,
    sgu_ln_g, sgu_ln_b, sgu_w, sgu_b, w_branch_a, w_branch_b, b_branch, w_out, w_router,
    b_router, w_exp_gate, w_exp_up, w_exp_down, g_final, mem_2, positions_2, norm_mix_2,
    norm_mem_2, w_in_2, b_gate_2, conv_w_2, a_log_2, dt_bias_2, dn_norm_2, w_mem_kv_2,
    w_branch_2, w_out_2, norm_ffn_2, w_ffn_in_2, w_ffn_out_2, norm_final_2,
):
    x = first_block(
        x, c, ctx, c_ctx, w_mod, b_mod, g_norm1, g_norm2, w_in, w_gate2, b_gate2, gla_norm_g,
        sgu_ln_g, sgu_ln_b, sgu_w, sgu_b, w_branch_a, w_branch_b, b_branch, w_out, w_router,
        b_router, w_exp_gate, w_exp_up, w_exp_down, g_final,
    )
    return second_block(
        x, mem_2, positions_2, norm_mix_2, norm_mem_2, w_in_2, b_gate_2, conv_w_2, a_log_2,
        dt_bias_2, dn_norm_2, w_mem_kv_2, w_branch_2, w_out_2, norm_ffn_2, w_ffn_in_2,
        w_ffn_out_2, norm_final_2,
    )


_drawn_inputs = setup_inputs


def setup_inputs(seed=0):
    import zlib

    import numpy as np

    out = dict(_drawn_inputs(seed))
    spreads = {}
    factors = {'g_norm1': 2.859,
     'b_gate2': 3.742,
     'gla_norm_g': 5.618,
     'sgu_ln_g': 8.0,
     'sgu_ln_b': 5.76,
     'sgu_b': 6.18,
     'b_branch': 8.0,
     'norm_mem_2': 8.0,
     'dn_norm_2': 13.623,
     'norm_final_2': 8.02,
     'g_norm2': 3.353,
     'b_router': 2.779,
     'norm_ffn_2': 5.645}
    for name, (base, spread) in spreads.items():
        noise = np.random.default_rng([zlib.crc32(name.encode()), seed]).standard_normal(out[name].shape)
        drawn = base * np.exp(spread * noise) if base else spread * noise
        out[name] = __import__('jax').numpy.asarray(drawn.astype(out[name].dtype))
    for name, factor in factors.items():
        out[name] = (out[name] * factor).astype(out[name].dtype)
    return out
```

```python
import numpy as np
import concourse.bass as bass
from concourse import mybir
from contextlib import ExitStack

F32 = mybir.dt.float32
F32R = mybir.dt.float32r
I32 = mybir.dt.int32
AF = mybir.ActivationFunctionType
OP = mybir.AluOpType
AX = mybir.AxisListType

T = 256
KT = 8
BASE = 16512

COLS = [("c", 8), ("c_ctx", 8), ("b_mod", 48), ("g_norm1", 8), ("g_norm2", 8), ("b_gate2", 8),
        ("gla_norm_g", 8), ("sgu_ln_g", 8), ("sgu_ln_b", 8), ("b_branch", 16), ("g_final", 8),
        ("norm_mix_2", 16), ("norm_mem_2", 16), ("b_gate_2", 48), ("conv_w_2", 192), ("dn_norm_2", 2),
        ("norm_ffn_2", 16), ("norm_final_2", 8)]
COL = {}
for _n, _c in COLS:
    COL[_n] = sum(c for _, c in COLS[:len(COL)])
NCOL = sum(c for _, c in COLS)

MASKS = ["one", "eye", "le", "ge", "lt", "gt"]


def constants():
    p, f = np.meshgrid(np.arange(128), np.arange(128), indexing="ij")
    m = {"one": p >= 0, "eye": p == f, "le": p <= f, "ge": p >= f, "lt": p < f, "gt": p > f}
    small = np.zeros((128, 128), np.float32)
    small[:, 0] = 1e-6
    small[:, 1] = np.pi / 2
    small[:, 16:32] = 16.0 - np.arange(16)
    small[:, 32:36] = 4.0 - np.arange(4)
    small[:, 36:40] = 64.0 * np.arange(4)
    small[:, 64:128] = np.arange(64)
    return np.concatenate([m[n].astype(np.float32) for n in MASKS] + [small], axis=1)


class Tok:

    def __init__(self, sem=None, count=0):
        self.sem, self.count, self.used = sem, count, False


def flat(waits):
    for w in waits:
        if isinstance(w, Tok):
            yield w
        elif w is not None:
            yield from flat(w)


class Stream:

    def __init__(self, sem):
        self.sem, self.q = sem, []

    def do(self, fn, *waits, tok=None):
        t, ws = tok or Tok(), list(flat(waits))
        for w in ws:
            w.used = True
        self.q.append((fn, ws, t))
        return t

    def count(self):
        n = 0
        for _, _, t in self.q:
            if t.used and t.sem is None:
                n += 1
                t.sem, t.count = self.sem, n

    def emit(self, e):
        seen = {}
        for fn, ws, t in self.q:
            for w in ws:
                if seen.get(w.sem.name, 0) < w.count:
                    e.wait_ge(w.sem, w.count)
                    seen[w.sem.name] = w.count
            i = fn(e)
            if t.sem is self.sem:
                i.then_inc(self.sem, 1)


class Bank:

    def __init__(self, t):
        self.t, self.free = t, []


class Part:

    def __init__(self, hi, lo):
        self.hi, self.lo, self.tok = hi, lo, {}


class Slot:
    def __init__(self, t, sem, i):
        self.t, self.sem, self.n, self.i = t, sem, 0, i


class Quarter:

    def __init__(self, hi, lo, th, tl, b):
        self.hi, self.lo, self.th, self.tl, self.b = hi, lo, th, tl, b


class Program:
    NB = 3
    SLOT = 4096

    def __init__(self, nc, A, ctx):
        self.nc, self.A, self.ctx = nc, A, ctx
        self.pe, self.act, self.dve, self.pool, self.sp = (
            Stream(self.sem("done_" + n)) for n in ("pe", "act", "dve", "pool", "sp"))
        self.nload = 0
        ctx.enter_context(nc.sbuf_tensor("arena", [128, 53200], F32))
        self.banks = [Bank(ctx.enter_context(nc.psum_tensor(f"bank{i}", [128, 512], F32))) for i in range(8)]

        self.pf = self.at("pf", 0, [NCOL])
        self.cst = self.at("cst", 448, [7 * 128])
        self.x = self.at("x", 1536, [KT, T])
        self.small = self.at("small", 3584, [512])
        hl = 4096
        self.hib = [self.at(f"hib{i}", hl + 2048 * i, [1024], F32R) for i in range(self.NB)]
        self.lob = [self.at(f"lob{i}", hl + 2048 * i + 1024, [1024], F32R) for i in range(self.NB)]
        self.R0 = hl + 2048 * self.NB
        self.Z = self.R0 + 3 * self.SLOT
        self.mask = {n: self.cst[:, 128 * i:128 * i + 128] for i, n in enumerate(MASKS)}
        self.ONE, self.EYE = self.mask["one"], self.mask["eye"]
        self.sm = self.cst[:, 128 * len(MASKS):128 * len(MASKS) + 128]
        self.EPS = self.sm[:, 0:1]

        self.want_, self.held, self.idle, self.lastslot = [], {}, [], {}
        self.todo, self.nq, self.nsplit, self.ahead, self.rot = [], 0, 0, 0, 0
        self.pe_read = [[] for _ in range(self.NB)]
        self.sides = []

    def sem(self, n):
        return self.ctx.enter_context(self.nc.semaphore(n))

    def at(self, name, off, shape, dt=F32):
        return self.nc.alloc_sbuf_tensor_at(name, [128] + shape, dt, offset=BASE + 4 * off)

    def col(self, n, i=0, k=1):
        return self.pf[:, COL[n] + i:COL[n] + i + k]

    def mm(self, out, l, r, start, stop, *w):
        return self.pe.do(lambda e: e.matmul(out, l, r, start=start, stop=stop, skip_group_check=True), *w)

    def tp(self, out, i, *w):
        k = i.shape[0]
        p0 = 0
        return self.pe.do(lambda e: e.transpose(out, i, self.EYE[0:k, 0:k]), *w)

    def af(self, out, i, func, *w, bias=0.0, scale=1.0, accum=None):
        return self.act.do(lambda e: e.activation(out, i, func, bias=bias, scale=scale, accum_out=accum), *w)

    def acp(self, out, i, *w):
        return self.act.do(lambda e: e.copy(out, i), *w)

    def tt(self, out, a, b, op, *w, on=None):
        return (on or self.dve).do(lambda e: e.tensor_tensor(out, a, b, op), *w)

    def ts(self, out, a, s1, s2, o1, o2, *w, on=None):
        if s2 is None:
            return (on or self.dve).do(lambda e: e.tensor_scalar(out, a, s1, None, o1), *w)
        return (on or self.dve).do(lambda e: e.tensor_scalar(out, a, s1, s2, o1, o2), *w)

    def stt(self, out, a, s, b, o1, o2, *w, rev1=False):
        return self.dve.do(lambda e: e.scalar_tensor_tensor(
            out=out, in0=a, scalar=s, in1=b, op0=o1, op1=o2, reverse1=rev1), *w)

    def cp(self, out, i, *w, on=None):
        return (on or self.dve).do(lambda e: e.tensor_copy(out, i), *w)

    def rcp(self, out, i, *w):
        return self.dve.do(lambda e: e.reciprocal(out, i), *w)

    def red(self, out, i, op, *w):
        return self.dve.do(lambda e: e.tensor_reduce(out, i, AX.X, op), *w)

    def fill(self, out, v, *w, on=None):
        return (on or self.dve).do(lambda e: e.memset(out, v), *w)

    def raw(self, stream, fn, *w):
        stream.do(fn, *w)

    def load(self, out, src, *w, q=None):
        self.nload += 1
        s = self.sem(f"load{self.nload}")
        return (q or self.sp).do(lambda e: e.dma_start(out, src).then_inc(s, 16), *w, tok=Tok(s, 16))

    def add_slot(self, i, off, *free):
        s = Slot(self.at(f"slot{i}", off, [self.SLOT]), self.sem(f"ring{i}"), i)
        self.idle.append((s, list(flat(free))))
        self.pump()

    def pump(self):
        while self.want_ and self.idle:
            key, parts, zone = self.want_[0]
            k = next((j for j, (s, _) in enumerate(self.idle) if s.i < zone), None)
            if k is None:
                return
            s, free = self.idle.pop(k)
            self.want_.pop(0)
            for view, src in parts:
                s.n += 16
                self.sp.do(lambda e, o=view(s.t), i=src, s=s: e.dma_start(o, i).then_inc(s.sem, 16), free,
                           tok=Tok(s.sem, s.n))
            self.held[key] = (s, Tok(s.sem, s.n))

    def want(self, key, parts, zone=3):
        self.want_.append((key, parts, zone))
        self.pump()

    def release(self, key, *read):
        s, _ = self.held.pop(key)
        self.idle.append((s, list(flat(read))))
        self.pump()

    @staticmethod
    def block(w, c0, n=512, k0=0, kt=8, o=0):
        return (lambda t: t[:, o:o + kt * n].rearrange("p (k n) -> p k n", k=kt),
                w[128 * k0:128 * (k0 + kt), c0:c0 + n].rearrange("(k p) n -> p k n", p=128))

    def split_w(self, src, k, ld):
        b = self.nq % self.NB
        self.nq += 1
        hi = self.hib[b][:].rearrange("p (k n) -> p k n", k=k)
        lo = self.lob[b][:].rearrange("p (k n) -> p k n", k=k)
        n = src.shape[-1]
        hi, lo = hi[:, :, 0:n], lo[:, :, 0:n]
        th = self.acp(hi, src, ld, self.pe_read[b])
        tl = self.tt(lo, src, hi.bitcast(F32), OP.subtract, ld, th, self.pe_read[b])
        return Quarter(hi, lo, th, tl, b)

    def split_x(self, part, k, src, *w):
        th = self.acp(part.hi[:, k, :], src, *w)
        tl = self.tt(part.lo[:, k, :], src, part.hi[:, k, :].bitcast(F32), OP.subtract, th, *w)
        part.tok[k] = [th, tl]

    def bank(self):
        self.rot += 1
        return self.banks[self.rot % 3]

    def plain(self, key, fn):
        self.todo.append(("plain", key, fn))

    def call(self, fn):
        self.todo.append(("call", fn))

    def source(self, key, src, ld, k, fn):
        self.held[key] = (None, ld)
        self.todo.append(["quarter", key, k, lambda s: src, False, fn, None])

    def quarter(self, key, k, view, last, fn):
        self.todo.append(["quarter", key, k, view, last, fn, None])

    def step(self):
        for t in self.todo:
            if self.ahead == self.NB:
                break
            if t[0] != "quarter" or t[6] is not None:
                continue
            if t[1] not in self.held:
                break
            s, ld = self.held[t[1]]
            t[6] = q = self.split_w(t[3](s and s.t), t[2], ld)
            self.ahead += 1
            if t[4]:
                self.release(t[1], q.th, q.tl)
        t = self.todo.pop(0)
        if t[0] == "call":
            t[1]()
        elif t[0] == "plain":
            s, ld = self.held[t[1]]
            self.release(t[1], t[2](s.t, ld))
        else:
            self.ahead -= 1
            self.pe_read[t[6].b] = [t[5](t[6])]

    def unit(self, key, c0, n, xs, tm, evac, last, view=None):
        st = {}

        def part(h):
            def f(q):
                if h == 0:
                    st["b"] = [self.bank() for _ in xs]
                t = None
                for j, (xp, bk) in enumerate(zip(xs, st["b"])):
                    first = h == 0
                    for g in range(2 if tm else n // 128):
                        gs = slice(128 * g, 128 * g + 128)
                        for k in range(4):
                            kk = 4 * h + k
                            for w, v, wt in ((q.hi, xp.hi, q.th), (q.hi, xp.lo, q.th), (q.lo, xp.hi, q.tl)):
                                l, r = (v[:, kk, gs], w[:, k, :]) if tm else (w[:, k, gs], v[:, kk, :])
                                t = self.mm(bk.t[:, 256 * g:256 * g + (n if tm else 256)], l, r, first,
                                            h == 1 and k == 3, wt, xp.tok[kk], bk.free if first else None)
                                first = False
                    if h == 1:
                        bk.free = list(flat([evac(xp, bk.t, c0, t)]))
                return t
            return f

        view = view or (lambda s: s[:, 0:4096].rearrange("p (k n) -> p k n", k=8))
        for h in range(2):
            self.quarter(key, 4, lambda s, h=h: view(s)[:, 4 * h:4 * h + 4, c0:c0 + n], last and h == 1, part(h))

    def unit_at(self, key, o, n, xs, evac, c0, last):
        self.unit(key, 0, n, xs, False, lambda xp, b, c, t: evac(xp, b, c0, t), last,
                  view=lambda s: s[:, o:o + 8 * n].rearrange("p (k n) -> p k n", k=8))

    def units(self, key, w, c0, xs, tm, evac):
        self.want(key, [self.block(w, c0)])
        for u in range(2):
            self.unit(key, 256 * u, 256, xs, tm, lambda xp, b, c, t: evac(xp, b, c0 + c, t), u == 1)

    def side_step(self):
        while self.sides:
            try:
                next(self.sides[0])
                return True
            except StopIteration:
                self.sides.pop(0)
        return False

    def run(self, ratio=1):
        while self.todo:
            self.step()
            for _ in range(ratio):
                self.side_step()

    @staticmethod
    def need(done, *keys):
        while any(k not in done for k in keys):
            yield

    def until(self, done, *keys):
        def f():
            while any(k not in done for k in keys):
                if not self.side_step():
                    assert all(k in done for k in keys), keys
        self.call(f)

    def drain(self):
        while self.side_step():
            pass

    def finish(self, *last):
        self.sp.do(lambda e: e.nop(), *last)
        streams = dict(sync=self.sp, tensor=self.pe, scalar=self.act, vector=self.dve, gpsimd=self.pool)
        for s in streams.values():
            s.count()
        with self.nc.Block() as block:
            block.sync(lambda e: self.sp.emit(e))
            block.tensor(lambda e: self.pe.emit(e))
            block.scalar(lambda e: self.act.emit(e))
            block.vector(lambda e: self.dve.emit(e))
            block.gpsimd(lambda e: self.pool.emit(e))


def bc(a, n, axis):
    a = a.unsqueeze(axis)
    s = list(a.shape)
    s[axis] = n
    return a.to_broadcast(s)


def phase_a(P):
    A, Z = P.A, P.Z
    mm, tp, af, acp, tt, ts, stt, cp, rcp, fill = P.mm, P.tp, P.af, P.acp, P.tt, P.ts, P.stt, P.cp, P.rcp, P.fill
    col, sm, ONE, EYE, EPS, x = P.col, P.sm, P.ONE, P.EYE, P.EPS, P.x
    LE, GE = P.mask["le"], P.mask["ge"]
    B = P.banks

    off = [Z]

    def new(name, shape, dt=F32):
        n = int(np.prod(shape))
        off[0] += n
        assert off[0] <= 53200, name
        return P.at(name, off[0] - n, shape, dt), off[0] - n

    hx = Part(new("hx_hi", [KT, T], F32R)[0], new("hx_lo", [KT, T], F32R)[0])
    hc_hi, HC = new("hc_hi", [KT, T], F32R)
    hc = Part(hc_hi, new("hc_lo", [KT, T], F32R)[0])
    ctx, CX = new("ctx", [KT, T])
    kx, QK = new("kx", [4, T])
    qx = new("qx", [4, T])[0]
    vx = new("vx", [2, 1024])[0]
    kc, KC = new("kc", [4, T])
    vc, VC = new("vc", [2, 1024])
    la, LA = new("la", [2, 4, T])
    lc, LC = new("lc", [2, 4, T])
    zv, ZV = new("zv", [2, 1024])
    u, UU = new("u", [KT, T])
    wg2 = new("wg2", [512])[0]
    wlr = new("wlr", [KT, 128])[0]
    sguw = new("sguw", [8, 128])[0]
    sgub = new("sgub", [8, 128])[0]
    lr, _ = new("lr", [2, T])
    cs, _ = new("cs", [KT, 32])
    md0, MD = new("md0", [16, 32])
    md1, md2 = P.at("md1", MD, [16, 32]), None
    lnr = P.at("lnr", HC, [2, 1024])
    gt_tmp = HC + 2048
    gates = P.at("gates", HC, [16, T])
    bb = P.at("bb", CX, [2, 4, T])
    rr = P.at("rr", CX, [KT, T])
    sgu_hi = P.at("sgu_hi", ZV, [KT, T], F32R)
    sgu = Part(sgu_hi, P.at("sgu_lo", UU, [KT, T], F32R))
    o = P.at("o", VC, [4, 2, T])
    ob = Part(P.at("ob_hi", LA, [KT, T], F32R), P.at("ob_lo", VC, [KT, T], F32R))
    m = P.at("m", LC, [KT, T])
    mp = Part(P.at("m_hi", QK, [KT, T], F32R), P.at("m_lo", LC, [KT, T], F32R))
    mod = P.small[:, 0:64]
    sqx = P.at("sqx", UU, [KT, T])
    sqc = P.at("sqc", ZV, [KT, T])
    rsx = P.at("rsx", LC, [T])
    rsc = P.at("rsc", LC + T, [T])
    ht = P.at("ht", LA, [KT, T])

    l_pf = P.load(P.pf[:], A["cols"])
    l_cst = P.load(P.cst[:], A["cst"])
    l_x = P.load(x[:], A["xT"])
    for i in range(4):
        P.want(("mod", 0, i), [(lambda t: t[:, 0:4096].rearrange("p (k n) -> p k n", k=2),
                               A["w_mod"][256 * i:256 * i + 256, 0:2048].rearrange("(k p) n -> p k n", p=128))])
    for i in range(3):
        P.add_slot(i, P.R0 + P.SLOT * i)
    l_ctx = P.load(ctx[:], A["ctxT"])

    f_lr = fill(wlr[:], 0.0, on=P.pool)
    f_g2 = fill(wg2[0:64, :], 0.0, on=P.pool)
    f_cs = fill(cs[:], 0.0, on=P.pool)
    l_lr = [P.load(wlr[:, :, 32 * d:32 * d + 16], A["w_lr"][:, :, 16 * d:16 * d + 16], f_lr) for d in range(2)]
    l_g2 = [P.load(wg2[32 * d:32 * d + 16, :], A["w_gate2"][d], f_g2) for d in range(2)]

    c0 = af(cs[:, :, 0], col("c", 0, 8), AF.Silu, l_pf, f_cs)
    c1 = af(cs[:, :, 1], col("c_ctx", 0, 8), AF.Silu, l_pf, f_cs)
    bank_mod = B[3]

    def mod_part(g, i):
        def f(s, ld):
            t = None
            w = s[:, 0:4096].rearrange("p (k t j n) -> p k t j n", k=2, t=16, j=4)
            for k in range(2):
                for j in range(4):
                    t = mm(bank_mod.t[32 * j:32 * j + 32, :].rearrange("p (t n) -> p t n", t=16),
                           cs[:, 2 * i + k, :], w[:, k, :, j, :], i == 0 and k == 0, i == 3 and k == 1,
                           ld, c1, c0, bank_mod.free if i == 0 else None)
            mods[g] = t
            return t
        return f

    mods, modcol = {}, {}

    def mod_done(g, md, *w):
        t = P.dve.do(lambda e: e.transpose(md[:].rearrange("p t n -> p (t n)"), bank_mod.t[:, :]), mods[g], *w)
        bank_mod.free = [t]
        return t

    def rstd(src, sq, out, bank, ld):
        t = af(sq[:], src, AF.Square, ld)
        for k in range(KT):
            t2 = mm(bank.t[:, 0:T], ONE, sq[:, k, :], k == 0, k == KT - 1, t, l_cst)
        t = af(out[:], bank.t[:, 0:T], AF.Sqrt, t2, bias=EPS, scale=1.0 / 1024)
        bank.free = [t]
        return rcp(out[:], out[:], t)

    t_rx = rstd(x[:], sqx, rsx, B[4], l_x)
    t_rc = rstd(ctx[:], sqc, rsc, B[5], l_ctx)
    for i in range(4):
        P.plain(("mod", 0, i), mod_part(0, i))
    nx = P.at("nx", UU, [KT, T])
    ncx = P.at("ncx", ZV, [KT, T])
    t_nx = tt(nx[:], x[:], bc(rsx[:], KT, 1), OP.mult, t_rx)
    t_nc = tt(ncx[:], ctx[:], bc(rsc[:], KT, 1), OP.mult, t_rc)
    P.run(0)
    t = mod_done(0, md0)
    sc = mod.rearrange("p (a k r) -> p a k r", a=4, k=8)[:, 0:2]
    t1 = tt(sc[:, 1], md0[:, 0:8, 0:2], bc(col("b_mod", 0, 8), 2, 2), OP.add, t)
    t0 = tt(sc[:, 0], md0[:, 8:16, 0:2], bc(col("b_mod", 8, 8), 2, 2), OP.add, t)
    t0 = stt(sc[:, 0], sc[:, 0], 1.0, bc(col("g_norm1", 0, 8), 2, 2), OP.add, OP.mult, t0)
    for r, (src, part, tn) in enumerate(((nx, hx, t_nx), (ncx, hc, t_nc))):
        for k in range(KT):
            t = ts(src[:, k, :], src[:, k, :], sc[:, 0, k, r:r + 1], sc[:, 1, k, r:r + 1], OP.mult, OP.add, tn, t0, t1)
            P.split_x(part, k, src[:, k, :], t)

    w_in = A["w_in"]
    done = {}
    pa = lambda a: a.rearrange("p a t -> p (a t)")

    def ev_k(xp, b, c, t):
        j = (c - 2560) // 128
        done["k", xp is hx, j // 2] = r = acp(pa((kx if xp is hx else kc)[:, j:j + 2, :]), b[:], t)
        return r

    def ev_v(xp, b, c, t):
        c -= 3072
        done["v", xp is hx, c // 256] = r = cp((vx if xp is hx else vc)[:, :, c:c + 256],
                                              b[:].rearrange("p (a n) -> p a n", a=2), t)
        return r

    def ev_q(xp, b, c, t):
        j = (c - 2048) // 128
        done["q", j // 2] = r = af(pa(qx[:, j:j + 2, :]), b[:], AF.Copy, t, scale=128 ** -0.5)
        return r

    def ev_zv(xp, b, c, t):
        done["zv", (c - 1024) // 256] = r = af(zv[:, :, c - 1024:c - 768], b[:].rearrange("p (a n) -> p a n", a=2),
                                              AF.Gelu_apprx_tanh, t, done["decay"])
        return r

    def ev_u(xp, b, c, t):
        done["u", c // 256] = r = af(pa(u[:, c // 128:c // 128 + 2, :]), b[:], AF.Gelu_apprx_tanh, t, done["gla"])
        return r

    def ev_r(xp, b, c, t):
        j = (c - 4096) // 128
        done["r", j // 2] = r = af(pa(rr[:, j:j + 2, :]), b[:], AF.Silu, t, done["gla"])
        return r

    def ev_g(xp, b, c, t):
        j = (c - 5152) // 128
        for a in range(2):
            r = af(gates[:, j + a, :], b[:, 256 * a:256 * a + 256], AF.Sigmoid, t, done["ln"], done["gla"],
                   bias=col("b_branch", j + a))
        done["g", j // 2] = r
        return r

    def need(*keys):
        while any(k not in done for k in keys):
            yield

    def lr_part(q):
        t = None
        for r, (xp, bk) in enumerate(((hx, P.bank()), (hc, P.bank()))):
            for k in range(KT):
                for w, v, wt in ((q.hi, xp.hi, q.th), (q.hi, xp.lo, q.th), (q.lo, xp.hi, q.tl)):
                    t = mm(bk.t[:, 0:T], w[:, k, :], v[:, k, :], k == 0 and w is q.hi and v is xp.hi,
                           k == KT - 1 and w is q.lo, wt, xp.tok[k], bk.free)
            done["lr", r] = acp(lr[0:64, r, :], bk.t[0:64, 0:T], t)
            bk.free = [done["lr", r]]
        return t

    gtmp = P.at("gtmp", ZV, [2, 4, T])
    gl = P.at("gl", UU, [8, T])
    S16 = 1.0 / 16

    def decays(r, dst, w):
        for d in range(2):
            tmp = gtmp[:, d]
            ta, tn = [], []
            for g in range(2):
                bk = B[4 + 2 * d + g]
                for a in range(2):
                    h = 2 * g + a
                    t = mm(bk.t[:, 256 * a:256 * a + 256], wg2[32 * d:32 * d + 32, 128 * h:128 * h + 128],
                           lr[32 * d:32 * d + 32, r, :], a == 0, a == 1, done["lr", r], l_g2, bk.free if a == 0 else None)
                for a in range(2):
                    h = 2 * g + a
                    src = bk.t[:, 256 * a:256 * a + 256]
                    ta.append(af(tmp[:, h, :], src, AF.Abs, t, w, bias=col("b_gate2", 4 * d + h)))
                for a in range(2):
                    h = 2 * g + a
                    src = bk.t[:, 256 * a:256 * a + 256]
                    tn.append(ts(dst[:, d, h, :], src, col("b_gate2", 4 * d + h), 0.0, OP.add, OP.min, ta[-1], w))
                bk.free = [tn[-1]]
            t = af(tmp, tmp, AF.Exp, ta, scale=-1.0)
            t = af(tmp, tmp, AF.Ln, t, bias=ONE[:, 0:1])
            done["la", r, d] = tt(dst[:, d], dst[:, d], tmp, OP.subtract, t, tn)
            yield
            w = [w, done["la", r, d]]

    def ctx_state(d, h, i):
        e, kt = gl[:, 2 * i, :], gl[:, 2 * i + 1, :].rearrange("p (a n) -> p a n", a=2)
        L = lc[:, d, h, :]
        w = done["la", 1, d]
        t = P.dve.do(lambda s: s.tensor_tensor_scan(e, L, L, 0.0, OP.add, OP.bypass), w, gfree[i])
        if d == 0:
            t = ts(P.small[:, 64 + i:65 + i], e[:, T - 1:T], S16, None, OP.mult, None, t, gfree[i])
            t = af(e, e, AF.Exp, t, bias=P.small[:, 64 + i:65 + i], scale=-S16)
        else:
            t = tt(e, e, L, OP.subtract, t)
            t = af(e, e, AF.Exp, t, scale=S16)
        t = tt(e, e, kc[:, h, :], OP.mult, t, done["k", False, h // 2])
        bk = B[4 + i % 4]
        for a in range(2):
            t2 = tp(bk.t[:, 128 * a:128 * a + 128], e[:, 128 * a:128 * a + 128], t, bk.free, l_cst)
        yield
        t = acp(kt, bk.t[:, 0:256].rearrange("p (a n) -> p a n", a=2), t2, gfree[i])
        for a in range(2):
            t2 = mm(bk.t[:, 256:512], kt[:, a, :], vc[:, a, 256 * h:256 * h + 256], a == 0, a == 1, t, bk.free,
                    done["v", False, h])
        yield
        done["s", d, h] = cp(L, bk.t[:, 256:512], t2)
        bk.free = [done["s", d, h]]
        gfree[i] = [done["s", d, h]]

    gfree = [[t_h for t_h in hx.tok[KT - 1]] for _ in range(4)]
    tm_ = {}

    def x_head(h):
        q, k = qx[:, h, :], kx[:, h, :]
        c2 = lambda a: a.rearrange("p (c n) -> p c n", c=2)
        fr = gfree[0]
        qm, km, qi = ([gl[:, 3 * d + i, :] for d in range(2)] for i in range(3))
        kst = [gl[:, 6, 128 * d:128 * d + 128] for d in range(2)]
        att = gl[:, 7, :]
        tq, tk, ti, tst = [], [], [], []
        for d in range(2):
            for c in range(2):
                b = bb[:, d, h, 128 * c:128 * c + 128]
                cc = slice(128 * c, 128 * c + 128)
                nm, pm = (sc_mid[i][:, d, h, c:c + 1] for i in range(2))
                tq.append(af(qm[d][:, cc], b, AF.Exp, done["bb"], fr, bias=nm, scale=S16))
                tk.append(af(km[d][:, cc], b, AF.Exp, done["bb"], fr, bias=pm, scale=-S16))
            ti.append(af(qi[d], bb[:, d, h, :], AF.Exp, done["bb"], fr, scale=S16))
            tst.append(af(kst[d], bb[:, d, h, 128 * d:128 * d + 128], AF.Exp, done["bb"], fr,
                          bias=sc_tot[:, d, h, d:d + 1], scale=-S16))
        yield
        wk, wq = done["k", True, h // 2], done["q", h // 2]
        mq, mk, mi, ms = [], [], [], []
        for d in range(2):
            mq.append(tt(qm[d], qm[d], q, OP.mult, tq, wq))
            mk.append(tt(km[d], km[d], k, OP.mult, tk, wk))
            ms.append(tt(kst[d], kst[d], k[:, 128 * d:128 * d + 128], OP.mult, tst, wk))
            mi.append(tt(qi[d], qi[d], q, OP.mult, ti, wq))
        b4, b5, b6, b7 = B[4], B[5], B[6], B[7]
        for d in range(2):
            for c in range(2):
                cc = slice(128 * c, 128 * c + 128)
                t = mm(b4.t[:, 256 * d + 128 * c:256 * d + 128 * c + 128], km[d][:, cc], qm[d][:, cc], d == 0 and c == 0,
                       d == 1 and c == 1, mq[d], mk[d], b4.free)
        for d in range(2):
            t2 = tp(b5.t[:, 128 * d:128 * d + 128], kst[d], ms[d], b5.free)
        yield
        t_kt = acp(gl[:, 6, :], b5.t[:, 0:256], t2)
        t1 = tt(c2(att), b4.t[:, 0:256].rearrange("p (c n) -> p c n", c=2), bc(LE, 2, 1), OP.mult, t, fr)
        t3 = tt(c2(km[0]), b4.t[:, 256:512].rearrange("p (c n) -> p c n", c=2), bc(GE, 2, 1), OP.mult, t)
        t_att = tt(att, att, km[0], OP.add, t1, t3)
        b4.free = [t1, t3]
        for d in range(2):
            t = mm(b5.t[:, 256:512] if d == 0 else b6.t[:, 0:256], kst[d], vx[:, d, 256 * h:256 * h + 256], True, True,
                   t_kt, b6.free, done["v", True, h])
            S1 = km[1] if d == 0 else qm[1]
            t = stt(S1, lc[:, d, h, :], sc_dec[:, d, h, d:d + 1], b5.t[:, 256:512] if d == 0 else b6.t[:, 0:256],
                    OP.mult, OP.add, t, done["s", d, h], t1, t3)
            (b5 if d == 0 else b6).free = [t, t_kt]
            tm_[d] = t
        first = True
        for j in range(2):
            js = slice(128 * j, 128 * j + 128)
            for c in range(2):
                cc = slice(128 * c, 128 * c + 128)
                out = b7.t[:, 256 * j + 128 * c:256 * j + 128 * c + 128]
                mm(out, vx[:, c, 256 * h + 128 * j:256 * h + 128 * j + 128], att[:, cc], first, False, t_att, b7.free)
                first = False
                mm(out, lc[:, c, h, js], qi[c][:, cc], False, False, mi[c], done["s", c, h])
        yield
        for j in range(2):
            js = slice(128 * j, 128 * j + 128)
            for c in range(2):
                cc = slice(128 * c, 128 * c + 128)
                S1 = km[1] if c == 1 else qm[1]
                t = mm(b7.t[:, 256 * j + 128 * c:256 * j + 128 * c + 128], S1[:, js], qi[1 - c][:, cc], False,
                       j == 1 and c == 1, tm_[0], tm_[1])
        yield
        t_o = acp(pa(o[:, h]), b7.t[:], t, done["ctx"])
        sq = [km[0], qm[0]]
        for j in range(2):
            t_s = af(sq[j], b7.t[:, 256 * j:256 * j + 256], AF.Square, t)
        b7.free = [t_s]
        for j in range(2):
            t = mm(b4.t[:, 0:T], ONE, sq[j], j == 0, j == 1, t_s, b4.free)
        yield
        rs = qi[0]
        t = af(rs, b4.t[:, 0:T], AF.Sqrt, t, bias=EPS, scale=1.0 / 256)
        b4.free = [t]
        t = rcp(rs, rs, t)
        for j in range(2):
            t = stt(o[:, h, j, :], o[:, h, j, :], col("gla_norm_g", 2 * h + j), rs, OP.mult, OP.mult, t, t_o)
        done["o", h] = t
        gfree[0] = [t]

    sc_mid = [P.small[:, 128 + 16 * i:144 + 16 * i].rearrange("p (d h c) -> p d h c", d=2, h=4) for i in range(2)]
    sc_tot = P.small[:, 160:176].rearrange("p (d h c) -> p d h c", d=2, h=4)
    sc_dec = P.small[:, 176:192].rearrange("p (d h c) -> p d h c", d=2, h=4)

    def gla():
        yield from need(("lr", 1), ("lr", 0))
        yield from decays(1, lc, [t_rc, t_nc, hc.tok[KT - 1]])
        yield from decays(0, la, [hx.tok[KT - 1], t_nx, t_nc])
        done["decay"] = [done["la", r, d] for r in range(2) for d in range(2)]
        t = None
        tb = []
        for d in range(2):
            for h in range(4):
                for c in range(2):
                    cc = slice(128 * c, 128 * c + 128)
                    L = la[:, d, h, cc]
                    t = P.dve.do(lambda s, a=bb[:, d, h, cc], L=L: s.tensor_tensor_scan(a, L, L, 0.0, OP.add, OP.bypass),
                                 done["la", 0, d], t_nc)
                    if d == 1:
                        t = ts(P.small[:, 192 + 2 * h + c:193 + 2 * h + c], bb[:, d, h, 128 * c + 127:128 * c + 128], 1.0,
                               None, OP.mult, None, t)
                        t = stt(bb[:, d, h, cc], bb[:, d, h, cc], P.small[:, 192 + 2 * h + c:193 + 2 * h + c], L,
                                OP.subtract, OP.subtract, t, rev1=True)
                    tb.append(t)
        yield
        b5 = bb[:].rearrange("p d h (c n) -> p d h c n", c=2)
        for d in range(2):
            mid, end = (63, 127) if d == 0 else (64, 0)
            ts(sc_mid[0][:, d], b5[:, d, :, :, mid], -S16, None, OP.mult, None, tb)
            ts(sc_mid[1][:, d], b5[:, d, :, :, mid], S16, None, OP.mult, None, tb)
            t = ts(sc_tot[:, d], b5[:, d, :, :, end], S16, None, OP.mult, None, tb)
        done["bb"] = af(sc_dec[:], sc_tot[:], AF.Exp, t)
        yield
        for h in range(4):
            yield from need(("k", False, h // 2), ("v", False, h))
            gs = [ctx_state(d, h, 2 * (h % 2) + d) for d in range(2)]
            while gs:
                for g in list(gs):
                    try:
                        next(g)
                    except StopIteration:
                        gs.remove(g)
                yield
        done["ctx"] = [done["s", d, h] for d in range(2) for h in range(4)]
        gfree[0] = list(flat(gfree))
        for h in range(4):
            yield from need(("k", True, h // 2), ("q", h // 2), ("v", True, h))
            yield from x_head(h)
            yield
        done["gla"] = [done["o", h] for h in range(4)]
        for h in range(4):
            yield from need(("r", h))
            t = tt(pa(o[:, h]), pa(o[:, h]), pa(rr[:, 2 * h:2 * h + 2, :]), OP.mult, done["r", h], done["o", h])
            for j in range(2):
                P.split_x(ob, 2 * h + j, o[:, h, j, :], t, done["gla"])
            yield

    def sgu_side():
        yield from need(*[("zv", i) for i in range(4)])
        st = P.small[:, 208:232].rearrange("p (a b s) -> p a b s", a=2, b=2)
        mv = P.small[:, 232:236].rearrange("p (a s) -> p a s", a=2)
        wz = [done["zv", i] for i in range(4)]
        t1 = []
        for a in range(2):
            t = [P.dve.do(lambda e, a=a, b=b: e.bn_stats(st[:, a, b, :], zv[:, a, 512 * b:512 * b + 512]), wz)
                 for b in range(2)]
            t = P.dve.do(lambda e, a=a: e.bn_aggr(mv[:, a, :], st[:, a].rearrange("p b s -> p (b s)")), t)
            t1.append(t)
        t = af(mv[:, :, 1], mv[:, :, 1], AF.Sqrt, t1, bias=EPS)
        t = rcp(mv[:, :, 1], mv[:, :, 1], t)
        tz = []
        for a in range(2):
            t2 = ts(zv[:, a, :], zv[:, a, :], mv[:, a, 0:1], mv[:, a, 1:2], OP.subtract, OP.mult, t)
            t2 = tt(zv[:, a, :], zv[:, a, :], lnr[:, 0, :], OP.mult, t2, l_lnr)
            tz.append(tt(zv[:, a, :], zv[:, a, :], lnr[:, 1, :], OP.add, t2, l_lnr))
        done["ln"] = tz
        yield
        yield from need(*[("u", i) for i in range(4)])
        tb = []
        for i in range(4):
            bk = B[4 + i]
            for g in range(2):
                for n in range(2):
                    gg = 2 * i + g
                    t = mm(bk.t[:, 256 * g + 128 * n:256 * g + 128 * n + 128], zv[:, n, 128 * gg:128 * gg + 128],
                           sguw[:, gg, :], g == 0 and n == 0, g == 1 and n == 1, tz, l_sgu, bk.free)
            tb.append(t)
        yield
        for i in range(4):
            bk = B[4 + i]
            d4 = mix[:, i].rearrange("p (g n t) -> p g n t", g=2, n=2)
            t = tt(d4, bk.t[:].rearrange("p (g n t) -> p g n t", g=2, n=2), bc(sgub[:, 2 * i:2 * i + 2, :], 2, 2),
                   OP.add, tb[i], l_sgu, done["gla"])
            bk.free = [t]
            t = tt(pa(u[:, 2 * i:2 * i + 2, :]), pa(u[:, 2 * i:2 * i + 2, :]), mix[:, i], OP.mult, t, done["u", i])
            for g in range(2):
                P.split_x(sgu, 2 * i + g, u[:, 2 * i + g, :], t, tb)
            yield

    mix = P.at("mix", LC, [4, 512])

    P.sides = [gla(), sgu_side()]
    P.source("lr", wlr[:], l_lr, 8, lr_part)
    P.units("k", w_in, 2560, [hx, hc], False, ev_k)
    P.units("q", w_in, 2048, [hx], False, ev_q)
    for i in range(2):
        P.units(f"v{i}", w_in, 3072 + 512 * i, [hx, hc], True, ev_v)

    l_lnr = []

    def late_loads():
        hcr = done["v", False, 3]
        w = [hcr]
        for i, n in enumerate(("sgu_ln_g", "sgu_ln_b")):
            l_lnr.append(P.load(lnr[:, i, :], A[n].partition_broadcast(128), w))
    P.call(late_loads)
    l_sgu = [P.load(sguw[:], A["sgu_wT"]), P.load(sgub[:], A["sgu_b"].partition_broadcast(128))]

    def mod_load(g, i):
        P.want(("mod", g, i), [(lambda t: t[:, 0:4096].rearrange("p (k n) -> p k n", k=2),
                               A["w_mod"][256 * i:256 * i + 256, 2048 * g:2048 * g + 2048].rearrange(
                                   "(k p) n -> p k n", p=128))])
        P.plain(("mod", g, i), mod_part(g, i))

    P.modcol = modcol
    gt1 = P.small[:, 32:40]
    gt2 = P.small[:, 56:64]
    sc2 = P.small[:, 40:56].rearrange("p (a k) -> p a k", a=2)

    def mod1():
        t = mod_done(1, md0, t0, t1)
        modcol["gt1"] = tt(gt1, md0[:, 0:8, 0], col("b_mod", 16, 8), OP.add, t)
        modcol["sh2"] = tt(sc2[:, 1], md0[:, 8:16, 0], col("b_mod", 24, 8), OP.add, t)

    def mod2():
        t = mod_done(2, md0, modcol["gt1"], modcol["sh2"])
        t2 = tt(sc2[:, 0], md0[:, 0:8, 0], col("b_mod", 32, 8), OP.add, t)
        modcol["sc2"] = stt(sc2[:, 0], sc2[:, 0], 1.0, col("g_norm2", 0, 8), OP.add, OP.mult, t2)
        modcol["gt2"] = tt(gt2, md0[:, 8:16, 0], col("b_mod", 40, 8), OP.add, t)

    P.until(done, "decay")
    for i in range(2):
        P.units(f"zv{i}", w_in, 1024 + 512 * i, [hx], True, ev_zv)
        mod_load(1, i)
    P.until(done, "gla")
    for i in range(2):
        P.units(f"u{i}", w_in, 512 * i, [hx], False, ev_u)
        mod_load(1, 2 + i)
    P.call(mod1)
    for i in range(2):
        P.units(f"r{i}", w_in, 4096 + 512 * i, [hx], False, ev_r)
        mod_load(2, i)
    P.until(done, "ln")
    for i in range(4):
        P.units(f"g{i}", w_in, 5152 + 512 * i, [hx], False, ev_g)
        if i < 2:
            mod_load(2, 2 + i)
    P.call(mod2)

    def ev_a(xp, b, c, t):
        j = c // 128
        done["m", j] = r = tt(pa(m[:, j:j + 2, :]), b[:], pa(gates[:, j:j + 2, :]), OP.mult, t, done["g", j // 2], lc_free())
        return r

    def lc_free():
        return [done["gla"]] + [sgu.tok[k] for k in range(KT)]

    def ev_b(xp, b, c, t):
        j = c // 128
        gb = pa(gates[:, 8 + j:10 + j, :])
        r = tt(gb, b[:], gb, OP.mult, t, done["g", 4 + j // 2])
        t = tt(pa(m[:, j:j + 2, :]), pa(m[:, j:j + 2, :]), gb, OP.add, r, done["m", j])
        for a in range(2):
            P.split_x(mp, j + a, m[:, j + a, :], t, done["gla"])
        return r

    def ev_o(xp, b, c, t):
        j = c // 128
        for a in range(2):
            r = stt(x[:, j + a, :], b[:, 256 * a:256 * a + 256], gt1[:, j + a:j + a + 1], x[:, j + a, :], OP.mult, OP.add, t,
                    modcol["gt1"], t_nx)
            P.x_tok[j + a] = r
        return r

    P.x_tok = {}
    P.call(P.drain)
    for i in range(2):
        P.units(f"wa{i}", A["w_a"], 512 * i, [sgu], False, ev_a)
    for i in range(2):
        P.units(f"wb{i}", A["w_b"], 512 * i, [ob], False, ev_b)
    for i in range(2):
        P.units(f"wo{i}", A["w_o"], 512 * i, [mp], False, ev_o)

    P.gt2, P.sc2, P.modcol, P.doneA, P.doneB = gt2, sc2, modcol, done, {}
    P.m_free = None


def phase_b(P):
    A, Z = P.A, P.Z
    mm, tp, af, acp, tt, ts, stt, cp, rcp, red = P.mm, P.tp, P.af, P.acp, P.tt, P.ts, P.stt, P.cp, P.rcp, P.red
    col, sm, ONE, EPS, x, B = P.col, P.sm, P.ONE, P.EPS, P.x, P.banks
    LT = P.mask["lt"]
    pa = lambda a: a.rearrange("p a t -> p (a t)")

    P.m_free = [P.x_tok[k] for k in range(KT)]
    P.modcol = list(P.modcol.values())
    h2 = P.at("h2", Z + 8192, [KT, T])
    h2t = P.at("h2t", Z + 10240, [2, 1024])
    mem = P.at("mem", Z + 12288, [KT, T])
    yacc = P.at("yacc", Z + 14336, [KT, T])
    xe = P.at("xe", Z + 16384, [KT, T])
    hid = [P.at(f"hid{i}", Z + 18432 + 768 * i, [768]) for i in range(2)]
    hidT = [P.at(f"hidT{i}", Z + 19968 + 768 * i, [6, 2, 64]) for i in range(2)]
    y = [P.at(f"y{i}", Z + 21504 + 512 * i, [512]) for i in range(2)]
    sel = P.at("sel", Z + 22528, [2, 4, 64])
    selw = P.at("selw", Z + 23040, [2, 2, 64])
    selT = [P.at(f"selT{i}", Z + 23296 + 256 * i, [T]) for i in range(2)]
    stage = [P.at(f"stage{i}", Z + 24064 + 512 * i, [512]) for i in range(2)]
    rs = P.at("rs", Z + 25088, [T])
    rsm = P.at("rsm", Z + 25344, [T])
    wr = P.at("wr", Z + 25600, [KT, 16])
    lg = P.at("lg", Z + 25728, [T])
    rt = P.at("rt", Z + 25984, [512])
    P.mk = P.at("mk", Z + 26576, [KT, T])
    P.mv = P.at("mv", Z + 28624, [2, 1024])
    sq = P.at("sq", Z + 16384, [KT, T])
    mems = P.at("mems", Z + 10240, [KT, T])
    br = P.small[:, 236:237]

    P.add_slot(3, Z, P.doneA["g", 7])
    P.add_slot(4, 4096, P.pe_read)
    P.add_slot(5, Z + 4096, P.m_free)

    done = P.doneB
    l_mem = P.load(mem[:], A["memT"], P.doneA["gla"])

    def mem_norm():
        t = af(mems[:], mem[:], AF.Square, l_mem, P.m_free)
        for k in range(KT):
            t2 = mm(B[3].t[:, 0:T], ONE, mems[:, k, :], k == 0, k == KT - 1, t, B[3].free)
        t = af(rsm[:], B[3].t[:, 0:T], AF.Sqrt, t2, P.m_free, bias=EPS, scale=1.0 / 1024)
        B[3].free = [t]
        done["rsm"] = rcp(rsm[:], rsm[:], t)

    def mem_scale(l, *w):
        for k in range(KT):
            done["mem", l, k] = stt(mem[:, k, :], mem[:, k, :], col("norm_mem_2", 8 * l + k), rsm[:], OP.mult, OP.mult,
                                    done["rsm"], l_mem, *w)

    nst = [0]

    def mem_kv(l, i):
        def f(s, ld):
            w = s[:, 0:4096].rearrange("p (k n) -> p k n", k=8)
            for v in range(2):
                bk = B[6 + v]
                if i < 2:
                    for g in range(2):
                        for k in range(KT):
                            c = 256 * v + 128 * g
                            t = mm(bk.t[:, 256 * g:256 * g + 256], w[:, k, c:c + 128], mem[:, k, :], g == 0 and k == 0,
                                   k == KT - 1, ld, done["mem", l, k], bk.free)
                    dst = P.mk[:, 4 * i + 2 * v:4 * i + 2 * v + 2, :]
                else:
                    for k in range(KT):
                        t = mm(bk.t[:], mem[:, k, 128 * v:128 * v + 128], w[:, k, :], k == 0, k == KT - 1, ld,
                               done["mem", l, k], bk.free)
                    dst = P.mv[:, v, 512 * (i - 2):512 * (i - 2) + 512]
                if l == 0:
                    r = acp(dst if i >= 2 else pa(dst), bk.t[:], t, P.m_free)
                    P.kv_tok.append(r)
                else:
                    n = nst[0]
                    nst[0] += 1
                    r = acp(stage[n % 2][:], bk.t[:], t, P.stage_free[n % 2])
                    P.stage_free[n % 2] = [P.load(A["kv1"][:, 512 * n:512 * n + 512], stage[n % 2][:], r)]
                    P.kv1_tok[n] = P.stage_free[n % 2]
                    P.kv1_at[n] = (i, v)
                bk.free = [r]
            done["memmm", l, i] = t
            return t
        return f

    def want_mem(l, i):
        P.want(("mem", l, i), [P.block(A["w_mem_kv"][l], 512 * i)], 6)
        P.plain(("mem", l, i), mem_kv(l, i))

    P.kv_tok, P.stage_free, P.kv1_tok, P.kv1_at = [], [[], []], {}, {}
    l_wr = [P.load(wr[:], A["w_router"], P.doneA["decay"]), P.load(br[0:16, :], A["b_router"])]

    def expert_loads(e):
        k1 = lambda w, c: P.block(A[w][e], c)
        for n, w, c in (("g0", "w_eg", 0), ("g1", "w_eg", 512), ("u0", "w_eu", 0), ("u1", "w_eu", 512),
                        ("g2", "w_eg", 1024), ("u2", "w_eu", 1024)):
            P.want((n, e), [k1(w, c)], 6)
        for j in range(3):
            P.want((f"d{j}", e), [P.block(A["w_ed"][e], 0, n=1024, k0=4 * j, kt=4)], 6)

    P.call(mem_norm)
    P.call(lambda: mem_scale(0))
    want_mem(0, 0)
    want_mem(0, 1)

    r_ = lambda o, *s: rt[:, o:o + int(np.prod(s))].rearrange(
        "p (a b) -> p a b", a=s[0]) if len(s) == 2 else rt[:, o:o + s[0]]
    prob, am, wt, posm = (r_(32 * i, 2, 16) for i in range(4))
    v_, e_ = r_(128, 2, 16), r_(160, 2, 16)
    oh = [r_(192, 2, 16), r_(224, 2, 16)]
    hi_, lo_ = r_(256, 8, 2), r_(272, 8, 2)
    t1_, t2_, gs_, gsel, gw = (r_(288 + 8 * i, 2, 4) for i in range(5))
    m_ = [r_(328 + 2 * i, 2) for i in range(8)]
    cnt, cnt1 = r_(352, 16), r_(368, 1)
    counts = P.nc.alloc_sbuf_tensor_at("counts", [128, 32], I32, offset=BASE + 4 * (Z + 26496))
    most = {}
    streams = {"act": P.act, "pe": P.pe, "dve": P.dve}
    b16, b4 = lambda a: bc(a, 16, 2), lambda a: bc(a, 4, 2)

    def route():
        xt = [P.x_tok[k] for k in range(KT)]
        t = af(sq[:], x[:], AF.Square, xt)
        for k in range(KT):
            t2 = mm(B[4].t[:, 0:T], ONE, sq[:, k, :], k == 0, k == KT - 1, t, B[4].free)
        t = af(rs[:], B[4].t[:, 0:T], AF.Sqrt, t2, bias=EPS, scale=1.0 / 1024)
        B[4].free = [t]
        t = rcp(rs[:], rs[:], t)
        t = tt(h2[:], x[:], bc(rs[:], KT, 1), OP.mult, t)
        th = [ts(h2[:, k, :], h2[:, k, :], P.sc2[:, 0, k:k + 1], P.sc2[:, 1, k:k + 1], OP.mult, OP.add, t, P.modcol)
              for k in range(KT)]
        for k in range(KT):
            t = mm(B[4].t[0:16, 0:T], wr[:, k, :], h2[:, k, :], k == 0, k == KT - 1, th[k], l_wr, B[4].free)
        t = af(lg[0:16, :], B[4].t[0:16, 0:T], AF.Identity, t, xt, l_wr, bias=br[0:16, :])
        for a in range(2):
            t2 = tp(B[5].t[:, 16 * a:16 * a + 16], lg[0:16, 128 * a:128 * a + 128], t, B[5].free)
        for a in range(2):
            for g in range(2):
                bk = B[2 * a + g] if False else B[(3, 4, 0, 1)[2 * a + g]]
                for j in range(4):
                    k = 4 * g + j
                    t3 = tp(bk.t[:, 128 * j:128 * j + 128], h2[:, k, 128 * a:128 * a + 128], th[k], t, bk.free)
                done["h2t", a, g] = acp(h2t[:, a, 512 * g:512 * g + 512], bk.t[:], t3, done["rsm"])
                bk.free = [done["h2t", a, g]]
        L = B[5].t[:, 0:32].rearrange("p (a b) -> p a b", a=2)
        t = red(m_[0], L, OP.max, t2)
        t = tt(prob, L, b16(m_[0]), OP.subtract, t)
        B[5].free = [t]
        t = af(prob, prob, AF.Exp, t)
        t = red(m_[1], prob, OP.add, t)
        t = rcp(m_[1], m_[1], t)
        t = tt(prob, prob, b16(m_[1]), OP.mult, t)
        p2 = prob.rearrange("p a (g j i) -> p (a g) j i", g=4, j=2)
        ta = tt(hi_, p2[:, :, :, 0], p2[:, :, :, 1], OP.max, t)
        tb = tt(lo_, p2[:, :, :, 0], p2[:, :, :, 1], OP.min, t)
        f8 = lambda a: a.rearrange("p a b -> p (a b)")
        tc = tt(f8(t1_), hi_[:, :, 0], hi_[:, :, 1], OP.max, ta)
        td = tt(f8(t2_), hi_[:, :, 0], hi_[:, :, 1], OP.min, ta)
        te = tt(f8(gs_), lo_[:, :, 0], lo_[:, :, 1], OP.max, tb)
        t = tt(t2_, t2_, gs_, OP.max, td, te)
        t = tt(gs_, t1_, t2_, OP.add, t, tc)
        t = red(m_[2], gs_, OP.max, t)
        t = tt(gw, gs_, b4(m_[2]), OP.is_equal, t)
        t = tt(gw, gw, bc(sm[:, 32:36], 2, 1), OP.mult, t)
        t = red(m_[3], gw, OP.max, t)
        t = tt(gsel, gw, b4(m_[3]), OP.is_equal, t)
        ta = ts(gw, gsel, -1.0, None, OP.add, None, t)
        p3 = lambda a: a.rearrange("p a (g i) -> p (a g) i", g=4)
        g8 = lambda a: bc(f8(a), 4, 2)
        t = tt(p3(v_), p3(prob), g8(gsel), OP.mult, t)
        t = tt(p3(v_), p3(v_), g8(gw), OP.add, t, ta)
        for i in range(2):
            t = red(m_[4 + i], v_, OP.max, t)
            t = tt(e_, v_, b16(m_[4 + i]), OP.is_equal, t)
            t = tt(e_, e_, bc(sm[:, 16:32], 2, 1), OP.mult, t)
            t = red(m_[6], e_, OP.max, t)
            t = tt(oh[i], e_, b16(m_[6]), OP.is_equal, t)
            if i == 0:
                t = stt(v_, oh[0], -4.0, v_, OP.mult, OP.add, t)
        ta = tt(am, oh[0], oh[1], OP.add, t)
        t = tt(m_[6], m_[4], m_[5], OP.add, t)
        t = rcp(m_[7], m_[6], t)
        t4 = tt(m_[4], m_[4], m_[7], OP.mult, t)
        t5 = tt(m_[5], m_[5], m_[7], OP.mult, t)
        t4 = tt(wt, oh[0], b16(m_[4]), OP.mult, t4)
        t5 = tt(e_, oh[1], b16(m_[5]), OP.mult, t5)
        done["wt"] = tt(wt, wt, e_, OP.add, t4, t5)
        pb = B[5].t
        mm(pb[:, 0:16], LT, am[:, 0, :], True, True, ta, B[5].free)
        mm(pb[:, 16:32], LT, am[:, 1, :], False, False)
        mm(pb[:, 16:32], ONE, am[:, 0, :], False, True)
        mm(pb[:, 32:48], ONE, am[:, 0, :], False, False)
        t = mm(pb[:, 32:48], ONE, am[:, 1, :], False, True)
        t2 = stt(posm, pb[:, 0:32].rearrange("p (a b) -> p a b", a=2), 1.0, am, OP.add, OP.mult, t)
        t = cp(cnt, pb[:, 32:48], t)
        B[5].free = [t]
        tm = red(cnt1, cnt, OP.max, t)
        done["cnt"] = cp(counts[:, 0:17], rt[:, 352:369], t, tm)
        for n in ("act", "pe", "dve"):
            P.raw(streams[n], lambda e, n=n: most.__setitem__(n, e.value_load(counts[0:1, 16:17])), done["cnt"])
        done["pos"] = ts(posm, posm, -1.0, None, OP.add, None, t2)

    IOTA = sm[:, 64:128]
    xe_read = []

    def gather(q):
        ps = [posm[:, a, 4 * q:4 * q + 4] for a in range(2)]
        t = [tt(sel[:, a], bc(IOTA, 4, 1), bc(ps[a], 64, 2), OP.is_equal, done["pos"], done.get("gather")) for a in range(2)]
        for g in range(4):
            bk = B[3 + g % 2]
            for j in range(2):
                k = 2 * g + j
                for a in range(2):
                    r = mm(bk.t[:, 256 * j:256 * j + 256], h2t[:, a, 128 * k:128 * k + 128],
                           sel[:, a].rearrange("p e s -> p (e s)"), j == 0 and a == 0, a == 1, t,
                           done["h2t", a, k // 4], bk.free)
            done["xe", q, g] = acp(pa(xe[:, 2 * g:2 * g + 2, :]), bk.t[:], r, xe_read)
            bk.free = [done["xe", q, g]]
        done["gather"] = r

    def xs(e, k):
        return xe[:, k, 64 * (e % 4):64 * (e % 4) + 64]

    def up(e, dst, j, first, last):
        def f(s, ld):
            w = s[:, 0:4096].rearrange("p (k n) -> p k n", k=8)
            bk = dst
            for k in range(KT):
                for h in range(2):
                    t = mm(bk.t[64 * h:64 * h + 64, 256 * j:256 * j + 256], xs(e, k), w[:, k, 256 * h:256 * h + 256],
                           first and k == 0, last and k == KT - 1, ld, done["xe", e // 4, k // 2], bk.free if first else None)
            done["up"] = t
            return t
        return f

    act_read = [[], []]

    def hidden(e, part):
        i = e % 2
        n = 512 if part == 0 else 256
        g_, u_ = (B[0].t[:], B[1].t[:]) if part == 0 else (B[2].t[:, 0:256], B[2].t[:, 256:512])
        h = hid[i][:, 512 * part:512 * part + n]
        t = af(h, g_, AF.Silu, done["up"], done.get(("hT", e - 2, part)))
        t = tt(h, h, u_, OP.mult, t)
        if part == 0:
            B[0].free = [t]
            B[1].free = [t]
        else:
            B[2].free = [t]
        bk = B[3 + part]
        for j in range(n // 128):
            t2 = tp(bk.t[:, 128 * j:128 * j + 128], h[:, 128 * j:128 * j + 128], t, bk.free)
        r = acp(hidT[i][:, 4 * part:4 * part + n // 128].rearrange("p a b c -> p (a b c)"), bk.t[:, 0:n], t2,
                done.get(("down", e - 2)))
        bk.free = [r]
        done["hT", e, part] = r

    def down(e, j):
        def f(s, ld):
            w = s[:, 0:4096].rearrange("p (k n) -> p k n", k=4)
            bk = B[5]
            for h in range(2):
                for u in range(2):
                    for c in range(2):
                        t = mm(bk.t[64 * c:64 * c + 64, :], hidT[e % 2][:, 2 * j + u, h, :], w[:, 2 * h + u, 512 * c:512 * c + 512],
                               j == 0 and h == 0 and u == 0, j == 2 and h == 1 and u == 1, ld, done["hT", e, j // 2],
                               bk.free if j == 0 else None)
            done["down", e] = t
            return t
        return f

    def weigh(e):
        i = e % 2
        t = [ts(selw[:, a], bc(IOTA, 2, 1), posm[:, a, e:e + 1], wt[:, a, e:e + 1], OP.is_equal, OP.mult,
                done["pos"], done["wt"], done.get("weigh")) for a in range(2)]
        bk = B[6]
        for a in range(2):
            t2 = tp(bk.t[:, 128 * a:128 * a + 128], selw[:, a].rearrange("p a b -> p (a b)"), t, bk.free)
        done["weigh"] = t2
        done["selT", e] = acp(selT[i][:], bk.t[:, 0:256], t2, done.get(("comb", e - 2)))
        bk.free = [done["selT", e]]

    def combine(e):
        i = e % 2
        t = acp(y[i][:], B[5].t[:], done["down", e], done.get(("comb", e - 2)))
        B[5].free = [t]
        for g in range(4):
            bk = B[6 + g % 2]
            c = g // 2
            for j in range(2):
                f = 2 * (g % 2) + j
                r = mm(bk.t[:, 256 * j:256 * j + 256], y[i][64 * c:64 * c + 64, 128 * f:128 * f + 128],
                       selT[i][64 * c:64 * c + 64, :], j == 0, j == 1, t, done["selT", e], bk.free)
            dst = pa(yacc[:, 4 * c + 2 * (g % 2):4 * c + 2 * (g % 2) + 2, :])
            if e == 0:
                bk.free = [cp(dst, bk.t[:], r, P.m_free)]
            else:
                bk.free = [tt(dst, dst, bk.t[:], OP.add, r, done["y", g])]
            done["y", g] = bk.free
        done["comb", e] = r

    P.call(route)
    for e in range(16):
        if e % 4 == 0:
            P.call(lambda e=e: gather(e // 4))
        expert_loads(e)
        P.plain(("g0", e), up(e, B[0], 0, True, False))
        P.plain(("g1", e), up(e, B[0], 1, False, True))
        P.plain(("u0", e), up(e, B[1], 0, True, False))
        P.plain(("u1", e), up(e, B[1], 1, False, True))
        P.call(lambda e=e: hidden(e, 0))
        P.plain(("g2", e), up(e, B[2], 0, True, False))
        P.plain(("u2", e), up(e, B[2], 1, False, True))

        def mark(e=e):
            xe_read[:] = [done["up"]]
            hidden(e, 1)
            weigh(e)
        P.call(mark)
        for j in range(3):
            P.plain((f"d{j}", e), down(e, j))
        P.call(lambda e=e: combine(e))
        if e in (1, 3):
            want_mem(0, 2 + e // 2)
        if e == 4:
            def second():
                t = P.load(mem[:], A["memT"], done["memmm", 0, 3], done["memmm", 0, 1])
                for k in range(KT):
                    done["mem", 1, k] = stt(mem[:, k, :], mem[:, k, :], col("norm_mem_2", 8 + k), rsm[:], OP.mult,
                                            OP.mult, t)
            P.call(second)
        if e in (5, 7, 9, 11):
            want_mem(1, (e - 5) // 2)

    class Loop:

        def __init__(self):
            self.q = {n: [] for n in streams}
            self.n = {n: 0 for n in ("act", "pe", "dve", "dma")}
            self.sem = {n: P.sem("more_" + n) for n in self.n}

        def do(self, n, fn, *w, dma=False):
            s = "dma" if dma else n
            self.n[s] += 16 if dma else 1
            self.q[n].append((fn, [x for x in w if x], s, 16 if dma else 1))
            return s, self.n[s]

        def emit(self, n, e, before):
            reg = {s: e.alloc_register(f"more_{n}_{s}") for s in self.n}
            tmp = e.alloc_register(f"more_{n}_tmp")
            with e.If(most[n] > 64):
                for t in before:
                    e.wait_ge(t.sem, t.count)
                for r in reg.values():
                    e.reg_mov(r, 0)
                with e.Fori(1, 4) as blk:
                    with e.Fori(0, 16) as ex:
                        c = e.value_load(counts[0:1, bass.ds(ex, 1)])
                        with e.If(c - blk * 64 > 0):
                            for fn, waits, s, k in self.q[n]:
                                for ws, wc in waits:
                                    e.reg_add(tmp, reg[ws], wc)
                                    e.wait_ge(self.sem[ws], tmp)
                                fn(e, ex, blk).then_inc(self.sem[s], k)
                            for s in self.n:
                                if n == "pe":
                                    e.reg_add(tmp, reg[s], self.whole[s])
                                    e.wait_ge(self.sem[s], tmp)
                            for s in self.n:
                                e.reg_add(reg[s], reg[s], self.n[s])

    def more():
        lp = Loop()
        W = P.at("more_w", Z, [4096])
        pc, wc, base = rt[:, 400:402], rt[:, 402:404], rt[:, 404:405]
        last = [None]

        def lmm(out, l, r, start, stop, *w):
            last[0] = lp.do("pe", lambda e, ex, blk: e.matmul(out, l, r, start=start, stop=stop, skip_group_check=True), *w)
            return last[0]

        def copy(out, i, *w):
            return lp.do("act", lambda e, ex, blk: e.copy(out, i), *w)

        def weights(w, view, *waits):
            return lp.do("act", lambda e, ex, blk: e.dma_start(view, w(ex)), *waits, dma=True)

        t = lp.do("dve", lambda e, ex, blk: e.tensor_copy(base, sm[:, 36:40][:, bass.ds(blk, 1)]))
        tp_ = None
        for a in range(2):
            tp_ = lp.do("dve", lambda e, ex, blk, a=a: e.tensor_copy(pc[:, a:a + 1], posm[:, a, bass.ds(ex, 1)]))
            tw = lp.do("dve", lambda e, ex, blk, a=a: e.tensor_copy(wc[:, a:a + 1], wt[:, a, bass.ds(ex, 1)]))
        t = lp.do("dve", lambda e, ex, blk: e.tensor_scalar(pc, pc, base, None, OP.subtract), t, tp_, tw)
        for a in range(2):
            ts_ = lp.do("dve", lambda e, ex, blk, a=a: e.tensor_scalar(sel[:, a, 0, :], IOTA, pc[:, a:a + 1], None, OP.is_equal), t)
            tw = lp.do("dve", lambda e, ex, blk, a=a: e.tensor_scalar(
                selw[:, a], bc(IOTA, 2, 1), pc[:, a:a + 1], wc[:, a:a + 1], OP.is_equal, OP.mult), t)
        for k in range(KT):
            for a in range(2):
                t = lmm(B[3].t[:, 64 * k:64 * k + 64], h2t[:, a, 128 * k:128 * k + 128], sel[:, a, 0, :], k == 0 and a == 0,
                        a == 1, ts_)
        x64 = xe[:, 0:2, :].rearrange("p a t -> p (a t)")
        tx = copy(x64, B[3].t[:], t)
        for a in range(2):
            t = lp.do("pe", lambda e, ex, blk, a=a: e.transpose(B[6].t[:, 128 * a:128 * a + 128],
                                                             selw[:, a].rearrange("p a b -> p (a b)"), P.EYE), tw)
        tT = copy(selT[0][:], B[6].t[:, 0:256], t)
        tw = None
        for n, w, j, bk, o, st in (("g", "w_eg", 0, 0, 0, True), ("g", "w_eg", 1, 0, 256, False), ("u", "w_eu", 0, 1, 0, True),
                                   ("u", "w_eu", 1, 1, 256, False), ("g", "w_eg", 2, 2, 0, True), ("u", "w_eu", 2, 2, 256, False)):
            w3 = W[:].rearrange("p (k n) -> p k n", k=8)
            ld = weights(lambda ex, w=w, j=j: A[w][bass.ds(ex, 1), :, 512 * j:512 * j + 512].rearrange(
                "o (k p) n -> p (o k) n", p=128), w3, tw)
            for k in range(KT):
                for h in range(2):
                    tw = lmm(B[bk].t[64 * h:64 * h + 64, o:o + 256], x64[:, 64 * k:64 * k + 64], w3[:, k, 256 * h:256 * h + 256],
                             st and k == 0, k == KT - 1, ld, tx)
        for part, (g_, u_) in enumerate(((B[0].t[:], B[1].t[:]), (B[2].t[:, 0:256], B[2].t[:, 256:512]))):
            n = 512 if part == 0 else 256
            h = hid[0][:, 512 * part:512 * part + n]
            t = lp.do("act", lambda e, ex, blk, h=h, g_=g_: e.activation(h, g_, AF.Silu), tw)
            t = lp.do("dve", lambda e, ex, blk, h=h, u_=u_: e.tensor_tensor(h, h, u_, OP.mult), t)
            for j in range(n // 128):
                t2 = lp.do("pe", lambda e, ex, blk, j=j, h=h, part=part: e.transpose(
                    B[3 + part].t[:, 128 * j:128 * j + 128], h[:, 128 * j:128 * j + 128], P.EYE), t, tx)
            th = copy(hidT[0][:, 4 * part:4 * part + n // 128].rearrange("p a b c -> p (a b c)"), B[3 + part].t[:, 0:n], t2)
        for j in range(3):
            w3 = W[:].rearrange("p (k n) -> p k n", k=4)
            ld = weights(lambda ex, j=j: A["w_ed"][bass.ds(ex, 1), 512 * j:512 * j + 512, :].rearrange(
                "o (k p) n -> p (o k) n", p=128), w3, tw)
            for h in range(2):
                for u in range(2):
                    for c in range(2):
                        tw = lmm(B[5].t[64 * c:64 * c + 64, :], hidT[0][:, 2 * j + u, h, :], w3[:, 2 * h + u, 512 * c:512 * c + 512],
                                 j == 0 and h == 0 and u == 0, j == 2 and h == 1 and u == 1, ld, th)
        ty = copy(y[0][:], B[5].t[:], tw)
        rd = [tT, None]
        for g in range(4):
            bk, c = B[6 + g % 2], g // 2
            for j in range(2):
                f = 2 * (g % 2) + j
                t = lmm(bk.t[:, 256 * j:256 * j + 256], y[0][64 * c:64 * c + 64, 128 * f:128 * f + 128],
                        selT[0][64 * c:64 * c + 64, :], j == 0, j == 1, ty, tT, rd[g % 2])
            dst = pa(yacc[:, 4 * c + 2 * (g % 2):4 * c + 2 * (g % 2) + 2, :])
            rd[g % 2] = lp.do("dve", lambda e, ex, blk, dst=dst, bk=bk: e.tensor_tensor(dst, dst, bk.t[:], OP.add), t)
        lp.whole = dict(lp.n)
        lp.do("act", lambda e, ex, blk: e.copy(rt[:, 406:407], sm[:, 0:1]), *lp.whole.items())
        lp.do("dve", lambda e, ex, blk: e.tensor_copy(rt[:, 407:408], sm[:, 0:1]), *lp.whole.items())
        before = list(flat([done["comb", 15], [done["y", g] for g in range(4)], P.kv_tok, P.stage_free, done["selT", 15]]))
        for t in before:
            t.used = True
        for n in streams:
            P.raw(streams[n], lambda e, n=n: lp.emit(n, e, before))
    P.call(more)

    def last_norm():
        gt2 = P.gt2
        for k in range(KT):
            P.x_tok[k] = stt(x[:, k, :], yacc[:, k, :], gt2[:, k:k + 1], x[:, k, :], OP.mult, OP.add, done["y", k // 2],
                             P.modcol, done["gather"])
        t = af(sq[:], x[:], AF.Square, P.x_tok.values(), xe_read)
        for k in range(KT):
            t2 = mm(B[4].t[:, 0:T], ONE, sq[:, k, :], k == 0, k == KT - 1, t, B[4].free)
        t = af(rs[:], B[4].t[:, 0:T], AF.Sqrt, t2, bias=EPS, scale=1.0 / 1024)
        B[4].free = [t]
        t = rcp(rs[:], rs[:], t)
        for k in range(KT):
            P.x_tok[k] = stt(x[:, k, :], x[:, k, :], col("g_final", k), rs[:], OP.mult, OP.mult, t)
    P.call(last_norm)


C_MASKS = ["sub"] + [f"level{i}" for i in range(1, 7)] + ["last"]
C_SMALL = ["freq_sa", "sign_sa", "freq_ix", "sign_ix", "lnq"]
TURN = 2 * np.pi
TURN1 = 6.28125
TURN2 = float(np.floor((TURN - TURN1) * 2.0 ** 20) / 2.0 ** 20)
TURN3 = float(np.float32(TURN - TURN1 - TURN2))
HALF_TURN = 3.1415925
BIG = -1e30
TAKEN = -3e38


def constants_c():
    p, f = np.meshgrid(np.arange(128), np.arange(128), indexing="ij")
    out = [((p // 2 == f // 2) & (f > p)).astype(np.float32)]
    for i in range(1, 7):
        b = 1 << i
        out.append(((p // (2 * b) == f // (2 * b)) & (p // b > f // b)).astype(np.float32))
    out.append((p == 127).astype(np.float32))
    q, key = np.arange(128)[:, None], np.arange(256)[None, :]
    out.append(np.where(key[:, :128] // 64 <= q // 64, 0.0, BIG).astype(np.float32))
    out.append(np.where(key // 64 <= (q + 128) // 64, 0.0, BIG).astype(np.float32))
    sm = np.zeros((128, 8), np.float32)
    for c, (head, half) in ((0, (128, 16)), (2, (64, 8))):
        rd = 2 * half
        freq = np.float32(500000.0) ** -(np.arange(half, dtype=np.float32) * np.float32(2.0) / np.float32(rd))
        for r in range(128):
            k = r % head
            if k < rd:
                sm[r, c] = freq[k % half]
                sm[r, c + 1] = -1.0 if k < half else 1.0
    sm[:, 4] = -0.5 * np.log(128.0)
    return np.concatenate(out + [sm], axis=1)


def phase_c(P, out):
    A, Z = P.A, P.Z
    mm, tp, af, acp, tt, ts, stt, cp, rcp, red = P.mm, P.tp, P.af, P.acp, P.tt, P.ts, P.stt, P.cp, P.rcp, P.red
    col, sm, ONE, EYE, EPS, x, B = P.col, P.sm, P.ONE, P.EYE, P.EPS, P.x, P.banks
    LE = P.mask["le"]
    pa = lambda a: a.rearrange("p a t -> p (a t)")
    at = lambda n, o, s, dt=F32: P.at(n, Z + o, s, dt)

    H = Part(at("h_hi", 0, [KT, T], F32R), at("h_lo", 2048, [KT, T], F32R))
    KQ = [at(f"kq{g}", 4096 + 3072 * g, [4, 2, 2, 128]) for g in range(2)]
    V = [at(f"v{g}", 6144 + 3072 * g, [4, 2, 128]) for g in range(2)]
    MT, Tm, Um, AT, D = (at(n, 10240 + 1024 * i, [4, 2, 128]) for i, n in enumerate(("mt", "tm", "um", "at", "dd")))
    kdec, ER = at("kdec", 15360, [4, 128]), at("er", 15872, [4, 128])
    odn = at("odn", 16384, [KT, T])
    iq, ik, smT = at("iq", 18432, [4, T]), at("ik", 19456, [T]), at("smT", 19712, [T])
    score, relu = at("score", 19968, [384]), at("relu", 20352, [512])
    maskb = at("maskb", 20992, [384])
    wsm = [at(f"wsm{i}", 21504 + 1024 * i, [KT, 128]) for i in range(2)]
    raw = [at(f"raw{i}", 21504 + 520 * i, [2, 260]) for i in range(2)]
    Y = [at(f"y_{i}", 22544 + 512 * i, [2, T]) for i in range(2)]
    xq = at("xq", 4096, [KT, T])
    osa = at("osa", 6144, [KT, T])
    sq_, sk_, sv_ = at("sq_", 8192, [KT, T]), at("sk_", 10240, [KT, T]), at("sv_", 12288, [2, 1024])
    PT = [at(f"pt{i}", 14336 + 512 * i, [512]) for i in range(4)]
    hiA, hiB = at("hiA", 18432, [KT, T], F32R), P.at("hiB", Z + 28624, [KT, T], F32R)
    gate = [at("gate0", 21504, [KT, T]), at("gate1", 8192, [KT, T])]
    mg = P.at("mg", Z + 26576, [KT, T])
    cc = at("cc", 24016, [1416])
    rope = at("rope", 25440, [4, T])
    hn = at("hn", 16384, [KT, T])
    hsq = at("hsq", 18432, [KT, T])
    rs = at("rs_", 23568, [T])
    FH, FL = at("f_hi", 4096, [22, T], F32R), at("f_lo", 9728, [22, T], F32R)
    fg = [at(f"fg{i}", 15360 + 1024 * i, [4, T]) for i in range(2)]
    fa = [at(f"fa{i}", 17408 + 512 * i, [512]) for i in range(2)]
    tokm = P.small[:, 240:384].rearrange("p (c n) -> p c n", c=2)
    ekd, gl_, nsc = P.small[:, 384:392], P.small[:, 392:400], P.small[:, 400:416]
    alog = P.small[:, 416:420]
    mx, nmx, sums = P.small[:, 420:436], P.small[:, 436:452], P.small[:, 452:468]
    top8 = P.small[:, 468:484]

    cm = {n: cc[:, 128 * i:128 * i + 128] for i, n in enumerate(C_MASKS)}
    adm = cc[:, 1024:1408]
    cs = {n: cc[:, 1408 + i:1409 + i] for i, n in enumerate(C_SMALL)}
    for i in range(P.NB):
        P.pe_read[i] = [P.pe_read[i], P.doneB["down", 15]]
    before = [P.x_tok[k] for k in range(KT)]

    l_cc = P.load(cc[:], A["cstc"], before, P.stage_free, q=P.pool)
    posi = P.nc.alloc_sbuf_tensor_at("posi", [128, T], I32, offset=BASE + 4 * (Z + 22544))
    l_pos = P.load(posi[:], A["positions"].partition_broadcast(128), before, P.stage_free, q=P.pool)

    def rope_tables():
        a0, a1, a2 = (at(f"rp{i}", 23056 + 256 * i, [T])[:] for i in range(3))
        t = cp(a2, posi[:], l_pos)
        for i, n in enumerate(("sa", "ix")):
            f, sg = cs["freq_" + n], cs["sign_" + n]
            for j in range(2):
                t = ts(a0, a2, f, None, OP.mult, None, t, l_cc)
                t = ts(a1, a0, 1.0 / TURN, 0.25 * (1 - j), OP.mult, OP.add, t)
                t = ts(a1, a1, 12582912.0, -12582912.0, OP.add, OP.add, t)
                for c in (TURN1, TURN2, TURN3):
                    t = stt(a0, a1, -c, a0, OP.mult, OP.add, t)
                if j == 0:
                    t = ts(a0, a0, TURN / 4, None, OP.add, None, t)
                t = ts(a0, a0, HALF_TURN, -HALF_TURN, OP.min, OP.max, t)
                t = af(rope[:, 2 * i + j, :], a0, AF.Sin, t, before)
                if j == 1:
                    t = ts(rope[:, 2 * i + 1, :], rope[:, 2 * i + 1, :], sg, None, OP.mult, None, t)
                P.rope_tok = [t]
    P.rope_tok = []
    rope_tables()

    SW16 = list(range(16, 32)) + list(range(16))
    SW8 = list(range(8, 16)) + list(range(8)) + list(range(16, 32))

    def rotate(a, n, ci, tmp, mask_, *w):
        p = a.shape[0]
        cos, sin = (bc(rope[0:p, 2 * ci + j, :], n, 1) for j in range(2))
        t0 = P.dve.do(lambda e: e.stream_shuffle(tmp, a, mask_), *w)
        t1 = tt(tmp, tmp, sin, OP.mult, t0, P.rope_tok)
        t2 = tt(a, a, cos, OP.mult, t0, P.rope_tok)
        return tt(a, a, tmp, OP.add, t1, t2)

    def norm(gname, l, xt, *w):
        t = af(hsq[:], x[:], AF.Square, xt, *w)
        for k in range(KT):
            t2 = mm(B[7].t[:, 0:T], ONE, hsq[:, k, :], k == 0, k == KT - 1, t, B[7].free)
        t = af(rs[:], B[7].t[:, 0:T], AF.Ln, t2, *w, bias=EPS, scale=1.0 / 1024)
        B[7].free = [t]
        t = af(rs[:], rs[:], AF.Exp, t, scale=-0.5)
        for k in range(KT):
            t3 = stt(hn[:, k, :], x[:, k, :], col(gname, 8 * l + k), rs[:], OP.mult, OP.mult, t, xt, *w)
            P.split_x(H, k, hn[:, k, :], t3, *w)

    def layer(l):
        done = {}
        w_in = A["w_in_2"][l]
        need = lambda *ks: P.need(done, *ks)
        xt = [P.x_tok[k] for k in range(KT)]
        ffn_free = [P.ffn_free]
        act_free = [P.gate_free]

        ld = []
        for i in range(2):
            ld.append(P.fill(wsm[i][:], 0.0, xt, act_free, P.rope_tok, on=P.pool))
        l_sm = [P.load(wsm[0][:, :, 32 * i:32 * i + 8], A["w_small"][l, i], ld, q=P.pool) for i in range(3)]
        l_sm += [P.load(wsm[1][:, :, 64 * i:64 * i + 64], A["w_ik"][l], ld, q=P.pool) for i in range(2)]
        l_al = [P.load(alog[0:8, 0:1], A["a_log"][l], P.alog_free, q=P.pool),
                P.load(alog[0:8, 1:2], A["dt_bias"][l], P.alog_free, q=P.pool)]
        if l == 1:
            def kv1():
                P.kv_tok = []
                for n in range(16):
                    if n in P.kv1_at:
                        i, v = P.kv1_at[n]
                        dst = pa(P.mk[:, 4 * i + 2 * v:4 * i + 2 * v + 2, :]) if i < 2 else P.mv[:, v, 512 * (i - 2):512 * (i - 2) + 512]
                        P.kv_tok.append(P.load(dst, A["kv1"][:, 512 * n:512 * n + 512], P.kv1_tok[n], xt, q=P.pool))
            P.call(kv1)
        P.call(lambda: norm("norm_mix_2", l, xt, ffn_free, before))

        def fm_one(i, dst):
            def f(q):
                bk = P.bank()
                for k in range(KT):
                    for w, v, wt in ((q.hi, H.hi, q.th), (q.hi, H.lo, q.th), (q.lo, H.hi, q.tl)):
                        t = mm(bk.t[:, 0:T], w[:, k, :], v[:, k, :], k == 0 and v is H.hi and w is q.hi,
                               k == KT - 1 and w is q.lo, wt, H.tok[k], bk.free)
                done["small", i] = acp(dst[:], bk.t[:, 0:T], t, xt, ffn_free)
                bk.free = [done["small", i]]
                return t
            return f

        def strengths():
            yield from need(("small", 0))
            w = done["small", 0]
            z, tmp = smT[0:8, :], relu[0:8, 0:256]
            t = af(alog[0:8, 2:3], alog[0:8, 0:1], AF.Exp, l_al)
            t0 = ts(alog[0:8, 2:3], alog[0:8, 2:3], -1.0, None, OP.mult, None, t)
            t = af(tmp, z, AF.Abs, w, l_al, bias=alog[0:8, 1:2])
            t = af(tmp, tmp, AF.Exp, t, scale=-1.0)
            t1 = af(tmp, tmp, AF.Ln, t, bias=ONE[0:8, 0:1])
            t = ts(z, z, alog[0:8, 1:2], 0.0, OP.add, OP.max, t1)
            t = tt(z, z, tmp, OP.add, t)
            t = ts(z, z, alog[0:8, 2:3], None, OP.mult, None, t, t0)
            P.alog_free = [t]
            for c in range(2):
                s_ = smT[0:8, 128 * c:128 * c + 128]
                t2 = P.dve.do(lambda e, s_=s_: e.tensor_tensor_scan(s_, s_, s_, 0.0, OP.add, OP.bypass), t)
            t3 = af(smT[32:40, :], smT[32:40, :], AF.Sigmoid, w)
            done["gcT"] = t2
            yield
            for c in range(2):
                t4 = tp(B[7].t[:, 128 * c:128 * c + 72], smT[0:72, 128 * c:128 * c + 128], t2, t3, B[7].free)
            for c in range(2):
                t = cp(tokm[:, c, :], B[7].t[:, 128 * c:128 * c + 72], t4, P.tokm_free)
            t = ts(tokm[:, :, 64:72], tokm[:, :, 64:72], 512 ** -0.5, None, OP.mult, None, t)
            B[7].free = [t]
            done["tokm"] = t
            yield
            t5 = mm(B[7].t[:, 0:8], cm["last"], tokm[:, 0, 0:8], True, True, t, B[7].free, l_cc)
            t = tt(ekd, B[7].t[:, 0:8], tokm[:, 0, 0:8], OP.subtract, t5, P.tokm_free)
            B[7].free = [t]
            done["ekd"] = af(ekd, ekd, AF.Exp, t)

        def index():
            yield from need("tokm", ("iq", 0), ("iq", 1), ("small", 1))
            ti = rotate(iq[:], 4, 1, D[:].rearrange("p a b c -> p (a b c)").rearrange("p (n t) -> p n t", n=4), SW8,
                        done["iq", 0], done["iq", 1], xt, ffn_free)
            tk = rotate(ik[:].unsqueeze(1), 1, 1, relu[:, 0:256].unsqueeze(1), SW8, done["small", 1], done["gcT"], ti)
            yield
            tr = [done["tokm"], tk]
            ta = [None, None]
            for h in range(8):
                ps = slice(64 * (h % 2), 64 * (h % 2) + 64)
                bk = B[3 + h % 2]
                for b in range(2):
                    n = 128 * (b + 1)
                    t = mm(bk.t[:, 128 * b:128 * b + n], iq[ps, h // 2, 128 * b:128 * b + 128], ik[ps, 0:n], b == 0, b == 1,
                           ti, tk, bk.free)
                t = af(relu[:, 0:384], bk.t[:, 0:384], AF.Relu, t, tr, ta)
                bk.free = [t]
                for b in range(2):
                    o_, n = 128 * b, 128 * (b + 1)
                    ta[b] = stt(score[:, o_:o_ + n], relu[:, o_:o_ + n], tokm[:, b, 64 + h:65 + h],
                                (adm if h == 0 else score)[:, o_:o_ + n], OP.mult, OP.add, t, ta[b], l_cc)
                yield
            for r in range(8):
                for b in range(2):
                    o_, n = 128 * b, 128 * (b + 1)
                    t8 = top8[:, 8 * b:8 * b + 8]
                    t = P.dve.do(lambda e, t8=t8, o_=o_, n=n: e.max(t8, score[:, o_:o_ + n]), ta[b])
                    ta[b] = P.dve.do(lambda e, t8=t8, o_=o_, n=n: e.match_replace(
                        score[:, o_:o_ + n], t8, score[:, o_:o_ + n], TAKEN), t)
                if r % 2:
                    yield
            done["maskb"] = ts(maskb[:], score[:], 0.5 * TAKEN, BIG, OP.is_gt, OP.mult, ta, P.maskb_free)

        nr = [0]

        def conv_in(kind, g):
            def f(xp, b, c, t):
                n = nr[0]
                nr[0] += 1
                r_, y_ = raw[n % 2], Y[n % 2]
                h = 2 * ((c % 512) // 256)
                hh = 4 * g + h
                bank = bnk(b)
                tc = [acp(r_[:, :, 3:259], b[:].rearrange("p (a t) -> p a t", a=2), t, conv_free[n % 2], zero_t)]
                ty = []
                for a in range(2):
                    w = lambda j, a=a: col("conv_w_2", 96 * l + 24 * j + 8 * kind + hh + a)
                    t2 = ts(y_[:, a, :], r_[:, a, 3:259], w(3), None, OP.mult, None, tc, conv_free[n % 2])
                    for j in range(3):
                        t2 = stt(y_[:, a, :], r_[:, a, j:j + 256], w(j), y_[:, a, :], OP.mult, OP.add, t2)
                    ty.append(t2)
                ts_ = af(pa(y_[:]), pa(y_[:]), AF.Silu, ty)
                if kind == 2:
                    bk = B[3]
                    for a in range(2):
                        for q in range(2):
                            t3 = tp(bk.t[:, 256 * a + 128 * q:256 * a + 128 * q + 128], y_[:, a, 128 * q:128 * q + 128], ts_,
                                    bk.free)
                    r = acp(V[g][:, h:h + 2].rearrange("p a b c -> p (a b c)"), bk.t[:], t3, xt, ffn_free)
                    bk.free = [r]
                    done["v", g, h] = r
                else:
                    sq2 = r_[:].rearrange("p a t -> p (a t)")[:, 0:512].rearrange("p (a t) -> p a t", a=2)
                    t3 = af(sq2, y_[:], AF.Square, ts_, ty)
                    bk = B[3]
                    for a in range(2):
                        t4 = mm(bk.t[:, 256 * a:256 * a + 256], ONE, sq2[:, a, :], a == 0, True, t3, bk.free)
                    t5 = af(pa(sq2), bk.t[:], AF.Ln, t4, bias=EPS)
                    bk.free = [t5]
                    t5 = af(pa(sq2), pa(sq2), AF.Exp, t5, scale=-0.5, bias=cs["lnq"] if kind == 0 else 0.0)
                    for a in range(2):
                        r = tt(KQ[g][:, h + a, :, 1 - kind, :], y_[:, a, :].rearrange("p (c n) -> p c n", c=2),
                               sq2[:, a, :].rearrange("p (c n) -> p c n", c=2), OP.mult, t5, xt, ffn_free)
                    zero_t[:] = [P.fill(r_[:, a, 0:3], 0.0, r) for a in range(2)]
                    done["kq"[1 - kind] if False else ("q" if kind == 0 else "k"), g, h] = r
                conv_free[n % 2] = [r] + list(zero_t)
                return tc
            return f

        bnk = lambda b: None
        conv_free = [[], []]
        zero_t = []

        def zero_raw():
            zero_t[:] = [P.fill(raw[i][:, :, 0:3], 0.0, done["small", 0], done["small", 1], P.rope_tok) for i in range(2)]
            conv_free[0] = conv_free[1] = list(zero_t) + [done["small", 0], done["small", 1]]
        c8 = lambda a: a.rearrange("p h c n -> p (h c n)")

        def delta(g):
            kq, v = KQ[g], V[g]
            yield from need("ekd", *[(n, g, h) for n in "kqv" for h in (0, 2)])
            if g == 1:
                yield from need(("dn", 0))
            pv = [done.get(("dn", 0)), done.get("maskb")] if g else [done.get("maskb")]
            if not g:
                yield from need("maskb")
                pv = [done["maskb"]]
            inp = [done[n, g, h] for n in "kqv" for h in (0, 2)]
            td, te = [], []
            for p in range(2):
                bk = B[4 + p]
                for a in range(2):
                    h = 4 * g + 2 * p + a
                    t = mm(bk.t[:, 256 * a:256 * a + 256], bc(EYE[0:32, h:h + 1].squeeze(1), 128, 1), smT[0:32, :], a == 0, a == 1,
                           done["gcT"], bk.free)
                for a in range(2):
                    h = 4 * g + 2 * p + a
                    for c in range(2):
                        t1 = ts(D[:, 2 * p + a, c, :], bk.t[:, 256 * a + 128 * c:256 * a + 128 * c + 128],
                                tokm[:, c, h:h + 1], 0.0, OP.subtract, OP.min, t, done["tokm"], pv)
                        td.append(t1)
                t = af(ER[:, 2 * p:2 * p + 2, :], bk.t[:].rearrange("p (a c n) -> p a c n", a=2, c=2)[:, :, 1, :], AF.Exp, td, pv)
                bk.free = [t]
                te.append(t)
            t = af(c8(D[:]), c8(D[:]), AF.Exp, td)
            tD = tt(D[:].rearrange("p h c n -> p (h c) n"), D[:].rearrange("p h c n -> p (h c) n"), bc(LE, 8, 1), OP.mult, t)
            bk = B[6]
            for h in range(4):
                t = tp(bk.t[:, 128 * h:128 * h + 128], kq[:, h, 0, 0, :], inp, bk.free)
            yield
            for h in range(4):
                tkd = ts(kdec[:, h, :], bk.t[:, 128 * h:128 * h + 128], ekd[:, 4 * g + h:4 * g + h + 1], None, OP.mult, None,
                         t, done["ekd"], pv)
            bk.free = [tkd]
            tM, tA = [], []
            for h in range(4):
                bk = B[4 + h]
                for c in range(2):
                    t = mm(bk.t[:, 256 * c:256 * c + 256], kq[:, h, c, 0, :], kq[:, h, c].rearrange("p a n -> p (a n)"), c == 0, c == 1,
                           inp, bk.free)
                for c in range(2):
                    t1 = stt(MT[:, h, c, :], bk.t[:, 256 * c:256 * c + 128], tokm[:, c, 32 + 4 * g + h:33 + 4 * g + h], D[:, h, c, :],
                             OP.mult, OP.mult, t, tD, pv)
                    tM.append(t1)
                t1 = tt(AT[:, h], bk.t[:].rearrange("p (c a n) -> p c a n", c=2, a=2)[:, :, 1, :], D[:, h], OP.mult, t, tD, pv)
                tA.append(t1)
                bk.free = [t1]
            tq = tt(kq[:, :, 1], kq[:, :, 1], bc(ER[:], 2, 2), OP.mult, tA, te)
            h8 = lambda a: a.rearrange("p h c n -> p (h c) n")
            t = tt(h8(D[:]), h8(MT[:]), bc(cm["sub"], 8, 1), OP.mult, tM, tA)
            tU = tt(h8(Um[:]), bc(EYE, 8, 1), h8(D[:]), OP.subtract, t, pv)
            yield
            tT = []
            for p in range(2):
                bk = B[4 + p]
                for i in range(4):
                    h, c = 2 * p + i // 2, i % 2
                    t = tp(bk.t[:, 128 * i:128 * i + 128], Um[:, h, c, :], tU, bk.free)
                r = acp(Tm[:, 2 * p:2 * p + 2].rearrange("p h c n -> p (h c n)"), bk.t[:], t, pv)
                bk.free = [r]
                tT.append(r)
            tU, tQf = [tU, tU], [None, None]
            yield
            hc = lambda a, p: a[:, 2 * p:2 * p + 2].rearrange("p h c n -> p (h c) n")
            b4 = lambda bk: bk.t[:].rearrange("p (a n) -> p a n", a=4)
            for lv in range(1, 7):
                tQ = []
                for p in range(2):
                    bk = B[4 + p]
                    for i in range(4):
                        h, c = 2 * p + i // 2, i % 2
                        t = mm(bk.t[:, 128 * i:128 * i + 128], MT[:, h, c, :], Tm[:, h, c, :], i == 0, i == 3, tM, tT[p], bk.free)
                    t = tt(hc(D[:], p), b4(bk), bc(cm[f"level{lv}"], 4, 1), OP.mult, t, tQf[p], l_cc)
                    bk.free = [t]
                    tQ.append(t)
                yield
                for p in range(2):
                    b6, b7 = B[6], B[7]
                    if lv < 6:
                        for i in range(4):
                            h, c = 2 * p + i // 2, i % 2
                            t = mm(b6.t[:, 128 * i:128 * i + 128], Um[:, h, c, :], D[:, h, c, :], i == 0, i == 3, tQ[p], tU[p], b6.free)
                    for i in range(4):
                        h, c = 2 * p + i // 2, i % 2
                        t2 = mm(b7.t[:, 128 * i:128 * i + 128], D[:, h, c, :], Um[:, h, c, :], i == 0, i == 3, tQ[p], tU[p], b7.free)
                    tQf[p] = t2
                    if lv < 6:
                        tT[p] = tt(hc(Tm[:], p), hc(Tm[:], p), b4(b6), OP.subtract, t)
                        b6.free = [tT[p]]
                    tU[p] = tt(hc(Um[:], p), hc(Um[:], p), b4(b7), OP.subtract, t2)
                    b7.free = [tU[p]]
                yield
            beta = lambda c, h: tokm[:, c, 32 + 4 * g + h:33 + 4 * g + h]
            b4_, b5, b6, b7 = B[4], B[5], B[6], B[7]
            sl = lambda h: slice(128 * h, 128 * h + 128)
            for h in range(4):
                t = mm(b4_.t[:, sl(h)], Um[:, h, 0, :], v[:, h, 0, :], h == 0, h == 3, tU, b4_.free)
            for h in range(4):
                tv = ts(v[:, h, 0, :], b4_.t[:, sl(h)], beta(0, h), None, OP.mult, None, t)
            b4_.free = [tv]
            yield
            for h in range(4):
                t = mm(b5.t[:, sl(h)], kdec[:, h, :], v[:, h, 0, :], h == 0, h == 3, tv, tkd, b5.free)
            tS = acp(ER[:].rearrange("p h n -> p (h n)"), b5.t[:], t, tq)
            b5.free = [tS]
            for h in range(4):
                t = mm(b6.t[:, sl(h)], v[:, h, 0, :], AT[:, h, 0, :], h == 0, h == 3, tv, tA, b6.free)
            to = [acp(odn[:, 4 * g:4 * g + 4, 0:128], b6.t[:].rearrange("p (h n) -> p h n", h=4), t, xt, ffn_free, P.odn_free)]
            b6.free = to
            yield
            for h in range(4):
                t = mm(b4_.t[:, sl(h)], kq[:, h, 1, 0, :], ER[:, h, :], h == 0, h == 3, tS, tq, b4_.free)
            t = tt(v[:, :, 1, :], v[:, :, 1, :], b4_.t[:].rearrange("p (h n) -> p h n", h=4), OP.subtract, t)
            b4_.free = [t]
            yield
            for h in range(4):
                t2 = mm(b5.t[:, sl(h)], Um[:, h, 1, :], v[:, h, 1, :], h == 0, h == 3, t, tU, b5.free)
            for h in range(4):
                tv = ts(v[:, h, 1, :], b5.t[:, sl(h)], beta(1, h), None, OP.mult, None, t2)
            b5.free = [tv]
            P.tokm_free = [tv]
            yield
            for h in range(4):
                mm(b6.t[:, sl(h)], v[:, h, 1, :], AT[:, h, 1, :], h == 0, False, tv, b6.free)
                t = mm(b6.t[:, sl(h)], ER[:, h, :], kq[:, h, 1, 1, :], False, h == 3, tS, tq)
            to.append(acp(odn[:, 4 * g:4 * g + 4, 128:256], b6.t[:].rearrange("p (h n) -> p h n", h=4), t, xt, ffn_free, P.odn_free))
            b6.free = [to[1]]
            o4 = odn[:, 4 * g:4 * g + 4, :]
            sqd = c8(D[:]).rearrange("p (h t) -> p h t", h=4)
            t = af(sqd, o4, AF.Square, to, tQf)
            for p in range(2):
                bk = B[4 + p]
                for a in range(2):
                    t2 = mm(bk.t[:, 256 * a:256 * a + 256], ONE, sqd[:, 2 * p + a, :], a == 0, True, t, bk.free)
                r = af(MT[:, 2 * p:2 * p + 2].rearrange("p h c n -> p (h c n)"), bk.t[:], AF.Ln, t2, tQf, bias=EPS, scale=1.0 / 128)
                bk.free = [r]
            yield
            t = af(c8(MT[:]), c8(MT[:]), AF.Exp, r, scale=-0.5)
            done["dn", g] = stt(o4, o4, col("dn_norm_2", l), c8(MT[:]).rearrange("p (h t) -> p h t", h=4), OP.mult, OP.mult, t)

        def memory(h):
            yield from need(*[("xq", i) for i in range(4)])
            bk, b2 = B[3], B[4 + h % 2]
            w = [done["xq", h], P.kv_tok]
            for b in range(2):
                for k in range(2):
                    t = mm(bk.t[:, 256 * b:256 * b + 256], xq[:, 2 * h + k, 128 * b:128 * b + 128], P.mk[:, 2 * h + k, :],
                           b == 0 and k == 0, b == 1 and k == 1, w, bk.free)
            yield
            m2, n2, s2 = mx[:, 2 * h:2 * h + 2], nmx[:, 2 * h:2 * h + 2], sums[:, 2 * h:2 * h + 2]
            p_, pt = PT[h % 2], PT[2 + h % 2]
            t = red(m2, bk.t[:].rearrange("p (b n) -> p b n", b=2), OP.max, t, P.sm_free)
            t = ts(n2, m2, -1.0 / 16, None, OP.mult, None, t)
            for b in range(2):
                t2 = af(p_[:, 256 * b:256 * b + 256], bk.t[:, 256 * b:256 * b + 256], AF.Exp, t, pt_free[h % 2], done["dn", 1],
                        bias=n2[:, b:b + 1], scale=1.0 / 16, accum=s2[:, b:b + 1])
            bk.free = [t2]
            t = rcp(s2, s2, t2)
            p3 = p_[:].rearrange("p (b n) -> p b n", b=2)
            t = tt(p3, p3, bc(s2, 256, 2), OP.mult, t)
            yield
            for k in range(2):
                for b in range(2):
                    t2 = tp(b2.t[:, 256 * k + 128 * b:256 * k + 128 * b + 128], p_[:, 256 * b + 128 * k:256 * b + 128 * k + 128], t,
                            b2.free)
            t = acp(pt[:], b2.t[:], t2, pt_free[2 + h % 2], done["dn", 1])
            b2.free = [t]
            pt_free[h % 2] = [t2]
            yield
            for j in range(2):
                for k in range(2):
                    t2 = mm(bk.t[:, 256 * j:256 * j + 256], P.mv[:, k, 256 * h + 128 * j:256 * h + 128 * j + 128],
                            pt[:, 256 * k:256 * k + 256], j == 0 and k == 0, j == 1 and k == 1, t, P.kv_tok, bk.free)
            pt_free[2 + h % 2] = [t2]
            r = acp(pa(xq[:, 2 * h:2 * h + 2, :]), bk.t[:], t2)
            bk.free = [r]
            done["xa", h] = r

        pt_free = [[], [], [], []]

        def chosen(h):
            bk, b2 = B[5 + h % 2], B[7]
            S = 128 ** -0.5
            w = [done["rq"], done["rk"]]
            for b in range(2):
                n = 128 * (b + 1)
                t = mm(bk.t[:, 128 * b:128 * b + n], sq_[:, h, 128 * b:128 * b + 128], sk_[:, h, 0:n], b == 0, b == 1, w, bk.free)
            yield
            m2, n2, s2 = mx[:, 2 * h:2 * h + 2], nmx[:, 2 * h:2 * h + 2], sums[:, 2 * h:2 * h + 2]
            p_, pt = PT[h % 2], PT[2 + h % 2]
            tb = []
            for b in range(2):
                o_, n = 128 * b, 128 * (b + 1)
                tb.append(P.dve.do(lambda e, b=b, o_=o_, n=n: e.tensor_tensor_reduce(
                    out=p_[:, o_:o_ + n], in0=bk.t[:, o_:o_ + n], in1=maskb[:, o_:o_ + n], op0=OP.add, op1=OP.max, scale=S,
                    scalar=-3e38, accum_out=m2[:, b:b + 1]), t, done["maskb"], pt_free[h % 2], xa_done()))
            bk.free = [tb]
            t = ts(n2, m2, -1.0, None, OP.mult, None, tb)
            for b in range(2):
                o_, n = 128 * b, 128 * (b + 1)
                t2 = af(p_[:, o_:o_ + n], p_[:, o_:o_ + n], AF.Exp, t, bias=n2[:, b:b + 1], accum=s2[:, b:b + 1])
            t = rcp(s2, s2, t2)
            for b in range(2):
                o_, n = 128 * b, 128 * (b + 1)
                t3 = ts(p_[:, o_:o_ + n], p_[:, o_:o_ + n], s2[:, b:b + 1], None, OP.mult, None, t)
            yield
            for i in range(3):
                t2 = tp(b2.t[:, 128 * i:128 * i + 128], p_[:, 128 * i:128 * i + 128], t3, b2.free)
            t = acp(pt[:, 0:384], b2.t[:, 0:384], t2, pt_free[2 + h % 2], xa_done())
            b2.free = [t]
            pt_free[h % 2] = [t2]
            yield
            mm(bk.t[:, 0:256], sv_[:, 0, 128 * h:128 * h + 128], pt[:, 0:256], True, False, t, done["sv"], bk.free)
            t2 = mm(bk.t[:, 128:256], sv_[:, 1, 128 * h:128 * h + 128], pt[:, 256:384], False, True)
            pt_free[2 + h % 2] = [t2]
            r = acp(osa[:, h, :], bk.t[:, 0:256], t2, done["dn", 1])
            bk.free = [r]
            done["sa", h] = r

        xa_done = lambda: [done["xa", h] for h in range(4)]

        def attend():
            yield from need(*[("xq", i) for i in range(4)], ("dn", 1))
            for h in range(4):
                yield from memory(h)
            done["xa"] = xa_done()
            yield from need(*[(n, i) for n in ("sq", "sk", "sv_") for i in range(4)])
            tmp = wsq[0:32]
            done["rq"] = rotate(sq_[0:32], 8, 0, tmp, SW16, [done["sq", i] for i in range(4)], done["dn", 1])
            yield
            done["rk"] = rotate(sk_[0:32], 8, 0, tmp, SW16, [done["sk", i] for i in range(4)], done["rq"])
            done["sv"] = [done["sv_", i] for i in range(4)]
            yield
            gs = [chosen(h) for h in range(8)]
            live = []
            while gs or live:
                if gs and len(live) < 2:
                    live.append(gs.pop(0))
                for g_ in list(live):
                    try:
                        next(g_)
                    except StopIteration:
                        live.remove(g_)
                    yield
            done["sa"] = [done["sa", h] for h in range(8)]
            P.maskb_free = [done["sa"]]
        wsq = P.wsq

        def ev_copy(name, dst, base, *w):
            def f(xp, b, c, t):
                j = (c - base) // 128
                done[name, j // 2] = r = acp(pa(dst[:, j:j + 2, :]), b[:], t, *[u() for u in w])
                return r
            return f

        def ev_tm(name, dst, base, *w):
            def f(xp, b, c, t):
                j = c - base
                done[name, j // 256] = r = acp(dst[:, :, j:j + 256], b[:].rearrange("p (a n) -> p a n", a=2), t, *[u() for u in w])
                return r
            return f
        fr = lambda: [xt, ffn_free]
        P.sides += [strengths(), index(), delta(0), delta(1), attend()]
        P.source(("sm", l, 0), wsm[0][:], l_sm, 8, fm_one(0, smT))
        P.source(("sm", l, 1), wsm[1][:], l_sm, 8, fm_one(1, ik))
        P.call(zero_raw)
        P.units(("iq", l), w_in, 7184, [H], False, ev_copy("iq", iq, 7184, fr))
        for g in range(2):
            if g == 1:
                pass
            for kind, o_, n in ((1, 1024, "dk"), (0, 0, "dq"), (2, 2048, "dv")):
                P.units((n, l, g), w_in, o_ + 512 * g, [H], False, conv_in(kind, g))
        P.until(done, ("dn", 0))
        for i in range(2):
            P.units(("xq", l, i), w_in, 7768 + 512 * i, [H], False, ev_copy("xq", xq, 7768, lambda: [done["dn", 0]]))
        P.until(done, ("dn", 1))
        dn1 = lambda: [done["dn", 1]]
        for i in range(2):
            P.units(("sq", l, i), w_in, 4112 + 512 * i, [H], False, ev_copy("sq", sq_, 4112, dn1))
        for i in range(2):
            P.units(("sk", l, i), w_in, 5136 + 512 * i, [H], False, ev_copy("sk", sk_, 5136, dn1))
        for i in range(2):
            P.units(("sv", l, i), w_in, 6160 + 512 * i, [H], True, ev_tm("sv_", sv_, 6160, dn1))

        DN, XA, SA = Part(hiA, at("o_lo0", 16384, [KT, T], F32R)), Part(hiB, at("o_lo1", 4096, [KT, T], F32R)), Part(
            hiA, at("o_lo2", 6144, [KT, T], F32R))

        def ev_z(xp, b, c, t):
            j = (c - 3072) // 128
            z = Y[(j // 2) % 2]
            t = af(pa(z[:]), b[:], AF.Silu, t, done["dn", 1], done.get(("z", j // 2 - 2)))
            r = tt(pa(odn[:, j:j + 2, :]), pa(odn[:, j:j + 2, :]), pa(z[:]), OP.mult, t, done["dn", 0], done["dn", 1])
            done["z", j // 2] = r
            for a in range(2):
                P.split_x(DN, j + a, odn[:, j + a, :], r, done["maskb"])
            return t

        def ev_gl(br, gt_, *w):
            def f(xp, b, c, t):
                j = (c - 8792 - 1024 * br) // 128
                for a in range(2):
                    r = af(gt_[:, j + a, :], b[:, 256 * a:256 * a + 256], AF.Sigmoid, t, *[u() for u in w],
                           bias=col("b_gate_2", 24 * l + 8 * br + j + a))
                done["g", br, j // 2] = r
                return r
            return f

        def ev_br(br, gt_, first, last):
            def f(xp, b, c, t):
                j = c // 128
                g2, m2 = pa(gt_[:, j:j + 2, :]), pa(mg[:, j:j + 2, :])
                if first:
                    done["m", br, j // 2] = r = tt(m2, b[:], g2, OP.mult, t, done["g", br, j // 2], done["xa"])
                    return r
                r = tt(g2, b[:], g2, OP.mult, t, done["g", br, j // 2])
                t = done["m", br, j // 2] = tt(m2, m2, g2, OP.add, r, done["m", first_of(br), j // 2])
                if last:
                    for a in range(2):
                        P.split_x(MG, j + a, mg[:, j + a, :], t, done["bx"])
                return r
            return f
        order = [0, 2, 1]
        first_of = lambda br: order[order.index(br) - 1]
        MG = Part(hiB, P.at("m_lo", Z + 26576, [KT, T], F32R))

        def split_o(part, o_, key, *w):
            def f():
                for k in range(KT):
                    P.split_x(part, k, o_[:, k, :], done[key], *[u() for u in w])
            return f

        P.units(("dz", l, 0), w_in, 3072, [H], False, ev_z)
        P.units(("dz", l, 1), w_in, 3584, [H], False, ev_z)
        for i in range(2):
            P.units(("gl0", l, i), w_in, 8792 + 512 * i, [H], False,
                    ev_gl(0, gate[0], lambda: [done["z", 3], done["z", 2], done["maskb"], conv_free]))
        P.until(done, "xa")
        for i in range(2):
            P.units(("wb0", l, i), A["w_branch_2"][l, 0], 512 * i, [DN], False, ev_br(0, gate[0], True, False))
        P.until(done, "sa")
        P.call(split_o(XA, xq, "xa"))
        for i in range(2):
            P.units(("gl2", l, i), w_in, 8792 + 2048 + 512 * i, [H], False, ev_gl(2, gate[1], lambda: [done["sa"]]))
        for i in range(2):
            P.units(("wb2", l, i), A["w_branch_2"][l, 2], 512 * i, [XA], False, ev_br(2, gate[1], False, False))
        P.call(split_o(SA, osa, "sa", lambda: [done["m", 0, 3]]))
        for i in range(2):
            P.units(("gl1", l, i), w_in, 8792 + 1024 + 512 * i, [H], False, ev_gl(1, gate[0], lambda: [
                done["m", 0, i] for i in range(4)]))

        def mark():
            done["bx"] = [done["m", 2, i] for i in range(4)]
        P.call(mark)
        for i in range(2):
            P.units(("wb1", l, i), A["w_branch_2"][l, 1], 512 * i, [SA], False, ev_br(1, gate[0], False, True))

        def ev_o(xp, b, c, t):
            j = c // 128
            r = tt(pa(x[:, j:j + 2, :]), pa(x[:, j:j + 2, :]), b[:], OP.add, t)
            P.x_tok[j] = P.x_tok[j + 1] = r
            return r
        for i in range(2):
            P.units(("wo", l, i), A["w_out_2"][l], 512 * i, [MG], False, ev_o)

        P.call(lambda: norm("norm_ffn_2", l, [P.x_tok[k] for k in range(KT)], done["sa"], done["m", 1, 3]))

        def ev_g(i):
            def f(xp, b, c, t):
                j = c // 128 - 4 * i
                done["fg", i, j // 2] = r = af(pa(fg[i % 2][:, j:j + 2, :]), b[:, 0:512], AF.Silu, t,
                                               [done.get(("fu", i - 2, u)) for u in range(2)], H.tok[KT - 1], done["m", 1, 3])
                return r
            return f

        def ev_u(i):
            def f(xp, b, c, t):
                j = (c - 2816) // 128 - 4 * i
                n = done.get("nf", 0)
                done["nf"] = n + 1
                a_ = fa[n % 2]
                r = tt(a_[:], b[:, 0:512], pa(fg[i % 2][:, j:j + 2, :]), OP.mult, t, done["fg", i, j // 2], ffa_free[n % 2],
                       H.tok[KT - 1])
                done["fu", i, j // 2] = r
                k0 = 4 * i + j
                th = acp(pa(FH[:, k0:k0 + 2, :]), a_[:], r, done["m", 1, 3])
                tl = tt(pa(FL[:, k0:k0 + 2, :]), a_[:], pa(FH[:, k0:k0 + 2, :]).bitcast(F32), OP.subtract, th)
                ffa_free[n % 2] = [th, tl]
                for a in range(2):
                    ftok[k0 + a] = [th, tl]
                return r
            return f
        ffa_free, ftok = [[], []], {}
        for i in range(5):
            P.units(("fg", l, i), A["w_ffn_in_2"][l], 512 * i, [H], False, ev_g(i))
            P.units(("fu", l, i), A["w_ffn_in_2"][l], 2816 + 512 * i, [H], False, ev_u(i))
        P.want(("fl", l), [P.block(A["w_ffn_in_2"][l], 2560, n=256), P.block(A["w_ffn_in_2"][l], 5376, n=256, o=2048)])
        for u, ev, c0 in ((0, ev_g(5), 2560), (1, ev_u(5), 5376)):
            P.unit_at(("fl", l), 2048 * u, 256, [H], ev, c0, u == 1)
        acc = [B[4 + i] for i in range(4)]

        def ffn_out(k):
            def f(q):
                for j in range(8):
                    bk = acc[j // 2]
                    for w, v, wt in ((q.hi, FH, q.th), (q.hi, FL, q.th), (q.lo, FH, q.tl)):
                        t = mm(bk.t[:, 256 * (j % 2):256 * (j % 2) + 256], w[:, 0, 128 * j:128 * j + 128], v[:, k, :],
                               k == 0 and j % 2 == 0 and v is FH and w is q.hi, k == 21 and w is q.lo, wt, ftok[k],
                               bk.free if k == 0 else None)
                if k == 21:
                    for i in range(4):
                        r = tt(pa(x[:, 2 * i:2 * i + 2, :]), pa(x[:, 2 * i:2 * i + 2, :]), acc[i].t[:], OP.add, t)
                        acc[i].free = [r]
                        P.x_tok[2 * i] = P.x_tok[2 * i + 1] = r
                    P.ffn_free = r
                    P.gate_free = [done["m", 1, i] for i in range(4)]
                return t
            return f
        for i in range(6):
            n = 4 if i < 5 else 2
            P.want(("fo", l, i), [P.block(A["w_ffn_out_2"][l], 0, n=1024, k0=4 * i, kt=n)])
            for k in range(n):
                P.quarter(("fo", l, i), 1, lambda s, k=k: s[:, 1024 * k:1024 * k + 1024].unsqueeze(1), k == n - 1,
                          ffn_out(4 * i + k))

    P.ffn_free, P.gate_free, P.alog_free, P.tokm_free, P.maskb_free, P.odn_free, P.sm_free = [], [], [], [], [], [], []
    P.wsq = at("wsq", 14336, [KT, T])
    for l in range(2):
        layer(l)
        P.run(1)
        P.drain()
    xt = [P.x_tok[k] for k in range(KT)]
    t = af(hsq[:], x[:], AF.Square, xt)
    for k in range(KT):
        t2 = mm(B[7].t[:, 0:T], ONE, hsq[:, k, :], k == 0, k == KT - 1, t, B[7].free)
    t = af(rs[:], B[7].t[:, 0:T], AF.Ln, t2, bias=EPS, scale=1.0 / 1024)
    t = af(rs[:], rs[:], AF.Exp, t, scale=-0.5)
    fin = []
    for k in range(KT):
        t3 = stt(x[:, k, :], x[:, k, :], col("norm_final_2", k), rs[:], OP.mult, OP.mult, t)
        if k % 4 == 3:
            fin.append(P.load(out[:, k - 3:k + 1, :], x[:, k - 3:k + 1, :], t3))
    return fin


def build(nc, A, out, stop=None):
    with ExitStack() as ctx:
        A = dict(A, kv1=nc.dram_tensor("kv1", (128, 4096), F32, kind="Internal").ap())
        P = Program(nc, A, ctx)
        phase_a(P)
        P.run(2)
        phase_b(P)
        P.run(2)
        P.drain()
        P.finish(phase_c(P, out), list(P.kv1_tok.values()))


def fm(a):
    return np.ascontiguousarray(a.T.reshape(-1, 128, a.shape[0]).transpose(1, 0, 2))


def layout(inp):
    g = {k: np.asarray(v) for k, v in inp.items()}
    d = {"xT": fm(g["x"][0]), "ctxT": fm(g["ctx"][0]), "cst": constants()}
    d["cols"] = np.ascontiguousarray(np.concatenate([g[n].reshape(-1, 128).T for n, _ in COLS], axis=1))
    d["w_mod"], d["w_in"] = g["w_mod"][0], g["w_in"][0]
    d["w_lr"] = np.ascontiguousarray(g["w_in"][0][:, 5120:5152].reshape(8, 128, 32).transpose(1, 0, 2))
    d["w_gate2"] = g["w_gate2"][0]
    d["sgu_wT"] = np.ascontiguousarray(g["sgu_w"][0].transpose(2, 0, 1))
    d["sgu_b"], d["sgu_ln_g"], d["sgu_ln_b"] = g["sgu_b"][0], g["sgu_ln_g"][0], g["sgu_ln_b"][0]
    d["memT"] = fm(g["mem_2"][0])
    d["w_mem_kv"], d["w_router"] = g["w_mem_kv_2"], np.ascontiguousarray(g["w_router"].reshape(8, 128, 16).transpose(1, 0, 2))
    d["b_router"] = g["b_router"].reshape(16, 1)
    d["w_eg"], d["w_eu"], d["w_ed"] = g["w_exp_gate"][0], g["w_exp_up"][0], g["w_exp_down"][0]
    d["cstc"] = constants_c()
    d["positions"] = g["positions_2"][0]
    d["w_in_2"] = w = g["w_in_2"]
    pk = lambda a: np.ascontiguousarray(a.reshape(8, 128, -1).transpose(1, 0, 2))
    d["w_small"] = np.stack([np.stack([pk(w[i][:, c:c + 8]) for c in (4104, 4096, 7760)]) for i in range(2)])
    d["w_ik"] = np.stack([pk(w[i][:, 7696:7760]) for i in range(2)])
    d["a_log"], d["dt_bias"] = g["a_log_2"].reshape(2, 8, 1), g["dt_bias_2"].reshape(2, 8, 1)
    d["w_branch_2"], d["w_out_2"] = g["w_branch_2"], g["w_out_2"]
    d["w_ffn_in_2"], d["w_ffn_out_2"] = g["w_ffn_in_2"], g["w_ffn_out_2"]
    d["w_a"], d["w_b"], d["w_o"] = g["w_branch_a"][0], g["w_branch_b"][0], g["w_out"][0]
    return d


def kernel(**inputs):
    import concourse.bacc as _bacc
    from concourse.bass_utils import run_bass_kernel_spmd as _run

    nc = _bacc.Bacc("TRN2", target_bir_lowering=False, num_devices=1)
    arrays, aps = {}, {}
    for name, a in layout(inputs).items():
        arrays[f"in_{name}_dram"] = a = np.ascontiguousarray(a)
        aps[name] = nc.dram_tensor(f"in_{name}_dram", a.shape, mybir.dt.from_np(a.dtype), kind="ExternalInput").ap()
    out = nc.dram_tensor("out_0_dram", (128, KT, T), F32, kind="ExternalOutput").ap()
    build(nc, aps, out)
    r = _run(nc, [arrays], core_ids=[0])
    o = r.results[0]["out_0_dram"]
    return np.ascontiguousarray(o.transpose(2, 1, 0)).reshape(1, T, 1024)
```

```python
import numpy as np
import concourse.bass as bass
from concourse import mybir
from contextlib import ExitStack

F32 = mybir.dt.float32
F32R = mybir.dt.float32r
I32 = mybir.dt.int32
AF = mybir.ActivationFunctionType
OP = mybir.AluOpType
AX = mybir.AxisListType

T = 256
KT = 8
BASE = 16512

COLS = [("c", 8), ("c_ctx", 8), ("b_mod", 48), ("g_norm1", 8), ("g_norm2", 8), ("b_gate2", 8),
        ("gla_norm_g", 8), ("sgu_ln_g", 8), ("sgu_ln_b", 8), ("b_branch", 16), ("g_final", 8),
        ("norm_mix_2", 16), ("norm_mem_2", 16), ("b_gate_2", 48), ("conv_w_2", 192), ("dn_norm_2", 2),
        ("norm_ffn_2", 16), ("norm_final_2", 8)]
COL = {}
for _n, _c in COLS:
    COL[_n] = sum(c for _, c in COLS[:len(COL)])
NCOL = sum(c for _, c in COLS)

MASKS = ["one", "eye", "le", "ge", "lt", "gt"]


def constants():
    p, f = np.meshgrid(np.arange(128), np.arange(128), indexing="ij")
    m = {"one": p >= 0, "eye": p == f, "le": p <= f, "ge": p >= f, "lt": p < f, "gt": p > f}
    small = np.zeros((128, 128), np.float32)
    small[:, 0] = 1e-6
    small[:, 1] = np.pi / 2
    small[:, 16:32] = 16.0 - np.arange(16)
    small[:, 32:36] = 4.0 - np.arange(4)
    small[:, 36:40] = 64.0 * np.arange(4)
    small[:, 64:128] = np.arange(64)
    return np.concatenate([m[n].astype(np.float32) for n in MASKS] + [small], axis=1)


class Tok:

    def __init__(self, sem=None, count=0):
        self.sem, self.count, self.used = sem, count, False


def flat(waits):
    for w in waits:
        if isinstance(w, Tok):
            yield w
        elif w is not None:
            yield from flat(w)


class Stream:

    def __init__(self, sem):
        self.sem, self.q = sem, []

    def do(self, fn, *waits, tok=None):
        t, ws = tok or Tok(), list(flat(waits))
        for w in ws:
            w.used = True
        self.q.append((fn, ws, t))
        return t

    def count(self):
        n = 0
        for _, _, t in self.q:
            if t.used and t.sem is None:
                n += 1
                t.sem, t.count = self.sem, n

    def emit(self, e):
        seen = {}
        for fn, ws, t in self.q:
            for w in ws:
                if seen.get(w.sem.name, 0) < w.count:
                    e.wait_ge(w.sem, w.count)
                    seen[w.sem.name] = w.count
            i = fn(e)
            if t.sem is self.sem:
                i.then_inc(self.sem, 1)


class Bank:

    def __init__(self, t):
        self.t, self.free = t, []


class Part:

    def __init__(self, hi, lo):
        self.hi, self.lo, self.tok = hi, lo, {}


class Slot:

    def __init__(self, t, r, sem, i):
        self.t, self.r, self.sem, self.n, self.i = t, r, sem, 0, i


class Quarter:

    def __init__(self, hi, lo, th, tl, b):
        self.hi, self.lo, self.th, self.tl, self.b = hi, lo, th, tl, b


class Program:
    NB = 6
    SLOT = 4096

    def __init__(self, nc, A, ctx):
        self.nc, self.A, self.ctx = nc, A, ctx
        self.pe, self.act, self.dve, self.pool, self.sp = (
            Stream(self.sem("done_" + n)) for n in ("pe", "act", "dve", "pool", "sp"))
        self.nload = 0
        ctx.enter_context(nc.sbuf_tensor("arena", [128, 53200], F32))
        self.banks = [Bank(ctx.enter_context(nc.psum_tensor(f"bank{i}", [128, 512], F32))) for i in range(8)]

        self.pf = self.at("pf", 0, [NCOL])
        self.cst = self.at("cst", 448, [7 * 128])
        self.x = self.at("x", 1536, [KT, T])
        self.small = self.at("small", 3584, [512])
        hl = 4096
        self.hib = [self.at(f"hib{i}", hl + 1024 * i, [1024], F32R) for i in range(self.NB)]
        self.R0 = hl + 1024 * self.NB
        self.Z = self.R0 + 3 * self.SLOT
        self.mask = {n: self.cst[:, 128 * i:128 * i + 128] for i, n in enumerate(MASKS)}
        self.ONE, self.EYE = self.mask["one"], self.mask["eye"]
        self.sm = self.cst[:, 128 * len(MASKS):128 * len(MASKS) + 128]
        self.EPS = self.sm[:, 0:1]

        self.want_, self.held, self.idle, self.lastslot = [], {}, [], {}
        self.todo, self.nq, self.nsplit, self.ahead, self.rot = [], 0, 0, 0, 0
        self.pe_read = [[] for _ in range(self.NB)]
        self.lanes = []

    def sem(self, n):
        return self.ctx.enter_context(self.nc.semaphore(n))

    def at(self, name, off, shape, dt=F32):
        return self.nc.alloc_sbuf_tensor_at(name, [128] + shape, dt, offset=BASE + 4 * off)

    def col(self, n, i=0, k=1):
        return self.pf[:, COL[n] + i:COL[n] + i + k]

    def mm(self, out, l, r, start, stop, *w):
        return self.pe.do(lambda e: e.matmul(out, l, r, start=start, stop=stop, skip_group_check=True), *w)

    def tp(self, out, i, *w):
        k = i.shape[0]
        p0 = 0
        return self.pe.do(lambda e: e.transpose(out, i, self.EYE[0:k, 0:k]), *w)

    def af(self, out, i, func, *w, bias=0.0, scale=1.0, accum=None):
        return self.act.do(lambda e: e.activation(out, i, func, bias=bias, scale=scale, accum_out=accum), *w)

    def acp(self, out, i, *w):
        return self.act.do(lambda e: e.copy(out, i), *w)

    def tt(self, out, a, b, op, *w, on=None):
        return (on or self.dve).do(lambda e: e.tensor_tensor(out, a, b, op), *w)

    def ts(self, out, a, s1, s2, o1, o2, *w, on=None):
        if s2 is None:
            return (on or self.dve).do(lambda e: e.tensor_scalar(out, a, s1, None, o1), *w)
        return (on or self.dve).do(lambda e: e.tensor_scalar(out, a, s1, s2, o1, o2), *w)

    def stt(self, out, a, s, b, o1, o2, *w, rev1=False):
        return self.dve.do(lambda e: e.scalar_tensor_tensor(
            out=out, in0=a, scalar=s, in1=b, op0=o1, op1=o2, reverse1=rev1), *w)

    def cp(self, out, i, *w, on=None):
        return (on or self.dve).do(lambda e: e.tensor_copy(out, i), *w)

    def rcp(self, out, i, *w):
        return self.dve.do(lambda e: e.reciprocal(out, i), *w)

    def red(self, out, i, op, *w):
        return self.dve.do(lambda e: e.tensor_reduce(out, i, AX.X, op), *w)

    def fill(self, out, v, *w, on=None):
        return (on or self.dve).do(lambda e: e.memset(out, v), *w)

    def raw(self, stream, fn, *w):
        stream.do(fn, *w)

    def load(self, out, src, *w, q=None):
        self.nload += 1
        s = self.sem(f"load{self.nload}")
        return (q or self.sp).do(lambda e: e.dma_start(out, src).then_inc(s, 16), *w, tok=Tok(s, 16))

    def add_slot(self, i, off, *free):
        s = Slot(self.at(f"slot{i}", off, [self.SLOT]), self.at(f"slot{i}r", off, [self.SLOT], F32R), self.sem(f"ring{i}"), i)
        self.idle.append((s, list(flat(free))))
        self.pump()

    def pump(self):
        while self.want_ and self.idle:
            key, parts, zone = self.want_[0]
            k = next((j for j, (s, _) in enumerate(self.idle) if s.i < zone), None)
            if k is None:
                return
            s, free = self.idle.pop(k)
            self.want_.pop(0)
            for view, src in parts:
                s.n += 16
                self.sp.do(lambda e, o=view(s.t), i=src, s=s: e.dma_start(o, i).then_inc(s.sem, 16), free,
                           tok=Tok(s.sem, s.n))
            self.held[key] = (s, Tok(s.sem, s.n))

    def want(self, key, parts, zone=3):
        self.want_.append((key, parts, zone))
        self.pump()

    def release(self, key, *read):
        s, _ = self.held.pop(key)
        self.idle.append((s, list(flat(read))))
        self.pump()

    @staticmethod
    def block(w, c0, n=512, k0=0, kt=8, o=0):
        return (lambda t: t[:, o:o + kt * n].rearrange("p (k n) -> p k n", k=kt),
                w[128 * k0:128 * (k0 + kt), c0:c0 + n].rearrange("(k p) n -> p k n", p=128))

    def split_w(self, src, lo, k, ld):
        b = self.nq % self.NB
        self.nq += 1
        n = src.shape[-1]
        hi = self.hib[b][:].rearrange("p (k n) -> p k n", k=k)[:, :, 0:n]
        th = self.acp(hi, src, ld, self.pe_read[b])
        tl = self.tt(lo, src, hi.bitcast(F32), OP.subtract, ld, th)
        return Quarter(hi, lo, th, tl, b)

    def split_x(self, part, k, src, *w):
        th = self.acp(part.hi[:, k, :], src, *w)
        tl = self.tt(part.lo[:, k, :], src, part.hi[:, k, :].bitcast(F32), OP.subtract, th, *w)
        part.tok[k] = [th, tl]

    def bank(self):
        self.rot += 1
        return self.banks[self.rot % 3]

    def plain(self, key, fn):
        self.todo.append(("plain", key, fn))

    def call(self, fn):
        self.todo.append(("call", fn))

    def source(self, key, src, lo, ld, k, fn):
        self.held[key] = (Slot(src, lo, None, None), ld)
        self.todo.append(["quarter", key, k, lambda s: s, False, fn, None])

    def quarter(self, key, k, view, last, fn):
        self.todo.append(["quarter", key, k, view, last, fn, None])

    def step(self):
        for t in self.todo:
            if self.ahead == self.NB:
                break
            if t[0] != "quarter" or t[6] is not None:
                continue
            if t[1] not in self.held:
                break
            s, ld = self.held[t[1]]
            t[6] = self.split_w(t[3](s.t), t[3](s.r), t[2], ld)
            self.ahead += 1
        t = self.todo.pop(0)
        if t[0] == "call":
            t[1]()
        elif t[0] == "plain":
            s, ld = self.held[t[1]]
            self.release(t[1], t[2](s.t, ld))
        else:
            self.ahead -= 1
            self.pe_read[t[6].b] = [t[5](t[6])]
            if t[4]:
                self.release(t[1], self.pe_read[t[6].b])

    def unit(self, key, c0, n, xs, tm, evac, last, view=None):
        st = {}

        def part(h):
            def f(q):
                if h == 0:
                    st["b"] = [self.bank() for _ in xs]
                t = None
                for j, (xp, bk) in enumerate(zip(xs, st["b"])):
                    first = h == 0
                    for g in range(2 if tm else n // 128):
                        gs = slice(128 * g, 128 * g + 128)
                        for k in range(4):
                            kk = 4 * h + k
                            for w, v, wt in ((q.hi, xp.hi, q.th), (q.hi, xp.lo, q.th), (q.lo, xp.hi, q.tl)):
                                l, r = (v[:, kk, gs], w[:, k, :]) if tm else (w[:, k, gs], v[:, kk, :])
                                t = self.mm(bk.t[:, 256 * g:256 * g + (n if tm else 256)], l, r, first,
                                            h == 1 and k == 3, wt, xp.tok[kk], bk.free if first else None)
                                first = False
                    if h == 1:
                        bk.free = list(flat([evac(xp, bk.t, c0, t)]))
                return t
            return f

        view = view or (lambda s: s[:, 0:4096].rearrange("p (k n) -> p k n", k=8))
        for h in range(2):
            self.quarter(key, 4, lambda s, h=h: view(s)[:, 4 * h:4 * h + 4, c0:c0 + n], last and h == 1, part(h))

    def unit_at(self, key, o, n, xs, evac, c0, last):
        self.unit(key, 0, n, xs, False, lambda xp, b, c, t: evac(xp, b, c0, t), last,
                  view=lambda s: s[:, o:o + 8 * n].rearrange("p (k n) -> p k n", k=8))

    def units(self, key, w, c0, xs, tm, evac):
        self.want(key, [self.block(w, c0)])
        for u in range(2):
            self.unit(key, 256 * u, 256, xs, tm, lambda xp, b, c, t: evac(xp, b, c0 + c, t), u == 1)

    def side_step(self):
        went = False
        for lane in self.lanes:
            while lane:
                if next(lane[0], "end") != "end":
                    went = True
                    break
                lane.pop(0)
        return went

    def run(self, ratio=1):
        while self.todo:
            self.step()
            for _ in range(ratio):
                self.side_step()

    @staticmethod
    def need(done, *keys):
        while any(k not in done for k in keys):
            yield

    @staticmethod
    def wait(n):
        for _ in range(n):
            yield

    def until(self, done, *keys):
        def f():
            for _ in range(999):
                if all(k in done for k in keys):
                    return
                self.side_step()
            assert False, keys
        self.call(f)

    def drain(self):
        while self.side_step():
            pass

    def finish(self, *last):
        self.sp.do(lambda e: e.nop(), *last)
        streams = dict(sync=self.sp, tensor=self.pe, scalar=self.act, vector=self.dve, gpsimd=self.pool)
        for s in streams.values():
            s.count()
        with self.nc.Block() as block:
            block.sync(lambda e: self.sp.emit(e))
            block.tensor(lambda e: self.pe.emit(e))
            block.scalar(lambda e: self.act.emit(e))
            block.vector(lambda e: self.dve.emit(e))
            block.gpsimd(lambda e: self.pool.emit(e))


def bc(a, n, axis):
    a = a.unsqueeze(axis)
    s = list(a.shape)
    s[axis] = n
    return a.to_broadcast(s)


def phase_a(P):
    A, Z = P.A, P.Z
    mm, tp, af, acp, tt, ts, stt, cp, rcp, fill = P.mm, P.tp, P.af, P.acp, P.tt, P.ts, P.stt, P.cp, P.rcp, P.fill
    col, sm, ONE, EYE, EPS, x = P.col, P.sm, P.ONE, P.EYE, P.EPS, P.x
    LE, GE = P.mask["le"], P.mask["ge"]
    B = P.banks

    off = [Z]

    def new(name, shape, dt=F32):
        n = int(np.prod(shape))
        off[0] += n
        assert off[0] <= 53200, name
        return P.at(name, off[0] - n, shape, dt), off[0] - n

    hx = Part(new("hx_hi", [KT, T], F32R)[0], new("hx_lo", [KT, T], F32R)[0])
    hc_hi, HC = new("hc_hi", [KT, T], F32R)
    hc = Part(hc_hi, new("hc_lo", [KT, T], F32R)[0])
    ctx, CX = new("ctx", [KT, T])
    kx, QK = new("kx", [4, T])
    qx = new("qx", [4, T])[0]
    vx = new("vx", [2, 1024])[0]
    kc, KC = new("kc", [4, T])
    vc, VC = new("vc", [2, 1024])
    la, LA = new("la", [2, 4, T])
    lc, LC = new("lc", [2, 4, T])
    zv, ZV = new("zv", [2, 1024])
    u, UU = new("u", [KT, T])
    wg2 = new("wg2", [512])[0]
    wlr, WLR = new("wlr", [KT, 128])
    wlr_lo = P.at("wlr_lo", WLR, [KT, 128], F32R)
    sguw = new("sguw", [8, 128])[0]
    sgub = new("sgub", [8, 128])[0]
    lr, _ = new("lr", [2, T])
    cs, _ = new("cs", [KT, 32])
    md0, MD = new("md0", [16, 32])
    md1, md2 = P.at("md1", MD, [16, 32]), None
    lnr = P.at("lnr", HC, [2, 1024])
    gt_tmp = HC + 2048
    gates = P.at("gates", HC, [16, T])
    bb = P.at("bb", CX, [2, 4, T])
    rr = P.at("rr", CX, [KT, T])
    sgu_hi = P.at("sgu_hi", ZV, [KT, T], F32R)
    sgu = Part(sgu_hi, P.at("sgu_lo", UU, [KT, T], F32R))
    o = P.at("o", VC, [4, 2, T])
    ob = Part(P.at("ob_hi", LA, [KT, T], F32R), P.at("ob_lo", VC, [KT, T], F32R))
    m = P.at("m", LC, [KT, T])
    mp = Part(P.at("m_hi", QK, [KT, T], F32R), P.at("m_lo", LC, [KT, T], F32R))
    mod = P.small[:, 0:64]
    sqx = P.at("sqx", UU, [KT, T])
    sqc = P.at("sqc", ZV, [KT, T])
    rsx = P.at("rsx", LC, [T])
    rsc = P.at("rsc", LC + T, [T])
    ht = P.at("ht", LA, [KT, T])

    l_pf = P.load(P.pf[:], A["cols"])
    l_cst = P.load(P.cst[:], A["cst"])
    l_x = P.load(x[:], A["xT"])
    for i in range(4):
        P.want(("mod", 0, i), [(lambda t: t[:, 0:4096].rearrange("p (k n) -> p k n", k=2),
                               A["w_mod"][256 * i:256 * i + 256, 0:2048].rearrange("(k p) n -> p k n", p=128))])
    for i in range(3):
        P.add_slot(i, P.R0 + P.SLOT * i)
    l_ctx = P.load(ctx[:], A["ctxT"])

    f_lr = fill(wlr[:], 0.0, on=P.pool)
    f_g2 = fill(wg2[0:64, :], 0.0, on=P.pool)
    f_cs = fill(cs[:], 0.0, on=P.pool)
    l_lr = [P.load(wlr[:, :, 32 * d:32 * d + 16], A["w_lr"][:, :, 16 * d:16 * d + 16], f_lr) for d in range(2)]
    l_g2 = [P.load(wg2[32 * d:32 * d + 16, :], A["w_gate2"][d], f_g2) for d in range(2)]

    c0 = af(cs[:, :, 0], col("c", 0, 8), AF.Silu, l_pf, f_cs)
    c1 = af(cs[:, :, 1], col("c_ctx", 0, 8), AF.Silu, l_pf, f_cs)
    bank_mod = B[3]

    def mod_part(g, i):
        def f(s, ld):
            t = None
            w = s[:, 0:4096].rearrange("p (k t j n) -> p k t j n", k=2, t=16, j=4)
            for k in range(2):
                for j in range(4):
                    t = mm(bank_mod.t[32 * j:32 * j + 32, :].rearrange("p (t n) -> p t n", t=16),
                           cs[:, 2 * i + k, :], w[:, k, :, j, :], i == 0 and k == 0, i == 3 and k == 1,
                           ld, c1, c0, bank_mod.free if i == 0 else None)
            mods[g] = t
            return t
        return f

    mods, modcol = {}, {}

    def mod_done(g, md, *w):
        t = P.dve.do(lambda e: e.transpose(md[:].rearrange("p t n -> p (t n)"), bank_mod.t[:, :]), mods[g], *w)
        bank_mod.free = [t]
        return t

    def rstd(src, sq, out, bank, ld):
        t = af(sq[:], src, AF.Square, ld)
        for k in range(KT):
            t2 = mm(bank.t[:, 0:T], ONE, sq[:, k, :], k == 0, k == KT - 1, t, l_cst)
        t = af(out[:], bank.t[:, 0:T], AF.Sqrt, t2, bias=EPS, scale=1.0 / 1024)
        bank.free = [t]
        return rcp(out[:], out[:], t)

    t_rx = rstd(x[:], sqx, rsx, B[4], l_x)
    t_rc = rstd(ctx[:], sqc, rsc, B[5], l_ctx)
    for i in range(4):
        P.plain(("mod", 0, i), mod_part(0, i))
    nx = P.at("nx", UU, [KT, T])
    ncx = P.at("ncx", ZV, [KT, T])
    t_nx = tt(nx[:], x[:], bc(rsx[:], KT, 1), OP.mult, t_rx)
    t_nc = tt(ncx[:], ctx[:], bc(rsc[:], KT, 1), OP.mult, t_rc)
    P.run(0)
    t = mod_done(0, md0)
    sc = mod.rearrange("p (a k r) -> p a k r", a=4, k=8)[:, 0:2]
    t1 = tt(sc[:, 1], md0[:, 0:8, 0:2], bc(col("b_mod", 0, 8), 2, 2), OP.add, t)
    t0 = tt(sc[:, 0], md0[:, 8:16, 0:2], bc(col("b_mod", 8, 8), 2, 2), OP.add, t)
    t0 = stt(sc[:, 0], sc[:, 0], 1.0, bc(col("g_norm1", 0, 8), 2, 2), OP.add, OP.mult, t0)
    for r, (src, part, tn) in enumerate(((nx, hx, t_nx), (ncx, hc, t_nc))):
        for k in range(KT):
            t = ts(src[:, k, :], src[:, k, :], sc[:, 0, k, r:r + 1], sc[:, 1, k, r:r + 1], OP.mult, OP.add, tn, t0, t1)
            P.split_x(part, k, src[:, k, :], t)

    w_in = A["w_in"]
    done = {}
    pa = lambda a: a.rearrange("p a t -> p (a t)")

    def ev_k(xp, b, c, t):
        j = (c - 2560) // 128
        done["k", xp is hx, j // 2] = r = acp(pa((kx if xp is hx else kc)[:, j:j + 2, :]), b[:], t)
        return r

    def ev_v(xp, b, c, t):
        c -= 3072
        done["v", xp is hx, c // 256] = r = cp((vx if xp is hx else vc)[:, :, c:c + 256],
                                              b[:].rearrange("p (a n) -> p a n", a=2), t)
        return r

    def ev_q(xp, b, c, t):
        j = (c - 2048) // 128
        done["q", j // 2] = r = af(pa(qx[:, j:j + 2, :]), b[:], AF.Copy, t, scale=128 ** -0.5)
        return r

    def ev_zv(xp, b, c, t):
        done["zv", (c - 1024) // 256] = r = af(zv[:, :, c - 1024:c - 768], b[:].rearrange("p (a n) -> p a n", a=2),
                                              AF.Gelu_apprx_tanh, t, done["decay"])
        return r

    def ev_u(xp, b, c, t):
        done["u", c // 256] = r = af(pa(u[:, c // 128:c // 128 + 2, :]), b[:], AF.Gelu_apprx_tanh, t, done["gla"])
        return r

    def ev_r(xp, b, c, t):
        j = (c - 4096) // 128
        done["r", j // 2] = r = af(pa(rr[:, j:j + 2, :]), b[:], AF.Silu, t, done["gla"])
        return r

    def ev_g(xp, b, c, t):
        j = (c - 5152) // 128
        for a in range(2):
            r = af(gates[:, j + a, :], b[:, 256 * a:256 * a + 256], AF.Sigmoid, t, done["ln"], done["gla"],
                   bias=col("b_branch", j + a))
        done["g", j // 2] = r
        return r

    def need(*keys):
        while any(k not in done for k in keys):
            yield

    def lr_part(q):
        t = None
        for r, (xp, bk) in enumerate(((hx, P.bank()), (hc, P.bank()))):
            for k in range(KT):
                for w, v, wt in ((q.hi, xp.hi, q.th), (q.hi, xp.lo, q.th), (q.lo, xp.hi, q.tl)):
                    t = mm(bk.t[:, 0:T], w[:, k, :], v[:, k, :], k == 0 and w is q.hi and v is xp.hi,
                           k == KT - 1 and w is q.lo, wt, xp.tok[k], bk.free)
            done["lr", r] = acp(lr[0:64, r, :], bk.t[0:64, 0:T], t)
            bk.free = [done["lr", r]]
        return t

    gtmp = P.at("gtmp", ZV, [2, 4, T])
    gl = P.at("gl", UU, [8, T])
    S16 = 1.0 / 16

    def decays(r, dst, w):
        for d in range(2):
            tmp = gtmp[:, d]
            ta, tn = [], []
            for g in range(2):
                bk = B[4 + 2 * d + g]
                for a in range(2):
                    h = 2 * g + a
                    t = mm(bk.t[:, 256 * a:256 * a + 256], wg2[32 * d:32 * d + 32, 128 * h:128 * h + 128],
                           lr[32 * d:32 * d + 32, r, :], a == 0, a == 1, done["lr", r], l_g2, bk.free if a == 0 else None)
                for a in range(2):
                    h = 2 * g + a
                    src = bk.t[:, 256 * a:256 * a + 256]
                    ta.append(af(tmp[:, h, :], src, AF.Abs, t, w, bias=col("b_gate2", 4 * d + h)))
                for a in range(2):
                    h = 2 * g + a
                    src = bk.t[:, 256 * a:256 * a + 256]
                    tn.append(ts(dst[:, d, h, :], src, col("b_gate2", 4 * d + h), 0.0, OP.add, OP.min, ta[-1], w))
                bk.free = [tn[-1]]
            t = af(tmp, tmp, AF.Exp, ta, scale=-1.0)
            t = af(tmp, tmp, AF.Ln, t, bias=ONE[:, 0:1])
            done["la", r, d] = tt(dst[:, d], dst[:, d], tmp, OP.subtract, t, tn)
            yield
            w = [w, done["la", r, d]]

    def ctx_state(d, h, i):
        e, kt = gl[:, 2 * i, :], gl[:, 2 * i + 1, :].rearrange("p (a n) -> p a n", a=2)
        L = lc[:, d, h, :]
        w = done["la", 1, d]
        t = P.dve.do(lambda s: s.tensor_tensor_scan(e, L, L, 0.0, OP.add, OP.bypass), w, gfree[i])
        if d == 0:
            t = ts(P.small[:, 64 + i:65 + i], e[:, T - 1:T], S16, None, OP.mult, None, t, gfree[i])
            t = af(e, e, AF.Exp, t, bias=P.small[:, 64 + i:65 + i], scale=-S16)
        else:
            t = tt(e, e, L, OP.subtract, t)
            t = af(e, e, AF.Exp, t, scale=S16)
        t = tt(e, e, kc[:, h, :], OP.mult, t, done["k", False, h // 2])
        bk = B[4 + i % 4]
        for a in range(2):
            t2 = tp(bk.t[:, 128 * a:128 * a + 128], e[:, 128 * a:128 * a + 128], t, bk.free, l_cst)
        yield
        t = acp(kt, bk.t[:, 0:256].rearrange("p (a n) -> p a n", a=2), t2, gfree[i])
        for a in range(2):
            t2 = mm(bk.t[:, 256:512], kt[:, a, :], vc[:, a, 256 * h:256 * h + 256], a == 0, a == 1, t, bk.free,
                    done["v", False, h])
        yield
        done["s", d, h] = cp(L, bk.t[:, 256:512], t2)
        bk.free = [done["s", d, h]]
        gfree[i] = [done["s", d, h]]

    gfree = [[t_h for t_h in hx.tok[KT - 1]] for _ in range(4)]
    tm_ = {}

    def x_head(h):
        q, k = qx[:, h, :], kx[:, h, :]
        c2 = lambda a: a.rearrange("p (c n) -> p c n", c=2)
        fr = gfree[0]
        qm, km, qi = ([gl[:, 3 * d + i, :] for d in range(2)] for i in range(3))
        kst = [gl[:, 6, 128 * d:128 * d + 128] for d in range(2)]
        att = gl[:, 7, :]
        tq, tk, ti, tst = [], [], [], []
        for d in range(2):
            for c in range(2):
                b = bb[:, d, h, 128 * c:128 * c + 128]
                cc = slice(128 * c, 128 * c + 128)
                nm, pm = (sc_mid[i][:, d, h, c:c + 1] for i in range(2))
                tq.append(af(qm[d][:, cc], b, AF.Exp, done["bb"], fr, bias=nm, scale=S16))
                tk.append(af(km[d][:, cc], b, AF.Exp, done["bb"], fr, bias=pm, scale=-S16))
            ti.append(af(qi[d], bb[:, d, h, :], AF.Exp, done["bb"], fr, scale=S16))
            tst.append(af(kst[d], bb[:, d, h, 128 * d:128 * d + 128], AF.Exp, done["bb"], fr,
                          bias=sc_tot[:, d, h, d:d + 1], scale=-S16))
        yield
        wk, wq = done["k", True, h // 2], done["q", h // 2]
        mq, mk, mi, ms = [], [], [], []
        for d in range(2):
            mq.append(tt(qm[d], qm[d], q, OP.mult, tq, wq))
            mk.append(tt(km[d], km[d], k, OP.mult, tk, wk))
            ms.append(tt(kst[d], kst[d], k[:, 128 * d:128 * d + 128], OP.mult, tst, wk))
            mi.append(tt(qi[d], qi[d], q, OP.mult, ti, wq))
        b4, b5, b6, b7 = B[4], B[5], B[6], B[7]
        for d in range(2):
            for c in range(2):
                cc = slice(128 * c, 128 * c + 128)
                t = mm(b4.t[:, 256 * d + 128 * c:256 * d + 128 * c + 128], km[d][:, cc], qm[d][:, cc], d == 0 and c == 0,
                       d == 1 and c == 1, mq[d], mk[d], b4.free)
        for d in range(2):
            t2 = tp(b5.t[:, 128 * d:128 * d + 128], kst[d], ms[d], b5.free)
        yield
        t_kt = acp(gl[:, 6, :], b5.t[:, 0:256], t2)
        t1 = tt(c2(att), b4.t[:, 0:256].rearrange("p (c n) -> p c n", c=2), bc(LE, 2, 1), OP.mult, t, fr)
        t3 = tt(c2(km[0]), b4.t[:, 256:512].rearrange("p (c n) -> p c n", c=2), bc(GE, 2, 1), OP.mult, t)
        t_att = tt(att, att, km[0], OP.add, t1, t3)
        b4.free = [t1, t3]
        for d in range(2):
            t = mm(b5.t[:, 256:512] if d == 0 else b6.t[:, 0:256], kst[d], vx[:, d, 256 * h:256 * h + 256], True, True,
                   t_kt, b6.free, done["v", True, h])
            S1 = km[1] if d == 0 else qm[1]
            t = stt(S1, lc[:, d, h, :], sc_dec[:, d, h, d:d + 1], b5.t[:, 256:512] if d == 0 else b6.t[:, 0:256],
                    OP.mult, OP.add, t, done["s", d, h], t1, t3)
            (b5 if d == 0 else b6).free = [t, t_kt]
            tm_[d] = t
        first = True
        for j in range(2):
            js = slice(128 * j, 128 * j + 128)
            for c in range(2):
                cc = slice(128 * c, 128 * c + 128)
                out = b7.t[:, 256 * j + 128 * c:256 * j + 128 * c + 128]
                mm(out, vx[:, c, 256 * h + 128 * j:256 * h + 128 * j + 128], att[:, cc], first, False, t_att, b7.free)
                first = False
                mm(out, lc[:, c, h, js], qi[c][:, cc], False, False, mi[c], done["s", c, h])
        yield
        for j in range(2):
            js = slice(128 * j, 128 * j + 128)
            for c in range(2):
                cc = slice(128 * c, 128 * c + 128)
                S1 = km[1] if c == 1 else qm[1]
                t = mm(b7.t[:, 256 * j + 128 * c:256 * j + 128 * c + 128], S1[:, js], qi[1 - c][:, cc], False,
                       j == 1 and c == 1, tm_[0], tm_[1])
        yield
        t_o = acp(pa(o[:, h]), b7.t[:], t, done["ctx"])
        sq = [km[0], qm[0]]
        for j in range(2):
            t_s = af(sq[j], b7.t[:, 256 * j:256 * j + 256], AF.Square, t)
        b7.free = [t_s]
        for j in range(2):
            t = mm(b4.t[:, 0:T], ONE, sq[j], j == 0, j == 1, t_s, b4.free)
        yield
        rs = qi[0]
        t = af(rs, b4.t[:, 0:T], AF.Sqrt, t, bias=EPS, scale=1.0 / 256)
        b4.free = [t]
        t = rcp(rs, rs, t)
        for j in range(2):
            t = stt(o[:, h, j, :], o[:, h, j, :], col("gla_norm_g", 2 * h + j), rs, OP.mult, OP.mult, t, t_o)
        done["o", h] = t
        gfree[0] = [t]

    sc_mid = [P.small[:, 128 + 16 * i:144 + 16 * i].rearrange("p (d h c) -> p d h c", d=2, h=4) for i in range(2)]
    sc_tot = P.small[:, 160:176].rearrange("p (d h c) -> p d h c", d=2, h=4)
    sc_dec = P.small[:, 176:192].rearrange("p (d h c) -> p d h c", d=2, h=4)

    def gla():
        yield from need(("lr", 1), ("lr", 0))
        yield from decays(1, lc, [t_rc, t_nc, hc.tok[KT - 1]])
        yield from decays(0, la, [hx.tok[KT - 1], t_nx, t_nc])
        done["decay"] = [done["la", r, d] for r in range(2) for d in range(2)]
        t = None
        tb = []
        for d in range(2):
            for h in range(4):
                for c in range(2):
                    cc = slice(128 * c, 128 * c + 128)
                    L = la[:, d, h, cc]
                    t = P.dve.do(lambda s, a=bb[:, d, h, cc], L=L: s.tensor_tensor_scan(a, L, L, 0.0, OP.add, OP.bypass),
                                 done["la", 0, d], t_nc)
                    if d == 1:
                        t = ts(P.small[:, 192 + 2 * h + c:193 + 2 * h + c], bb[:, d, h, 128 * c + 127:128 * c + 128], 1.0,
                               None, OP.mult, None, t)
                        t = stt(bb[:, d, h, cc], bb[:, d, h, cc], P.small[:, 192 + 2 * h + c:193 + 2 * h + c], L,
                                OP.subtract, OP.subtract, t, rev1=True)
                    tb.append(t)
        yield
        b5 = bb[:].rearrange("p d h (c n) -> p d h c n", c=2)
        for d in range(2):
            mid, end = (63, 127) if d == 0 else (64, 0)
            ts(sc_mid[0][:, d], b5[:, d, :, :, mid], -S16, None, OP.mult, None, tb)
            ts(sc_mid[1][:, d], b5[:, d, :, :, mid], S16, None, OP.mult, None, tb)
            t = ts(sc_tot[:, d], b5[:, d, :, :, end], S16, None, OP.mult, None, tb)
        done["bb"] = af(sc_dec[:], sc_tot[:], AF.Exp, t)
        yield
        for h in range(4):
            yield from need(("k", False, h // 2), ("v", False, h))
            gs = [ctx_state(d, h, 2 * (h % 2) + d) for d in range(2)]
            while gs:
                for g in list(gs):
                    try:
                        next(g)
                    except StopIteration:
                        gs.remove(g)
                yield
        done["ctx"] = [done["s", d, h] for d in range(2) for h in range(4)]
        gfree[0] = list(flat(gfree))
        for h in range(4):
            yield from need(("k", True, h // 2), ("q", h // 2), ("v", True, h))
            yield from x_head(h)
            yield
        done["gla"] = [done["o", h] for h in range(4)]
        for h in range(4):
            yield from need(("r", h))
            t = tt(pa(o[:, h]), pa(o[:, h]), pa(rr[:, 2 * h:2 * h + 2, :]), OP.mult, done["r", h], done["o", h])
            for j in range(2):
                P.split_x(ob, 2 * h + j, o[:, h, j, :], t, done["gla"])
            yield

    def sgu_side():
        yield from need(*[("zv", i) for i in range(4)])
        st = P.small[:, 208:232].rearrange("p (a b s) -> p a b s", a=2, b=2)
        mv = P.small[:, 232:236].rearrange("p (a s) -> p a s", a=2)
        wz = [done["zv", i] for i in range(4)]
        t1 = []
        for a in range(2):
            t = [P.dve.do(lambda e, a=a, b=b: e.bn_stats(st[:, a, b, :], zv[:, a, 512 * b:512 * b + 512]), wz)
                 for b in range(2)]
            t = P.dve.do(lambda e, a=a: e.bn_aggr(mv[:, a, :], st[:, a].rearrange("p b s -> p (b s)")), t)
            t1.append(t)
        t = af(mv[:, :, 1], mv[:, :, 1], AF.Sqrt, t1, bias=EPS)
        t = rcp(mv[:, :, 1], mv[:, :, 1], t)
        tz = []
        for a in range(2):
            t2 = ts(zv[:, a, :], zv[:, a, :], mv[:, a, 0:1], mv[:, a, 1:2], OP.subtract, OP.mult, t)
            t2 = tt(zv[:, a, :], zv[:, a, :], lnr[:, 0, :], OP.mult, t2, l_lnr)
            tz.append(tt(zv[:, a, :], zv[:, a, :], lnr[:, 1, :], OP.add, t2, l_lnr))
        done["ln"] = tz
        yield
        yield from need(*[("u", i) for i in range(4)])
        tb = []
        for i in range(4):
            bk = B[4 + i]
            for g in range(2):
                for n in range(2):
                    gg = 2 * i + g
                    t = mm(bk.t[:, 256 * g + 128 * n:256 * g + 128 * n + 128], zv[:, n, 128 * gg:128 * gg + 128],
                           sguw[:, gg, :], g == 0 and n == 0, g == 1 and n == 1, tz, l_sgu, bk.free)
            tb.append(t)
        yield
        for i in range(4):
            bk = B[4 + i]
            d4 = mix[:, i].rearrange("p (g n t) -> p g n t", g=2, n=2)
            t = tt(d4, bk.t[:].rearrange("p (g n t) -> p g n t", g=2, n=2), bc(sgub[:, 2 * i:2 * i + 2, :], 2, 2),
                   OP.add, tb[i], l_sgu, done["gla"])
            bk.free = [t]
            t = tt(pa(u[:, 2 * i:2 * i + 2, :]), pa(u[:, 2 * i:2 * i + 2, :]), mix[:, i], OP.mult, t, done["u", i])
            for g in range(2):
                P.split_x(sgu, 2 * i + g, u[:, 2 * i + g, :], t, tb)
            yield

    mix = P.at("mix", LC, [4, 512])

    P.lanes = [[gla(), sgu_side()]]
    P.source("lr", wlr[:], wlr_lo[:], l_lr, 8, lr_part)
    P.units("k", w_in, 2560, [hx, hc], False, ev_k)
    P.units("q", w_in, 2048, [hx], False, ev_q)
    for i in range(2):
        P.units(f"v{i}", w_in, 3072 + 512 * i, [hx, hc], True, ev_v)

    l_lnr = []

    def late_loads():
        hcr = done["v", False, 3]
        w = [hcr]
        for i, n in enumerate(("sgu_ln_g", "sgu_ln_b")):
            l_lnr.append(P.load(lnr[:, i, :], A[n].partition_broadcast(128), w))
    P.call(late_loads)
    l_sgu = [P.load(sguw[:], A["sgu_wT"]), P.load(sgub[:], A["sgu_b"].partition_broadcast(128))]

    def mod_load(g, i):
        P.want(("mod", g, i), [(lambda t: t[:, 0:4096].rearrange("p (k n) -> p k n", k=2),
                               A["w_mod"][256 * i:256 * i + 256, 2048 * g:2048 * g + 2048].rearrange(
                                   "(k p) n -> p k n", p=128))])
        P.plain(("mod", g, i), mod_part(g, i))

    P.modcol = modcol
    gt1 = P.small[:, 32:40]
    gt2 = P.small[:, 56:64]
    sc2 = P.small[:, 40:56].rearrange("p (a k) -> p a k", a=2)

    def mod1():
        t = mod_done(1, md0, t0, t1)
        modcol["gt1"] = tt(gt1, md0[:, 0:8, 0], col("b_mod", 16, 8), OP.add, t)
        modcol["sh2"] = tt(sc2[:, 1], md0[:, 8:16, 0], col("b_mod", 24, 8), OP.add, t)

    def mod2():
        t = mod_done(2, md0, modcol["gt1"], modcol["sh2"])
        t2 = tt(sc2[:, 0], md0[:, 0:8, 0], col("b_mod", 32, 8), OP.add, t)
        modcol["sc2"] = stt(sc2[:, 0], sc2[:, 0], 1.0, col("g_norm2", 0, 8), OP.add, OP.mult, t2)
        modcol["gt2"] = tt(gt2, md0[:, 8:16, 0], col("b_mod", 40, 8), OP.add, t)

    P.until(done, "decay")
    for i in range(2):
        P.units(f"zv{i}", w_in, 1024 + 512 * i, [hx], True, ev_zv)
        mod_load(1, i)
    P.until(done, "gla")
    for i in range(2):
        P.units(f"u{i}", w_in, 512 * i, [hx], False, ev_u)
        mod_load(1, 2 + i)
    P.call(mod1)
    for i in range(2):
        P.units(f"r{i}", w_in, 4096 + 512 * i, [hx], False, ev_r)
        mod_load(2, i)
    P.until(done, "ln")
    for i in range(4):
        P.units(f"g{i}", w_in, 5152 + 512 * i, [hx], False, ev_g)
        if i < 2:
            mod_load(2, 2 + i)
    P.call(mod2)

    def ev_a(xp, b, c, t):
        j = c // 128
        done["m", j] = r = tt(pa(m[:, j:j + 2, :]), b[:], pa(gates[:, j:j + 2, :]), OP.mult, t, done["g", j // 2], lc_free())
        return r

    def lc_free():
        return [done["gla"]] + [sgu.tok[k] for k in range(KT)]

    def ev_b(xp, b, c, t):
        j = c // 128
        gb = pa(gates[:, 8 + j:10 + j, :])
        r = tt(gb, b[:], gb, OP.mult, t, done["g", 4 + j // 2])
        t = tt(pa(m[:, j:j + 2, :]), pa(m[:, j:j + 2, :]), gb, OP.add, r, done["m", j])
        for a in range(2):
            P.split_x(mp, j + a, m[:, j + a, :], t, done["gla"])
        return r

    def ev_o(xp, b, c, t):
        j = c // 128
        for a in range(2):
            r = stt(x[:, j + a, :], b[:, 256 * a:256 * a + 256], gt1[:, j + a:j + a + 1], x[:, j + a, :], OP.mult, OP.add, t,
                    modcol["gt1"], t_nx)
            P.x_tok[j + a] = r
        return r

    P.x_tok = {}
    P.call(P.drain)
    for i in range(2):
        P.units(f"wa{i}", A["w_a"], 512 * i, [sgu], False, ev_a)
    for i in range(2):
        P.units(f"wb{i}", A["w_b"], 512 * i, [ob], False, ev_b)
    for i in range(2):
        P.units(f"wo{i}", A["w_o"], 512 * i, [mp], False, ev_o)

    P.gt2, P.sc2, P.modcol, P.doneA, P.doneB = gt2, sc2, modcol, done, {}
    P.m_free = None


def phase_b(P):
    A, Z = P.A, P.Z
    mm, tp, af, acp, tt, ts, stt, cp, rcp, red = P.mm, P.tp, P.af, P.acp, P.tt, P.ts, P.stt, P.cp, P.rcp, P.red
    col, sm, ONE, EPS, x, B = P.col, P.sm, P.ONE, P.EPS, P.x, P.banks
    LT = P.mask["lt"]
    pa = lambda a: a.rearrange("p a t -> p (a t)")

    P.m_free = [P.x_tok[k] for k in range(KT)]
    P.modcol = list(P.modcol.values())
    h2 = P.at("h2", Z + 8192, [KT, T])
    h2t = P.at("h2t", Z + 10240, [2, 1024])
    mem = P.at("mem", Z + 12288, [KT, T])
    yacc = P.at("yacc", Z + 14336, [KT, T])
    xe = P.at("xe", Z + 16384, [KT, T])
    hid = [P.at(f"hid{i}", Z + 18432 + 768 * i, [768]) for i in range(2)]
    hidT = [P.at(f"hidT{i}", Z + 19968 + 768 * i, [6, 2, 64]) for i in range(2)]
    y = [P.at(f"y{i}", Z + 21504 + 512 * i, [512]) for i in range(2)]
    sel = P.at("sel", Z + 22528, [2, 4, 64])
    selw = P.at("selw", Z + 23040, [2, 2, 64])
    selT = [P.at(f"selT{i}", Z + 23296 + 256 * i, [T]) for i in range(2)]
    stage = [P.at(f"stage{i}", Z + 24064 + 512 * i, [512]) for i in range(2)]
    rs = P.at("rs", Z + 25088, [T])
    rsm = P.at("rsm", Z + 25344, [T])
    wr = P.at("wr", Z + 25600, [KT, 16])
    lg = P.at("lg", Z + 25728, [T])
    rt = P.at("rt", Z + 25984, [512])
    P.mk = P.at("mk", Z + Layout2.MK, [KT, T])
    P.mv = P.at("mv", Z + Layout2.MV, [2, 1024])
    sq = P.at("sq", Z + 16384, [KT, T])
    mems = P.at("mems", Z + 10240, [KT, T])
    br = P.small[:, 236:237]

    P.add_slot(3, Z, P.doneA["g", 7])
    P.add_slot(4, 4096, P.pe_read)
    P.add_slot(5, Z + 4096, P.m_free)

    done = P.doneB
    l_mem = P.load(mem[:], A["memT"], P.doneA["gla"])

    def mem_norm():
        t = af(mems[:], mem[:], AF.Square, l_mem, P.m_free)
        for k in range(KT):
            t2 = mm(B[3].t[:, 0:T], ONE, mems[:, k, :], k == 0, k == KT - 1, t, B[3].free)
        t = af(rsm[:], B[3].t[:, 0:T], AF.Sqrt, t2, P.m_free, bias=EPS, scale=1.0 / 1024)
        B[3].free = [t]
        done["rsm"] = rcp(rsm[:], rsm[:], t)

    def mem_scale(l, *w):
        for k in range(KT):
            done["mem", l, k] = stt(mem[:, k, :], mem[:, k, :], col("norm_mem_2", 8 * l + k), rsm[:], OP.mult, OP.mult,
                                    done["rsm"], l_mem, *w)

    nst = [0]

    def mem_kv(l, i):
        def f(s, ld):
            w = s[:, 0:4096].rearrange("p (k n) -> p k n", k=8)
            for v in range(2):
                bk = B[6 + v]
                if i < 2:
                    for g in range(2):
                        for k in range(KT):
                            c = 256 * v + 128 * g
                            t = mm(bk.t[:, 256 * g:256 * g + 256], w[:, k, c:c + 128], mem[:, k, :], g == 0 and k == 0,
                                   k == KT - 1, ld, done["mem", l, k], bk.free)
                    dst = P.mk[:, 4 * i + 2 * v:4 * i + 2 * v + 2, :]
                else:
                    for k in range(KT):
                        t = mm(bk.t[:], mem[:, k, 128 * v:128 * v + 128], w[:, k, :], k == 0, k == KT - 1, ld,
                               done["mem", l, k], bk.free)
                    dst = P.mv[:, v, 512 * (i - 2):512 * (i - 2) + 512]
                if l == 0:
                    r = acp(dst if i >= 2 else pa(dst), bk.t[:], t, P.m_free)
                    P.kv_tok.append(r)
                else:
                    n = nst[0]
                    nst[0] += 1
                    r = acp(stage[n % 2][:], bk.t[:], t, P.stage_free[n % 2])
                    P.stage_free[n % 2] = [P.load(A["kv1"][:, 512 * n:512 * n + 512], stage[n % 2][:], r)]
                    P.kv1_tok[n] = P.stage_free[n % 2]
                    P.kv1_at[n] = (i, v)
                bk.free = [r]
            done["memmm", l, i] = t
            return t
        return f

    def want_mem(l, i):
        P.want(("mem", l, i), [P.block(A["w_mem_kv"][l], 512 * i)], 6)
        P.plain(("mem", l, i), mem_kv(l, i))

    P.kv_tok, P.stage_free, P.kv1_tok, P.kv1_at = [], [[], []], {}, {}
    l_wr = [P.load(wr[:], A["w_router"], P.doneA["decay"]), P.load(br[0:16, :], A["b_router"])]

    def expert_loads(e):
        k1 = lambda w, c: P.block(A[w][e], c)
        for n, w, c in (("g0", "w_eg", 0), ("g1", "w_eg", 512), ("u0", "w_eu", 0), ("u1", "w_eu", 512),
                        ("g2", "w_eg", 1024), ("u2", "w_eu", 1024)):
            P.want((n, e), [k1(w, c)], 6)
        for j in range(3):
            P.want((f"d{j}", e), [P.block(A["w_ed"][e], 0, n=1024, k0=4 * j, kt=4)], 6)

    P.call(mem_norm)
    P.call(lambda: mem_scale(0))
    want_mem(0, 0)
    want_mem(0, 1)

    r_ = lambda o, *s: rt[:, o:o + int(np.prod(s))].rearrange(
        "p (a b) -> p a b", a=s[0]) if len(s) == 2 else rt[:, o:o + s[0]]
    prob, am, wt, posm = (r_(32 * i, 2, 16) for i in range(4))
    v_, e_ = r_(128, 2, 16), r_(160, 2, 16)
    oh = [r_(192, 2, 16), r_(224, 2, 16)]
    hi_, lo_ = r_(256, 8, 2), r_(272, 8, 2)
    t1_, t2_, gs_, gsel, gw = (r_(288 + 8 * i, 2, 4) for i in range(5))
    m_ = [r_(328 + 2 * i, 2) for i in range(8)]
    cnt, cnt1 = r_(352, 16), r_(368, 1)
    counts = P.nc.alloc_sbuf_tensor_at("counts", [128, 32], I32, offset=BASE + 4 * (Z + 26496))
    most = {}
    streams = {"act": P.act, "pe": P.pe, "dve": P.dve}
    b16, b4 = lambda a: bc(a, 16, 2), lambda a: bc(a, 4, 2)

    def route():
        xt = [P.x_tok[k] for k in range(KT)]
        t = af(sq[:], x[:], AF.Square, xt)
        for k in range(KT):
            t2 = mm(B[4].t[:, 0:T], ONE, sq[:, k, :], k == 0, k == KT - 1, t, B[4].free)
        t = af(rs[:], B[4].t[:, 0:T], AF.Sqrt, t2, bias=EPS, scale=1.0 / 1024)
        B[4].free = [t]
        t = rcp(rs[:], rs[:], t)
        t = tt(h2[:], x[:], bc(rs[:], KT, 1), OP.mult, t)
        th = [ts(h2[:, k, :], h2[:, k, :], P.sc2[:, 0, k:k + 1], P.sc2[:, 1, k:k + 1], OP.mult, OP.add, t, P.modcol)
              for k in range(KT)]
        for k in range(KT):
            t = mm(B[4].t[0:16, 0:T], wr[:, k, :], h2[:, k, :], k == 0, k == KT - 1, th[k], l_wr, B[4].free)
        t = af(lg[0:16, :], B[4].t[0:16, 0:T], AF.Identity, t, xt, l_wr, bias=br[0:16, :])
        for a in range(2):
            t2 = tp(B[5].t[:, 16 * a:16 * a + 16], lg[0:16, 128 * a:128 * a + 128], t, B[5].free)
        for a in range(2):
            for g in range(2):
                bk = B[(3, 4, 0, 1)[2 * a + g]]
                for j in range(4):
                    k = 4 * g + j
                    t3 = tp(bk.t[:, 128 * j:128 * j + 128], h2[:, k, 128 * a:128 * a + 128], th[k], t, bk.free)
                done["h2t", a, g] = acp(h2t[:, a, 512 * g:512 * g + 512], bk.t[:], t3, done["rsm"])
                bk.free = [done["h2t", a, g]]
        L = B[5].t[:, 0:32].rearrange("p (a b) -> p a b", a=2)
        t = red(m_[0], L, OP.max, t2)
        t = tt(prob, L, b16(m_[0]), OP.subtract, t)
        B[5].free = [t]
        t = af(prob, prob, AF.Exp, t)
        t = red(m_[1], prob, OP.add, t)
        t = rcp(m_[1], m_[1], t)
        t = tt(prob, prob, b16(m_[1]), OP.mult, t)
        p2 = prob.rearrange("p a (g j i) -> p (a g) j i", g=4, j=2)
        ta = tt(hi_, p2[:, :, :, 0], p2[:, :, :, 1], OP.max, t)
        tb = tt(lo_, p2[:, :, :, 0], p2[:, :, :, 1], OP.min, t)
        f8 = lambda a: a.rearrange("p a b -> p (a b)")
        tc = tt(f8(t1_), hi_[:, :, 0], hi_[:, :, 1], OP.max, ta)
        td = tt(f8(t2_), hi_[:, :, 0], hi_[:, :, 1], OP.min, ta)
        te = tt(f8(gs_), lo_[:, :, 0], lo_[:, :, 1], OP.max, tb)
        t = tt(t2_, t2_, gs_, OP.max, td, te)
        t = tt(gs_, t1_, t2_, OP.add, t, tc)
        t = red(m_[2], gs_, OP.max, t)
        t = tt(gw, gs_, b4(m_[2]), OP.is_equal, t)
        t = tt(gw, gw, bc(sm[:, 32:36], 2, 1), OP.mult, t)
        t = red(m_[3], gw, OP.max, t)
        t = tt(gsel, gw, b4(m_[3]), OP.is_equal, t)
        ta = ts(gw, gsel, -1.0, None, OP.add, None, t)
        p3 = lambda a: a.rearrange("p a (g i) -> p (a g) i", g=4)
        g8 = lambda a: bc(f8(a), 4, 2)
        t = tt(p3(v_), p3(prob), g8(gsel), OP.mult, t)
        t = tt(p3(v_), p3(v_), g8(gw), OP.add, t, ta)
        for i in range(2):
            t = red(m_[4 + i], v_, OP.max, t)
            t = tt(e_, v_, b16(m_[4 + i]), OP.is_equal, t)
            t = tt(e_, e_, bc(sm[:, 16:32], 2, 1), OP.mult, t)
            t = red(m_[6], e_, OP.max, t)
            t = tt(oh[i], e_, b16(m_[6]), OP.is_equal, t)
            if i == 0:
                t = stt(v_, oh[0], -4.0, v_, OP.mult, OP.add, t)
        ta = tt(am, oh[0], oh[1], OP.add, t)
        t = tt(m_[6], m_[4], m_[5], OP.add, t)
        t = rcp(m_[7], m_[6], t)
        t4 = tt(m_[4], m_[4], m_[7], OP.mult, t)
        t5 = tt(m_[5], m_[5], m_[7], OP.mult, t)
        t4 = tt(wt, oh[0], b16(m_[4]), OP.mult, t4)
        t5 = tt(e_, oh[1], b16(m_[5]), OP.mult, t5)
        done["wt"] = tt(wt, wt, e_, OP.add, t4, t5)
        pb = B[5].t
        mm(pb[:, 0:16], LT, am[:, 0, :], True, True, ta, B[5].free)
        mm(pb[:, 16:32], LT, am[:, 1, :], False, False)
        mm(pb[:, 16:32], ONE, am[:, 0, :], False, True)
        mm(pb[:, 32:48], ONE, am[:, 0, :], False, False)
        t = mm(pb[:, 32:48], ONE, am[:, 1, :], False, True)
        t2 = stt(posm, pb[:, 0:32].rearrange("p (a b) -> p a b", a=2), 1.0, am, OP.add, OP.mult, t)
        t = cp(cnt, pb[:, 32:48], t)
        B[5].free = [t]
        tm = red(cnt1, cnt, OP.max, t)
        done["cnt"] = cp(counts[:, 0:17], rt[:, 352:369], t, tm)
        for n in ("act", "pe", "dve"):
            P.raw(streams[n], lambda e, n=n: most.__setitem__(n, e.value_load(counts[0:1, 16:17])), done["cnt"])
        done["pos"] = ts(posm, posm, -1.0, None, OP.add, None, t2)

    IOTA = sm[:, 64:128]
    xe_read = []

    def gather(q):
        ps = [posm[:, a, 4 * q:4 * q + 4] for a in range(2)]
        t = [tt(sel[:, a], bc(IOTA, 4, 1), bc(ps[a], 64, 2), OP.is_equal, done["pos"], done.get("gather")) for a in range(2)]
        for g in range(4):
            bk = B[3 + g % 2]
            for j in range(2):
                k = 2 * g + j
                for a in range(2):
                    r = mm(bk.t[:, 256 * j:256 * j + 256], h2t[:, a, 128 * k:128 * k + 128],
                           sel[:, a].rearrange("p e s -> p (e s)"), j == 0 and a == 0, a == 1, t,
                           done["h2t", a, k // 4], bk.free)
            done["xe", q, g] = acp(pa(xe[:, 2 * g:2 * g + 2, :]), bk.t[:], r, xe_read)
            bk.free = [done["xe", q, g]]
        done["gather"] = r

    def xs(e, k):
        return xe[:, k, 64 * (e % 4):64 * (e % 4) + 64]

    def up(e, dst, j, first, last):
        def f(s, ld):
            w = s[:, 0:4096].rearrange("p (k n) -> p k n", k=8)
            bk = dst
            for k in range(KT):
                for h in range(2):
                    t = mm(bk.t[64 * h:64 * h + 64, 256 * j:256 * j + 256], xs(e, k), w[:, k, 256 * h:256 * h + 256],
                           first and k == 0, last and k == KT - 1, ld, done["xe", e // 4, k // 2], bk.free if first else None)
            done["up"] = t
            return t
        return f

    act_read = [[], []]

    def hidden(e, part):
        i = e % 2
        n = 512 if part == 0 else 256
        g_, u_ = (B[0].t[:], B[1].t[:]) if part == 0 else (B[2].t[:, 0:256], B[2].t[:, 256:512])
        h = hid[i][:, 512 * part:512 * part + n]
        t = af(h, g_, AF.Silu, done["up"], done.get(("hT", e - 2, part)))
        t = tt(h, h, u_, OP.mult, t)
        if part == 0:
            B[0].free = [t]
            B[1].free = [t]
        else:
            B[2].free = [t]
        bk = B[3 + part]
        for j in range(n // 128):
            t2 = tp(bk.t[:, 128 * j:128 * j + 128], h[:, 128 * j:128 * j + 128], t, bk.free)
        r = acp(hidT[i][:, 4 * part:4 * part + n // 128].rearrange("p a b c -> p (a b c)"), bk.t[:, 0:n], t2,
                done.get(("down", e - 2)))
        bk.free = [r]
        done["hT", e, part] = r

    def down(e, j):
        def f(s, ld):
            w = s[:, 0:4096].rearrange("p (k n) -> p k n", k=4)
            bk = B[5]
            for h in range(2):
                for u in range(2):
                    for c in range(2):
                        t = mm(bk.t[64 * c:64 * c + 64, :], hidT[e % 2][:, 2 * j + u, h, :], w[:, 2 * h + u, 512 * c:512 * c + 512],
                               j == 0 and h == 0 and u == 0, j == 2 and h == 1 and u == 1, ld, done["hT", e, j // 2],
                               bk.free if j == 0 else None)
            done["down", e] = t
            return t
        return f

    def weigh(e):
        i = e % 2
        t = [ts(selw[:, a], bc(IOTA, 2, 1), posm[:, a, e:e + 1], wt[:, a, e:e + 1], OP.is_equal, OP.mult,
                done["pos"], done["wt"], done.get("weigh")) for a in range(2)]
        bk = B[6]
        for a in range(2):
            t2 = tp(bk.t[:, 128 * a:128 * a + 128], selw[:, a].rearrange("p a b -> p (a b)"), t, bk.free)
        done["weigh"] = t2
        done["selT", e] = acp(selT[i][:], bk.t[:, 0:256], t2, done.get(("comb", e - 2)))
        bk.free = [done["selT", e]]

    def combine(e):
        i = e % 2
        t = acp(y[i][:], B[5].t[:], done["down", e], done.get(("comb", e - 2)))
        B[5].free = [t]
        for g in range(4):
            bk = B[6 + g % 2]
            c = g // 2
            for j in range(2):
                f = 2 * (g % 2) + j
                r = mm(bk.t[:, 256 * j:256 * j + 256], y[i][64 * c:64 * c + 64, 128 * f:128 * f + 128],
                       selT[i][64 * c:64 * c + 64, :], j == 0, j == 1, t, done["selT", e], bk.free)
            dst = pa(yacc[:, 4 * c + 2 * (g % 2):4 * c + 2 * (g % 2) + 2, :])
            if e == 0:
                bk.free = [cp(dst, bk.t[:], r, P.m_free)]
            else:
                bk.free = [tt(dst, dst, bk.t[:], OP.add, r, done["y", g])]
            done["y", g] = bk.free
        done["comb", e] = r

    P.call(route)
    for e in range(16):
        if e % 4 == 0:
            P.call(lambda e=e: gather(e // 4))
        expert_loads(e)
        P.plain(("g0", e), up(e, B[0], 0, True, False))
        P.plain(("g1", e), up(e, B[0], 1, False, True))
        P.plain(("u0", e), up(e, B[1], 0, True, False))
        P.plain(("u1", e), up(e, B[1], 1, False, True))
        P.call(lambda e=e: hidden(e, 0))
        P.plain(("g2", e), up(e, B[2], 0, True, False))
        P.plain(("u2", e), up(e, B[2], 1, False, True))

        def mark(e=e):
            xe_read[:] = [done["up"]]
            hidden(e, 1)
            weigh(e)
        P.call(mark)
        for j in range(3):
            P.plain((f"d{j}", e), down(e, j))
        P.call(lambda e=e: combine(e))
        if e in (1, 3):
            want_mem(0, 2 + e // 2)
        if e == 4:
            def second():
                t = P.load(mem[:], A["memT"], done["memmm", 0, 3], done["memmm", 0, 1])
                for k in range(KT):
                    done["mem", 1, k] = stt(mem[:, k, :], mem[:, k, :], col("norm_mem_2", 8 + k), rsm[:], OP.mult,
                                            OP.mult, t)
            P.call(second)
        if e in (5, 7, 9, 11):
            want_mem(1, (e - 5) // 2)
        if e == 12:
            P.call(lambda: prepare_c(P, [done["memmm", 1, i] for i in range(4)], [done["h2t", a, g] for a in range(2) for g in range(2)],
                                     done["pos"]))

    class Loop:

        def __init__(self):
            self.q = {n: [] for n in streams}
            self.n = {n: 0 for n in ("act", "pe", "dve", "dma")}
            self.sem = {n: P.sem("more_" + n) for n in self.n}

        def do(self, n, fn, *w, dma=False):
            s = "dma" if dma else n
            self.n[s] += 16 if dma else 1
            self.q[n].append((fn, [x for x in w if x], s, 16 if dma else 1))
            return s, self.n[s]

        def emit(self, n, e, before):
            reg = {s: e.alloc_register(f"more_{n}_{s}") for s in self.n}
            tmp = e.alloc_register(f"more_{n}_tmp")
            with e.If(most[n] > 64):
                for t in before:
                    e.wait_ge(t.sem, t.count)
                for r in reg.values():
                    e.reg_mov(r, 0)
                with e.Fori(1, 4) as blk:
                    with e.Fori(0, 16) as ex:
                        c = e.value_load(counts[0:1, bass.ds(ex, 1)])
                        with e.If(c - blk * 64 > 0):
                            for fn, waits, s, k in self.q[n]:
                                for ws, wc in waits:
                                    e.reg_add(tmp, reg[ws], wc)
                                    e.wait_ge(self.sem[ws], tmp)
                                fn(e, ex, blk).then_inc(self.sem[s], k)
                            for s in self.n:
                                if n == "pe":
                                    e.reg_add(tmp, reg[s], self.whole[s])
                                    e.wait_ge(self.sem[s], tmp)
                            for s in self.n:
                                e.reg_add(reg[s], reg[s], self.n[s])

    def more():
        lp = Loop()
        W = P.at("more_w", Z, [4096])
        pc, wc, base = rt[:, 400:402], rt[:, 402:404], rt[:, 404:405]
        last = [None]

        def lmm(out, l, r, start, stop, *w):
            last[0] = lp.do("pe", lambda e, ex, blk: e.matmul(out, l, r, start=start, stop=stop, skip_group_check=True), *w)
            return last[0]

        def copy(out, i, *w):
            return lp.do("act", lambda e, ex, blk: e.copy(out, i), *w)

        def weights(w, view, *waits):
            return lp.do("act", lambda e, ex, blk: e.dma_start(view, w(ex)), *waits, dma=True)

        t = lp.do("dve", lambda e, ex, blk: e.tensor_copy(base, sm[:, 36:40][:, bass.ds(blk, 1)]))
        tp_ = None
        for a in range(2):
            tp_ = lp.do("dve", lambda e, ex, blk, a=a: e.tensor_copy(pc[:, a:a + 1], posm[:, a, bass.ds(ex, 1)]))
            tw = lp.do("dve", lambda e, ex, blk, a=a: e.tensor_copy(wc[:, a:a + 1], wt[:, a, bass.ds(ex, 1)]))
        t = lp.do("dve", lambda e, ex, blk: e.tensor_scalar(pc, pc, base, None, OP.subtract), t, tp_, tw)
        for a in range(2):
            ts_ = lp.do("dve", lambda e, ex, blk, a=a: e.tensor_scalar(sel[:, a, 0, :], IOTA, pc[:, a:a + 1], None, OP.is_equal), t)
            tw = lp.do("dve", lambda e, ex, blk, a=a: e.tensor_scalar(
                selw[:, a], bc(IOTA, 2, 1), pc[:, a:a + 1], wc[:, a:a + 1], OP.is_equal, OP.mult), t)
        for k in range(KT):
            for a in range(2):
                t = lmm(B[3].t[:, 64 * k:64 * k + 64], h2t[:, a, 128 * k:128 * k + 128], sel[:, a, 0, :], k == 0 and a == 0,
                        a == 1, ts_)
        x64 = xe[:, 0:2, :].rearrange("p a t -> p (a t)")
        tx = copy(x64, B[3].t[:], t)
        for a in range(2):
            t = lp.do("pe", lambda e, ex, blk, a=a: e.transpose(B[6].t[:, 128 * a:128 * a + 128],
                                                             selw[:, a].rearrange("p a b -> p (a b)"), P.EYE), tw)
        tT = copy(selT[0][:], B[6].t[:, 0:256], t)
        tw = None
        for n, w, j, bk, o, st in (("g", "w_eg", 0, 0, 0, True), ("g", "w_eg", 1, 0, 256, False), ("u", "w_eu", 0, 1, 0, True),
                                   ("u", "w_eu", 1, 1, 256, False), ("g", "w_eg", 2, 2, 0, True), ("u", "w_eu", 2, 2, 256, False)):
            w3 = W[:].rearrange("p (k n) -> p k n", k=8)
            ld = weights(lambda ex, w=w, j=j: A[w][bass.ds(ex, 1), :, 512 * j:512 * j + 512].rearrange(
                "o (k p) n -> p (o k) n", p=128), w3, tw)
            for k in range(KT):
                for h in range(2):
                    tw = lmm(B[bk].t[64 * h:64 * h + 64, o:o + 256], x64[:, 64 * k:64 * k + 64], w3[:, k, 256 * h:256 * h + 256],
                             st and k == 0, k == KT - 1, ld, tx)
        for part, (g_, u_) in enumerate(((B[0].t[:], B[1].t[:]), (B[2].t[:, 0:256], B[2].t[:, 256:512]))):
            n = 512 if part == 0 else 256
            h = hid[0][:, 512 * part:512 * part + n]
            t = lp.do("act", lambda e, ex, blk, h=h, g_=g_: e.activation(h, g_, AF.Silu), tw)
            t = lp.do("dve", lambda e, ex, blk, h=h, u_=u_: e.tensor_tensor(h, h, u_, OP.mult), t)
            for j in range(n // 128):
                t2 = lp.do("pe", lambda e, ex, blk, j=j, h=h, part=part: e.transpose(
                    B[3 + part].t[:, 128 * j:128 * j + 128], h[:, 128 * j:128 * j + 128], P.EYE), t, tx)
            th = copy(hidT[0][:, 4 * part:4 * part + n // 128].rearrange("p a b c -> p (a b c)"), B[3 + part].t[:, 0:n], t2)
        for j in range(3):
            w3 = W[:].rearrange("p (k n) -> p k n", k=4)
            ld = weights(lambda ex, j=j: A["w_ed"][bass.ds(ex, 1), 512 * j:512 * j + 512, :].rearrange(
                "o (k p) n -> p (o k) n", p=128), w3, tw)
            for h in range(2):
                for u in range(2):
                    for c in range(2):
                        tw = lmm(B[5].t[64 * c:64 * c + 64, :], hidT[0][:, 2 * j + u, h, :], w3[:, 2 * h + u, 512 * c:512 * c + 512],
                                 j == 0 and h == 0 and u == 0, j == 2 and h == 1 and u == 1, ld, th)
        ty = copy(y[0][:], B[5].t[:], tw)
        rd = [tT, None]
        for g in range(4):
            bk, c = B[6 + g % 2], g // 2
            for j in range(2):
                f = 2 * (g % 2) + j
                t = lmm(bk.t[:, 256 * j:256 * j + 256], y[0][64 * c:64 * c + 64, 128 * f:128 * f + 128],
                        selT[0][64 * c:64 * c + 64, :], j == 0, j == 1, ty, tT, rd[g % 2])
            dst = pa(yacc[:, 4 * c + 2 * (g % 2):4 * c + 2 * (g % 2) + 2, :])
            rd[g % 2] = lp.do("dve", lambda e, ex, blk, dst=dst, bk=bk: e.tensor_tensor(dst, dst, bk.t[:], OP.add), t)
        lp.whole = dict(lp.n)
        lp.do("act", lambda e, ex, blk: e.copy(rt[:, 406:407], sm[:, 0:1]), *lp.whole.items())
        lp.do("dve", lambda e, ex, blk: e.tensor_copy(rt[:, 407:408], sm[:, 0:1]), *lp.whole.items())
        before = list(flat([done["comb", 15], [done["y", g] for g in range(4)], P.kv_tok, P.stage_free, done["selT", 15]]))
        for t in before:
            t.used = True
        for n in streams:
            P.raw(streams[n], lambda e, n=n: lp.emit(n, e, before))
    P.call(more)

    def last_norm():
        gt2 = P.gt2
        for k in range(KT):
            P.x_tok[k] = stt(x[:, k, :], yacc[:, k, :], gt2[:, k:k + 1], x[:, k, :], OP.mult, OP.add, done["y", k // 2],
                             P.modcol, done["gather"])
        t = af(sq[:], x[:], AF.Square, P.x_tok.values(), xe_read)
        for k in range(KT):
            t2 = mm(B[4].t[:, 0:T], ONE, sq[:, k, :], k == 0, k == KT - 1, t, B[4].free)
        t = af(rs[:], B[4].t[:, 0:T], AF.Sqrt, t2, bias=EPS, scale=1.0 / 1024)
        B[4].free = [t]
        t = rcp(rs[:], rs[:], t)
        for k in range(KT):
            P.x_tok[k] = stt(x[:, k, :], x[:, k, :], col("g_final", k), rs[:], OP.mult, OP.mult, t)
    P.call(last_norm)


C_MASKS = ["level4", "level5", "level6", "last", "dup", "sixteen", "same"]
C_SMALL = ["freq_sa", "sign_sa", "freq_ix", "sign_ix", "eps_q"]
N_CC = 128 * len(C_MASKS) + 32
TURN = 2 * np.pi
TURN1 = 6.28125
TURN2 = float(np.floor((TURN - TURN1) * 2.0 ** 20) / 2.0 ** 20)
TURN3 = float(np.float32(TURN - TURN1 - TURN2))
HALF_TURN = 3.1415925
BIG = -1e30
TAKEN = -3e38


def constants_c():
    p, f = np.meshgrid(np.arange(128), np.arange(128), indexing="ij")
    m = {f"level{i}": (p >> (i + 1) == f >> (i + 1)) & (p >> i > f >> i) for i in (4, 5, 6)}
    m["last"] = p == 127
    m["dup"] = p == f % 64
    m["sixteen"] = p // 16 == f // 16
    m["same"] = np.where(f // 64 <= p // 64, 0.0, BIG)
    sm = np.zeros((128, 32), np.float32)
    for c, (head, half) in ((0, (128, 16)), (2, (64, 8))):
        rd = 2 * half
        freq = np.float32(500000.0) ** -(np.arange(half, dtype=np.float32) * np.float32(2.0) / np.float32(rd))
        for r in range(128):
            k = r % head
            if k < rd:
                sm[r, c] = freq[k % half]
                sm[r, c + 1] = -1.0 if k < half else 1.0
    sm[:, 4] = 1.28e-10
    sm[:, 16:32] = np.arange(128)[:, None] % 16 == np.arange(16)
    return np.concatenate([m[n].astype(np.float32) for n in C_MASKS] + [sm], axis=1)


class Layout2:
    KQ, V = (4096, 10240), (6144, 12288)
    CC, ROPE = 8192, 9152
    D, G, U, TT = 13312, 14848, 17920, 18944
    ODN, XQ = 19968, 22016
    IQ, SMT, IK, SCORE, RELU = 24064, 25088, 25344, 25600, 25984
    MK, MV = 26576, 28624
    WSM, TURNS = (13312, 22016), 12288
    Y = 7168


def small_weights(P, l, *w):
    A, Z = P.A, P.Z
    o = Z + Layout2.WSM[l]
    t = P.at(f"wsm{l}", o, [KT, 128])
    z = P.fill(t[:], 0.0, *w, on=P.pool)
    return t, P.at(f"wsm{l}_lo", o, [KT, 128], F32R), [
        P.load(t[:, :, c:c + n], A["w_small"][l, :, :, s:s + n], z, q=P.pool)
        for c, s, n in ((0, 0, 64), (64, 64, 8), (96, 72, 16))]


def prepare_c(P, *w):
    A, Z, L = P.A, P.Z, Layout2
    tt, ts, stt, cp, af = P.tt, P.ts, P.stt, P.cp, P.af
    cc = P.cc = P.at("cc", Z + L.CC, [N_CC])
    rope = P.rope = P.at("rope", Z + L.ROPE, [4, T])
    P.cm = {n: cc[:, 128 * i:128 * i + 128] for i, n in enumerate(C_MASKS)}
    o = 128 * len(C_MASKS)
    cs = P.ccol = {n: cc[:, o + i:o + i + 1] for i, n in enumerate(C_SMALL)}
    P.e16 = cc[:, o + 16:o + 32]
    P.l_cc = l_cc = P.load(cc[:], A["cstc"], *w, q=P.pool)
    posi = P.nc.alloc_sbuf_tensor_at("posi", [128, T], I32, offset=BASE + 4 * (Z + L.TURNS))
    l_pos = P.load(posi[:], A["positions"].partition_broadcast(128), *w, q=P.pool)
    P.wsm = [small_weights(P, 0, *w), None]
    P.hb = P.small[:, 376:424]
    P.hb_tok = ts(P.hb, P.col("b_gate_2", 0, 48), 0.5, None, OP.mult, None)

    def tables():
        a0, a1, a2 = (P.at(f"rp{i}", Z + L.TURNS + 256 + 256 * i, [T])[:] for i in range(3))
        t = cp(a2, posi[:], l_pos)
        for i, n in enumerate(("sa", "ix")):
            f, sg = cs["freq_" + n], cs["sign_" + n]
            for j in range(2):
                t = ts(a0, a2, f, None, OP.mult, None, t, l_cc)
                t = ts(a1, a0, 1.0 / TURN, 0.25 * (1 - j), OP.mult, OP.add, t)
                t = ts(a1, a1, 12582912.0, -12582912.0, OP.add, OP.add, t)
                for c in (TURN1, TURN2, TURN3):
                    t = stt(a0, a1, -c, a0, OP.mult, OP.add, t)
                if j == 0:
                    t = ts(a0, a0, TURN / 4, None, OP.add, None, t)
                t = ts(a0, a0, HALF_TURN, -HALF_TURN, OP.min, OP.max, t)
                t = af(rope[:, 2 * i + j, :], a0, AF.Sin, t, *w)
                if j == 1:
                    t = ts(rope[:, 2 * i + 1, :], rope[:, 2 * i + 1, :], sg, None, OP.mult, None, t)
                yield
        P.rope_tok = [t]
    P.lanes.append([tables()])


def phase_c(P, out):
    A, Z, L = P.A, P.Z, Layout2
    mm, tp, af, acp, tt, ts, stt, cp, rcp, red = P.mm, P.tp, P.af, P.acp, P.tt, P.ts, P.stt, P.cp, P.rcp, P.red
    col, sm, ONE, EYE, EPS, x, B = P.col, P.sm, P.ONE, P.EYE, P.EPS, P.x, P.banks
    LE, cm, l_cc, rope, hb = P.mask["le"], P.cm, P.l_cc, P.rope, P.hb
    pa = lambda a: a.rearrange("p a t -> p (a t)")
    at = lambda n, o, s, dt=F32: P.at(n, Z + o, s, dt)

    H = Part(at("h_hi", 0, [KT, T], F32R), at("h_lo", 2048, [KT, T], F32R))
    KQ = [at(f"kq{g}", L.KQ[g], [4, 2, 2, 128]) for g in range(2)]
    V = [at(f"v{g}", L.V[g], [4, 2, 128]) for g in range(2)]
    D, G = at("dd", L.D, [4, 3, 128]), at("gg", L.G, [24, 128])
    U, Tm = at("uu", L.U, [8, 128]), at("tt", L.TT, [8, 128])
    sys_u, sys_t, sys_m = at("su", L.D, [8, 16]), at("st", L.D + 128, [8, 16]), at("sm_", L.D + 256, [8, 16])
    Q = at("qq", L.D + 512, [8, 128])
    rows = at("rows", L.U, [16, 128])
    odn, xq = at("odn", L.ODN, [KT, T]), at("xq", L.XQ, [KT, T])
    iq, ik, smT = at("iq", L.IQ, [4, T]), at("ik", L.IK, [T]), at("smT", L.SMT, [T])
    score, relu = at("score", L.SCORE, [384]), at("relu", L.RELU, [512])
    Y = [at(f"y_{i}", L.Y + 512 * i, [2, T]) for i in range(2)]
    PM = [at(f"pm{i}", L.ODN + 512 * i, [512]) for i in range(4)]
    PC = [at(f"pc{i}", L.V[0] + 512 * i, [512]) for i in range(4)]
    mk, mv = P.mk, P.mv
    mg = at("mg", L.MK, [KT, T])
    sq_, sk_, sv_ = at("sq_", L.XQ, [KT, T]), at("sk_", L.KQ[0], [KT, T]), at("sv_", L.MV, [2, 1024])
    gate = at("gate", L.IQ, [4, T])
    XA = Part(at("xa_hi", L.MV, [KT, T], F32R), at("xa_lo", L.XQ, [KT, T], F32R))
    SA = Part(at("sa_hi", L.KQ[0], [KT, T], F32R), at("sa_lo", L.XQ, [KT, T], F32R))
    DN = Part(at("dn_hi", L.D, [KT, T], F32R), at("dn_lo", L.ODN, [KT, T], F32R))
    MG = Part(at("m_hi2", L.U, [KT, T], F32R), at("m_lo2", L.MK, [KT, T], F32R))
    zt = [at(f"zt{i}", L.KQ[1] + 512 * i, [2, T]) for i in range(2)]
    hsq, hn = at("hsq", L.G, [KT, T]), at("hn", L.G + 2048, [KT, T])
    rs = at("rs_", L.RELU, [T])
    FH, FL = at("f_hi", L.KQ[1], [22, T], F32R), at("f_lo", L.KQ[1] + 5632, [22, T], F32R)
    fg = [at(f"fg{i}", L.KQ[0] + 1024 * i, [4, T]) for i in range(2)]
    fa = [at(f"fa{i}", L.V[0] + 512 * i, [512]) for i in range(2)]
    tokm = P.small[:, 240:336].rearrange("p (c n) -> p c n", c=2)
    ekd = P.small[:, 336:344]
    ss, r8, bp, s8 = (P.small[:, 344 + 8 * i:352 + 8 * i] for i in range(4))
    alog = P.small[64:72, 424:428]
    mx, nmx, sums = P.small[:, 428:444], P.small[:, 444:460], P.small[:, 460:476]
    top8 = P.small[:, 476:492]
    for i in range(P.NB):
        P.pe_read[i] = [P.pe_read[i], P.doneB["down", 15]]

    SW16 = list(range(16, 32)) + list(range(16))
    SW8 = list(range(8, 16)) + list(range(8)) + list(range(16, 32))

    def rotate(a, n, ci, tmp, mask_, *w):
        p = a.shape[0]
        cos, sin = (bc(rope[0:p, 2 * ci + j, :], n, 1) for j in range(2))
        t0 = P.dve.do(lambda e: e.stream_shuffle(tmp, a, mask_), *w)
        t1 = tt(tmp, tmp, sin, OP.mult, t0, P.rope_tok)
        t2 = tt(a, a, cos, OP.mult, t0, P.rope_tok)
        return tt(a, a, tmp, OP.add, t1, t2)

    sqt = {}

    def square(j, n, t):
        t = af(pa(hsq[:, j:j + n, :]), pa(x[:, j:j + n, :]), AF.Square, t)
        for k in range(j, j + n):
            sqt[k] = t

    def norm(gname, c, to):
        for k in range(KT):
            t = mm(B[7].t[:, 0:T], ONE, hsq[:, k, :], k == 0, k == KT - 1, sqt[k], B[7].free)
        t = af(rs[:], B[7].t[:, 0:T], AF.Ln, t, bias=EPS, scale=1.0 / 1024)
        B[7].free = [t]
        t = af(rs[:], rs[:], AF.Exp, t, scale=-0.5)
        for k in range(KT):
            to(k, stt((hn if to is split_h else x)[:, k, :], x[:, k, :], col(gname, c + k), rs[:], OP.mult, OP.mult, t,
                      P.x_tok[k]))

    def split_h(k, t):
        P.split_x(H, k, hn[:, k, :], t)

    def layer(l):
        done = {}
        w_in = A["w_in_2"][l]
        need, wait = lambda *ks: P.need(done, *ks), P.wait
        xt = [P.x_tok[k] for k in range(KT)]
        wsm, wsm_lo, l_sm = P.wsm[l]
        l_al = [P.load(alog[:, 0:1], A["a_log"][l], P.alog_free, q=P.pool),
                P.load(alog[:, 1:2], A["dt_bias"][l], P.alog_free, q=P.pool)]

        def narrow(q):
            bk = P.bank()
            for k in range(KT):
                for w, v, wt in ((q.hi, H.hi, q.th), (q.hi, H.lo, q.th), (q.lo, H.hi, q.tl)):
                    t = mm(bk.t[:, 0:T], w[:, k, :], v[:, k, :], k == 0 and v is H.hi and w is q.hi,
                           k == KT - 1 and w is q.lo, wt, H.tok[k], bk.free)
            done["small"] = acp(smT[:], bk.t[:, 0:T], t)
            bk.free = [done["small"]]
            return t

        def strengths():
            yield from need("small")
            w = done["small"]
            z, tmp, be = smT[64:72, :], relu[64:72, 0:256], smT[96:104, :]
            t = af(alog[:, 2:3], alog[:, 0:1], AF.Exp, l_al)
            t0 = ts(alog[:, 2:3], alog[:, 2:3], -1.0, None, OP.mult, None, t)
            t = af(tmp, z, AF.Abs, w, l_al, bias=alog[:, 1:2])
            t = af(tmp, tmp, AF.Exp, t, scale=-1.0)
            t3 = af(be, be, AF.Tanh, w, scale=0.5)
            t1 = af(tmp, tmp, AF.Ln, t, bias=ONE[64:72, 0:1])
            t3 = ts(be, be, 0.5, 0.5, OP.mult, OP.add, t3)
            t = ts(z, z, alog[:, 1:2], 0.0, OP.add, OP.max, t1)
            t = tt(z, z, tmp, OP.add, t)
            t = ts(z, z, alog[:, 2:3], None, OP.mult, None, t, t0)
            P.alog_free = [t]
            for c in range(2):
                s_ = smT[64:72, 128 * c:128 * c + 128]
                t2 = P.dve.do(lambda e, s_=s_: e.tensor_tensor_scan(s_, s_, s_, 0.0, OP.add, OP.bypass), t)
            done["gcT"] = t2
            yield
            bk = B[7]
            for c in range(2):
                t4 = tp(bk.t[:, 128 * c:128 * c + 128], smT[:, 128 * c:128 * c + 128], t2, t3, bk.free)
            t = cp(tokm[:], bk.t[:, 0:256].rearrange("p (c n) -> p c n", c=2)[:, :, 64:112], t4)
            bk.free = [t]
            done["tokm"] = t = ts(tokm[:, :, 40:48], tokm[:, :, 40:48], 512 ** -0.5, None, OP.mult, None, t)
            yield
            t5 = mm(bk.t[:, 0:8], cm["last"], tokm[:, 0, 0:8], True, True, t, bk.free, l_cc)
            done["ekd"] = tt(ekd, bk.t[:, 0:8], tokm[:, 0, 0:8], OP.subtract, t5)
            bk.free = [done["ekd"]]

        def index():
            yield from need("small")
            bk = B[3]
            t = mm(bk.t[:, 0:T], cm["dup"][0:64, :], smT[0:64, :], True, True, done["small"], bk.free, l_cc)
            t = acp(ik[:], bk.t[:, 0:T], t)
            bk.free = [t]
            yield from need("tokm", ("iq", 0), ("iq", 1))
            tmp = PM[0][:].rearrange("p (n t) -> p n t", n=2)
            tk = rotate(ik[:].unsqueeze(1), 1, 1, tmp[:, 0:1], SW8, t)
            ti = rotate(iq[:, 0:2, :], 2, 1, tmp, SW8, done["iq", 0], tk)
            yield
            ti = rotate(iq[:, 2:4, :], 2, 1, tmp, SW8, done["iq", 1], ti)
            yield from wait(2)
            ta = [None, None]
            for h in range(8):
                ps = slice(64 * (h % 2), 64 * (h % 2) + 64)
                bk = B[3 + h % 2]
                for b in range(2):
                    n = 128 * (b + 1)
                    t = mm(bk.t[:, 128 * b:128 * b + n], iq[ps, h // 2, 128 * b:128 * b + 128], ik[ps, 0:n], b == 0, b == 1,
                           ti, tk, bk.free)
                t = af(relu[:, 0:384], bk.t[:, 0:384], AF.Relu, t, ta, done["tokm"])
                bk.free = [t]
                if h == 0:
                    for b in range(2):
                        t2 = stt(score[:, 256 * b:256 * b + 128], relu[:, 256 * b:256 * b + 128], tokm[:, b, 40:41], cm["same"],
                                 OP.mult, OP.add, t, P.maskb_free, l_cc)
                    ta = [ts(score[:, 128:256], relu[:, 128:256], tokm[:, 1, 40:41], None, OP.mult, None, t), t2]
                else:
                    ta = [stt(score[:, o_:o_ + n], relu[:, o_:o_ + n], tokm[:, b, 40 + h:41 + h], score[:, o_:o_ + n],
                              OP.mult, OP.add, t, ta[b]) for b, o_, n in ((0, 0, 128), (1, 128, 256))]
                yield
            done["score"] = ta

        def best():
            ta = list(done["score"])
            for r in range(8):
                t = []
                for b, o_, n in ((0, 0, 128), (1, 128, 256)):
                    t.append(P.dve.do(lambda e, b=b, o_=o_, n=n: e.max(top8[:, 8 * b:8 * b + 8], score[:, o_:o_ + n]), ta[b]))
                for b, o_, n in ((0, 0, 128), (1, 128, 256)):
                    ta[b] = P.dve.do(lambda e, b=b, o_=o_, n=n: e.match_replace(
                        score[:, o_:o_ + n], top8[:, 8 * b:8 * b + 8], score[:, o_:o_ + n], TAKEN), t[b])
                yield
            done["maskb"] = ts(score[:], score[:], 0.5 * TAKEN, BIG, OP.is_gt, OP.mult, ta)

        nr, y_free = [0], [[], []]

        def conv_in(kind, g):
            def f(xp, b, c, t):
                n = nr[0]
                nr[0] += 1
                y_ = Y[n % 2]
                h = 2 * ((c % 512) // 256)
                w = lambda j, a: col("conv_w_2", 96 * l + 24 * j + 8 * kind + 4 * g + h + a)
                src = [b[:, 256 * a:256 * a + 256] for a in range(2)]
                ty = [af(y_[:, a, :], src[a], AF.Copy, t, y_free[n % 2], scale=w(3, a)) for a in range(2)]
                ty = [ty, ty]
                for j in (2, 1, 0):
                    s = 3 - j
                    ty = [stt(y_[:, a, s:], src[a][:, 0:T - s], w(j, a), y_[:, a, s:], OP.mult, OP.add, ty[a]) for a in range(2)]
                dst = V[g][:, h:h + 2] if kind == 2 else KQ[g][:, h:h + 2, :, 1 - kind, :]
                r = af(dst, y_[:].rearrange("p a (c n) -> p a c n", c=2), AF.Silu, ty)
                y_free[n % 2] = [r]
                done["qkv"[kind], g, h] = r
                return ty
            return f

        def delta(g):
            kq, v = KQ[g], V[g]
            bank = [B[5], B[6], B[7]]
            g8 = lambda i: G[:, 8 * i:8 * i + 8, :]
            gcol = lambda c, h: tokm[:, c, 4 * g + h:4 * g + h + 1]
            M = g8(0)
            MA = G[:].rearrange("p (k b) n -> p k b n", k=3)
            KA = G[:, 16:24, :].rearrange("p (k h) n -> p k h n", k=2)
            yield from need("ekd", *[(n, g, h) for n in "kq" for h in (0, 2)])
            if g:
                yield from need(("dn", 0))
            for p in range(2):
                bk = bank[p]
                for a in range(2):
                    h = 2 * p + a
                    t = mm(bk.t[:, 256 * a:256 * a + 256], bc(EYE[64:96, 64 + 4 * g + h:65 + 4 * g + h].squeeze(1), 128, 1),
                           smT[64:96, :], a == 0, a == 1, done["gcT"], bk.free)
                for a in range(2):
                    h = 2 * p + a
                    s0, s1 = bk.t[:, 256 * a:256 * a + 128], bk.t[:, 256 * a + 128:256 * a + 256]
                    ts(D[:, h, 0, :], s0, gcol(0, h), 0.0, OP.subtract, OP.min, t, done["tokm"])
                    ts(D[:, h, 1, :], s1, ekd[:, 4 * g + h:4 * g + h + 1], 0.0, OP.add, OP.min, done["ekd"])
                    td = ts(D[:, h, 2, :], s1, gcol(1, h), 0.0, OP.subtract, OP.min)
                bk.free = [td]
                yield
            tD = af(D[:], D[:], AF.Exp, td)
            yield from wait(2)
            for p in range(2):
                bw = bank[2]
                inp = [done[n, g, 2 * p] for n in "kq"]
                tm = []
                for a in range(2):
                    h = 2 * p + a
                    bk = bank[a]
                    t = mm(bk.t[:], kq[:, h, 0, 0, :], kq[:, h].rearrange("p c a n -> p (c a n)"), True, True, inp, bk.free)
                    t2 = mm(bw.t[:, 256 * a:256 * a + 256], kq[:, h, 1, 0, :], kq[:, h, 1].rearrange("p a n -> p (a n)"), a == 0,
                            a == 1, bw.free)
                    tm.append((t, t2))
                for a in range(2):
                    h = 2 * p + a
                    bk = bank[a]
                    b2 = lambda o: bk.t[:, o:o + 256].rearrange("p (a n) -> p a n", a=2)
                    tt(MA[:, 0:2, 2 * h, :], b2(0), bc(D[:, h, 0, :], 2, 1), OP.mult, tm[a][0], tD)
                    tG = tt(KA[:, :, h, :], b2(256), bc(D[:, h, 1, :], 2, 1), OP.mult)
                    bk.free = [tG]
                for a in range(2):
                    h = 2 * p + a
                    tG = tt(MA[:, 0:2, 2 * h + 1, :], bw.t[:, 256 * a:256 * a + 256].rearrange("p (a n) -> p a n", a=2),
                            bc(D[:, h, 2, :], 2, 1), OP.mult, tm[1][1], tD)
                bw.free = [tG]
                yield
            t = tt(U[:], M, bc(cm["sixteen"], 8, 1), OP.mult, tG, l_cc)
            t = red(sys_m[:], U[:].rearrange("p s (b i) -> p s i b", b=8), OP.add, t)
            t2 = tt(sys_t[:], sys_m[:], bc(P.e16, 8, 1), OP.mult, t)
            t2 = red(ss, sys_t[:], OP.add, t2)
            t2 = ts(ss, ss, 1e-6, None, OP.add, None, t2)
            ts8 = af(s8, ss, AF.Sqrt, t2)
            t2 = rcp(r8, ss, t2)
            tb = tt(bp.rearrange("p (h c) -> p h c", h=4), r8.rearrange("p (h c) -> p h c", h=4),
                    tokm[:, :, 32 + 4 * g:36 + 4 * g].rearrange("p c h -> p h c"), OP.mult, t2)
            t = tt(sys_m[:], sys_m[:], bc(bp, 16, 2), OP.mult, tb)
            tu = cp(sys_u[:], bc(P.e16, 8, 1))
            yield
            yield from wait(2)
            md = sys_m[:].rearrange("p s i -> p (s i)")
            tj = []

            def spread(i):
                n = 4 if i < 3 else 3
                te = tt(rows[:, 4 * i:4 * i + n, :], bc(md, n, 1), bc(P.e16[:, 4 * i:4 * i + n], 128, 2), OP.mult, t)
                tj.append(mm(bank[i % 3].t[:, 0:128 * n], cm["sixteen"], rows[:, 4 * i:4 * i + n, :].rearrange("p j n -> p (j n)"),
                             True, True, te, bank[i % 3].free))
            for i in range(4):
                if i < 3:
                    spread(i)
            tM = tt(M, M, bc(bp, 128, 2), OP.mult, tb)
            tA = tt(g8(1), g8(1), bc(LE, 8, 1), OP.mult, tG)
            yield
            for j in range(15):
                if j == 4:
                    spread(3)
                bk = bank[j // 4 % 3]
                mj = bk.t[:, 128 * (j % 4):128 * (j % 4) + 128].rearrange("p (s i) -> p s i", s=8)[:, :, j + 1:]
                tu = tt(sys_t[:, :, j + 1:], mj, bc(sys_u[:, :, j:j + 1].squeeze(2), 15 - j, 2), OP.mult, tu, tj[j // 4])
                tu = tt(sys_u[:, :, j + 1:], sys_u[:, :, j + 1:], sys_t[:, :, j + 1:], OP.subtract, tu)
                if j % 4 == 3 or j == 14:
                    bk.free = [tu]
                    yield
            tU = tt(U[:].rearrange("p s (b i) -> p s b i", b=8), bc(sys_u[:], 8, 2),
                    bc(cm["sixteen"].rearrange("p (b i) -> p b i", b=8), 8, 1), OP.mult, tu)
            yield from need(("v", g, 0), ("v", g, 2))
            for p in range(2):
                bk = bank[p]
                for i in range(4):
                    t = tp(bk.t[:, 128 * i:128 * i + 128], v[:, 2 * p + i // 2, i % 2, :], done["v", g, 2 * p], bk.free)
                tv = tt(v[:, 2 * p:2 * p + 2].rearrange("p h c n -> p (h c) n"), bk.t[:].rearrange("p (s n) -> p s n", s=4),
                        bc(s8[:, 4 * p:4 * p + 4], 128, 2), OP.mult, t, ts8)
                bk.free = [tv]
            yield
            tT = []
            for p in range(2):
                bk = bank[(2 + p) % 3]
                for i in range(4):
                    t = tp(bk.t[:, 128 * i:128 * i + 128], U[:, 4 * p + i, :], tU, bk.free)
                r = acp(Tm[:, 4 * p:4 * p + 4, :], bk.t[:].rearrange("p (s n) -> p s n", s=4), t)
                bk.free = [r]
                tT.append(r)
            tU, tQf = [tU, tU], [None, None]
            yield
            b4 = lambda bk: bk.t[:].rearrange("p (s n) -> p s n", s=4)
            for lv in (4, 5, 6):
                tQ = []
                for p in range(2):
                    bk = bank[p]
                    for i in range(4):
                        s = 4 * p + i
                        t = mm(bk.t[:, 128 * i:128 * i + 128], M[:, s, :], Tm[:, s, :], i == 0, i == 3, tM, tT[p], bk.free)
                    t = tt(Q[:, 4 * p:4 * p + 4, :], b4(bk), bc(cm[f"level{lv}"], 4, 1), OP.mult, t, tQf[p])
                    bk.free = [t]
                    tQ.append(t)
                yield from wait(2)
                for p in range(2):
                    bu, bt = bank[p], bank[2]
                    p4 = slice(4 * p, 4 * p + 4)
                    if lv < 6:
                        for i in range(4):
                            s = 4 * p + i
                            t = mm(bt.t[:, 128 * i:128 * i + 128], U[:, s, :], Q[:, s, :], i == 0, i == 3, tQ[p], tU[p], bt.free)
                    for i in range(4):
                        s = 4 * p + i
                        t2 = mm(bu.t[:, 128 * i:128 * i + 128], Q[:, s, :], U[:, s, :], i == 0, i == 3, tQ[p], tU[p], bu.free)
                    tQf[p] = t2
                    if lv < 6:
                        tT[p] = tt(Tm[:, p4, :], Tm[:, p4, :], b4(bt), OP.subtract, t)
                        bt.free = [tT[p]]
                    tU[p] = tt(U[:, p4, :], U[:, p4, :], b4(bu), OP.subtract, t2)
                    bu.free = [tU[p]]
                yield
            X, Y_, W = bank
            sl = lambda h: slice(128 * h, 128 * h + 128)
            h4 = lambda bk: bk.t[:].rearrange("p (h n) -> p h n", h=4)
            bpc = lambda c: bc(bp.rearrange("p (h c) -> p h c", h=4)[:, :, c:c + 1].squeeze(2), 128, 2)
            for h in range(4):
                t = mm(Y_.t[:, sl(h)], U[:, 2 * h, :], v[:, h, 0, :], h == 0, h == 3, tU, tv, Y_.free)
            t0 = tt(v[:, :, 0, :], h4(Y_), bpc(0), OP.mult, t)
            Y_.free = [t0]
            tq = af(Tm[:].rearrange("p (h c) n -> p h c n", h=4), kq[:, :, :, 1, :], AF.Square, tT, tQf, scale=0.128)
            yield
            for h in range(4):
                t = mm(Y_.t[:, sl(h)], KA[:, 0, h, :], v[:, h, 0, :], h == 0, h == 3, t0, Y_.free)
            t1 = tt(v[:, :, 1, :], v[:, :, 1, :], h4(Y_), OP.subtract, t)
            Y_.free = [t1]
            for h in range(4):
                bk, o_ = (X, W)[h // 2], 256 * (h % 2)
                mm(bk.t[:, o_:o_ + 128], v[:, h, 0, :], MA[:, 1, 2 * h, :], h % 2 == 0, False, t0, tA, bk.free)
                mm(bk.t[:, o_ + 128:o_ + 256], v[:, h, 0, :], KA[:, 1, h, :], False, False)
            yield
            for h in range(4):
                t = mm(Y_.t[:, sl(h)], U[:, 2 * h + 1, :], v[:, h, 1, :], h == 0, h == 3, t1, Y_.free)
            t1 = tt(v[:, :, 1, :], h4(Y_), bpc(1), OP.mult, t)
            Y_.free = [t1]
            yield
            to = []
            for h in range(4):
                bk, o_ = (X, W)[h // 2], 256 * (h % 2)
                t = mm(bk.t[:, o_ + 128:o_ + 256], v[:, h, 1, :], MA[:, 1, 2 * h + 1, :], False, h % 2 == 1, t1)
                if h % 2:
                    to.append(t)
            sqd = Q[:].rearrange("p (h c) n -> p h (c n)", h=4)
            q2 = Tm[:].rearrange("p (h c) n -> p h (c n)", h=4)
            tc, ts_ = [], []
            for p, bk in enumerate((X, W)):
                i = bk.t[:].rearrange("p (h n) -> p h n", h=2)
                t = af(sqd[:, 2 * p:2 * p + 2, :], i, AF.Square, to[p], tQf)
                r = acp(odn[:, 4 * g + 2 * p:4 * g + 2 * p + 2, :], i, to[p], xa_done())
                bk.free = [t, r]
                tc.append(r)
                ts_.append(tt(sqd[:, 2 * p:2 * p + 2, :], sqd[:, 2 * p:2 * p + 2, :], q2[:, 2 * p:2 * p + 2, :], OP.add, t, tq))
            yield from wait(2)
            rn = U[:].rearrange("p (h c) n -> p h (c n)", h=4)
            for p in range(2):
                bk = (Y_, X)[p]
                for a in range(2):
                    t = mm(bk.t[:, 256 * a:256 * a + 256], ONE, sqd[:, 2 * p + a, :], a == 0, a == 1, ts_[p], bk.free)
                r = af(pa(rn[:, 2 * p:2 * p + 2, :]), bk.t[:], AF.Ln, t, bias=P.ccol["eps_q"], scale=1.0 / 128)
                bk.free = [r]
            yield
            t = af(rn, rn, AF.Exp, r, scale=-0.5)
            o4 = odn[:, 4 * g:4 * g + 4, :]
            done["dn", g] = stt(o4, o4, col("dn_norm_2", l), rn, OP.mult, OP.mult, t, tc)

        def memory(h):
            bk = B[3 + h % 2]
            w = [done["xq", h], P.kv_tok]
            for b in range(2):
                for k in range(2):
                    t = mm(bk.t[:, 256 * b:256 * b + 256], xq[:, 2 * h + k, 128 * b:128 * b + 128], mk[:, 2 * h + k, :],
                           b == 0 and k == 0, b == 1 and k == 1, w, bk.free)
            m2, n2, s2 = mx[:, 2 * h:2 * h + 2], nmx[:, 2 * h:2 * h + 2], sums[:, 2 * h:2 * h + 2]
            p_, pt = PM[h % 2], PM[2 + h % 2]
            t = red(m2, bk.t[:].rearrange("p (b n) -> p b n", b=2), OP.max, t, P.sm_free)
            t = ts(n2, m2, -1.0 / 16, None, OP.mult, None, t)
            for b in range(2):
                t2 = af(p_[:, 256 * b:256 * b + 256], bk.t[:, 256 * b:256 * b + 256], AF.Exp, t, pt_free[h % 2], done["tokm"],
                        bias=n2[:, b:b + 1], scale=1.0 / 16, accum=s2[:, b:b + 1])
            t = rcp(s2, s2, t2)
            p3 = p_[:].rearrange("p (b n) -> p b n", b=2)
            t = tt(p3, p3, bc(s2, 256, 2), OP.mult, t)
            yield
            for k in range(2):
                for b in range(2):
                    t2 = tp(bk.t[:, 256 * k + 128 * b:256 * k + 128 * b + 128], p_[:, 256 * b + 128 * k:256 * b + 128 * k + 128], t)
            t = acp(pt[:], bk.t[:], t2, pt_free[2 + h % 2])
            pt_free[h % 2] = [t2]
            yield
            for j in range(2):
                for k in range(2):
                    t2 = mm(bk.t[:, 256 * j:256 * j + 256], mv[:, k, 256 * h + 128 * j:256 * h + 128 * j + 128],
                            pt[:, 256 * k:256 * k + 256], j == 0 and k == 0, j == 1 and k == 1, t)
            pt_free[2 + h % 2] = [t2]
            r = acp(pa(xq[:, 2 * h:2 * h + 2, :]), bk.t[:], t2)
            bk.free = [r]
            done["xa", h] = r

        pt_free = [[], [], [], []]

        def chosen(h):
            bk = B[3 + h % 2]
            S = 128 ** -0.5
            w = [done["rq", h // 2], done["rk", h // 2]]
            for b in range(2):
                n = 128 * (b + 1)
                t = mm(bk.t[:, 128 * b:128 * b + n], sq_[:, h, 128 * b:128 * b + 128], sk_[:, h, 0:n], b == 0, b == 1, w, bk.free)
            m2, n2, s2 = mx[:, 2 * h:2 * h + 2], nmx[:, 2 * h:2 * h + 2], sums[:, 2 * h:2 * h + 2]
            p_, pt = PC[h % 2], PC[2 + h % 2]
            tb = []
            for b in range(2):
                o_, n = 128 * b, 128 * (b + 1)
                tb.append(P.dve.do(lambda e, b=b, o_=o_, n=n: e.tensor_tensor_reduce(
                    out=p_[:, o_:o_ + n], in0=bk.t[:, o_:o_ + n], in1=score[:, o_:o_ + n], op0=OP.add, op1=OP.max, scale=S,
                    scalar=-3e38, accum_out=m2[:, b:b + 1]), t, done["maskb"], pt_free[h % 2], done["dn", 0], done["xa"]))
            t = ts(n2, m2, -1.0, None, OP.mult, None, tb)
            for b in range(2):
                o_, n = 128 * b, 128 * (b + 1)
                t2 = af(p_[:, o_:o_ + n], p_[:, o_:o_ + n], AF.Exp, t, bias=n2[:, b:b + 1], accum=s2[:, b:b + 1])
            t = rcp(s2, s2, t2)
            for b in range(2):
                o_, n = 128 * b, 128 * (b + 1)
                t3 = ts(p_[:, o_:o_ + n], p_[:, o_:o_ + n], s2[:, b:b + 1], None, OP.mult, None, t)
            yield
            for i in range(3):
                t2 = tp(bk.t[:, 128 * i:128 * i + 128], p_[:, 128 * i:128 * i + 128], t3, tb)
            t = acp(pt[:, 0:384], bk.t[:, 0:384], t2, pt_free[2 + h % 2], done["dn", 0])
            pt_free[h % 2] = [t2]
            yield
            mm(bk.t[:, 0:256], sv_[:, 0, 128 * h:128 * h + 128], pt[:, 0:256], True, False, t, done["sv_", h // 2])
            t2 = mm(bk.t[:, 128:256], sv_[:, 1, 128 * h:128 * h + 128], pt[:, 256:384], False, True)
            pt_free[2 + h % 2] = [t2]
            r = acp(sq_[:, h, :], bk.t[:, 0:256], t2)
            bk.free = [r]
            done["sa", h] = r

        xa_done = lambda: [done["xa", h] for h in range(4)]

        def attend():
            yield from index()
            for i in range(0, 4, 2):
                yield from need(("xq", i), ("xq", i + 1))
                gs = [memory(i), memory(i + 1)]
                while gs:
                    gs = [g_ for g_ in gs if next(g_, "end") != "end"]
                    yield
            done["xa"] = xa_done()
            yield from best()
            yield from need(("dn", 0))
            for i in range(4):
                yield from need(("rk", i), ("sv_", i))
                yield from wait(2)
                gs = [chosen(2 * i), chosen(2 * i + 1)]
                while gs:
                    gs = [g_ for g_ in gs if next(g_, "end") != "end"]
                    yield
            done["sa"] = [done["sa", h] for h in range(8)]
            P.maskb_free = [done["sa"]]

        def ev_copy(name, dst, base, *w):
            def f(xp, b, c, t):
                j = (c - base) // 128
                done[name, j // 2] = r = acp(pa(dst[:, j:j + 2, :]), b[:], t, *[u() for u in w])
                return r
            return f

        rtmp = relu[0:32, :].rearrange("p (n t) -> p n t", n=2)

        def ev_rope(name, dst, base, *w):
            def f(xp, b, c, t):
                j = (c - base) // 128
                r = acp(pa(dst[:, j:j + 2, :]), b[:], t, *[u() for u in w])
                done["r" + name, j // 2] = done["rtmp"] = rotate(dst[0:32, j:j + 2, :], 2, 0, rtmp, SW16, r, done["maskb"],
                                                               done.get("rtmp"))
                return r
            return f

        def ev_tm(name, dst, base, *w):
            def f(xp, b, c, t):
                j = c - base
                done[name, j // 256] = r = acp(dst[:, :, j:j + 256], b[:].rearrange("p (a n) -> p a n", a=2), t, *[u() for u in w])
                return r
            return f

        def ev_z(xp, b, c, t):
            j = (c - 3072) // 128
            z = zt[(j // 2) % 2]
            t = af(pa(z[:]), b[:], AF.Silu, t, done["dn", 1], done.get(("z", j // 2 - 2)))
            o_ = pa(odn[:, j:j + 2, :])
            done["z", j // 2] = r = tt(o_, o_, pa(z[:]), OP.mult, t, done["dn", 0], done["dn", 1])
            split2(DN, j, o_, r)
            return t

        def split2(part, j, src, *w):
            hi, lo = pa(part.hi[:, j:j + 2, :]), pa(part.lo[:, j:j + 2, :])
            th = acp(hi, src, *w)
            tl = tt(lo, src, hi.bitcast(F32), OP.subtract, th, *w)
            part.tok[j] = part.tok[j + 1] = [th, tl]

        def ev_gl(br):
            def f(xp, b, c, t):
                j = (c - 8792 - 1024 * br) // 128
                for a in range(2):
                    k = 24 * l + 8 * br + j + a
                    r = af(gate[:, (j + a) % 4, :], b[:, 256 * a:256 * a + 256], AF.Tanh, t, done.get(("gm", j % 4)), done["maskb"],
                           P.hb_tok, bias=hb[:, k:k + 1], scale=0.5)
                done["g", j % 4] = r
                return r
            return f

        def ev_br(br, first, last):
            def f(xp, b, c, t):
                j = c // 128
                g2, m2 = pa(gate[:, j % 4:j % 4 + 2, :]), pa(mg[:, j:j + 2, :])
                if first:
                    done["gm", j % 4] = done["m", j] = r = stt(m2, g2, 1.0, b[:], OP.add, OP.mult, t, done["g", j % 4], done["xa"])
                    return r
                r = stt(g2, g2, 1.0, b[:], OP.add, OP.mult, t, done["g", j % 4])
                done["gm", j % 4] = done["m", j] = t = tt(m2, m2, g2, OP.add, r, done["m", j])
                if last:
                    split2(MG, j, m2, t)
                return r
            return f

        def branch(br, part, first, last):
            for i in range(2):
                P.units((f"gl{br}", l, i), w_in, 8792 + 1024 * br + 512 * i, [H], False, ev_gl(br))
                P.units((f"wb{br}", l, i), A["w_branch_2"][l, br], 512 * i, [part], False, ev_br(br, first, last))

        def split_o(part, o_, key):
            def f():
                for j in range(0, KT, 2):
                    split2(part, j, pa(o_[:, j:j + 2, :]), done[key])
            return f

        if l == 0:
            for k in range(0, KT, 2):
                square(k, 2, xt)
        P.call(lambda: norm("norm_mix_2", 8 * l, split_h))
        P.lanes[:] = [[strengths(), delta(0), delta(1)], [attend()]]
        P.source(("sm", l), wsm[:], wsm_lo[:], l_sm, 8, narrow)
        P.units(("iq", l), w_in, 7184, [H], False, ev_copy("iq", iq, 7184))
        conv = lambda g: [P.units((n, l, g), w_in, o_ + 512 * g, [H], False, conv_in(kind, g))
                          for kind, o_, n in ((1, 1024, "dk"), (0, 0, "dq"), (2, 2048, "dv"))]
        conv(0)
        for i in range(2):
            P.units(("xq", l, i), w_in, 7768 + 512 * i, [H], False, ev_copy("xq", xq, 7768))
        conv(1)
        P.until(done, "xa")
        P.call(split_o(XA, xq, "xa"))
        branch(2, XA, True, False)
        P.until(done, ("dn", 0))
        for i in range(2):
            P.units(("sv", l, i), w_in, 6160 + 512 * i, [H], True, ev_tm("sv_", sv_, 6160))
        for i in range(2):
            P.units(("sq", l, i), w_in, 4112 + 512 * i, [H], False, ev_rope("q", sq_, 4112))
            P.units(("sk", l, i), w_in, 5136 + 512 * i, [H], False, ev_rope("k", sk_, 5136, lambda: [done["dn", 0]]))
        P.until(done, ("dn", 1))
        P.units(("dz", l, 0), w_in, 3072, [H], False, ev_z)
        P.units(("dz", l, 1), w_in, 3584, [H], False, ev_z)
        branch(0, DN, False, False)
        P.until(done, "sa")
        P.call(split_o(SA, sq_, "sa"))
        branch(1, SA, False, True)

        def ev_o(xp, b, c, t):
            j = c // 128
            x2 = pa(x[:, j:j + 2, :])
            P.x_tok[j] = P.x_tok[j + 1] = r = stt(x2, b[:], 0.5, x2, OP.mult, OP.add, t)
            square(j, 2, r)
            return r
        for i in range(2):
            P.units(("wo", l, i), A["w_out_2"][l], 512 * i, [MG], False, ev_o)

        def next_loads():
            w = [P.x_tok[k] for k in range(KT)]
            P.wsm[1] = small_weights(P, 1, w)
            P.kv_tok = []
            for n in range(16):
                if n in P.kv1_at:
                    i, v = P.kv1_at[n]
                    dst = pa(mk[:, 4 * i + 2 * v:4 * i + 2 * v + 2, :]) if i < 2 else mv[:, v, 512 * (i - 2):512 * (i - 2) + 512]
                    P.kv_tok.append(P.load(dst, A["kv1"][:, 512 * n:512 * n + 512], P.kv1_tok[n], w, q=P.pool))

        P.call(lambda: norm("norm_ffn_2", 8 * l, split_h))
        if l == 0:
            P.call(next_loads)

        def ev_g(i):
            def f(xp, b, c, t):
                j = c // 128 - 4 * i
                done["fg", i, j // 2] = r = af(pa(fg[i % 2][:, j:j + 2, :]), b[:, 0:512], AF.Silu, t, done.get(("fu", i - 2, j // 2)))
                return r
            return f

        def ev_u(i):
            def f(xp, b, c, t):
                j = (c - 2816) // 128 - 4 * i
                n = done.get("nf", 0)
                done["nf"] = n + 1
                a_ = fa[n % 2]
                r = tt(a_[:], b[:, 0:512], pa(fg[i % 2][:, j:j + 2, :]), OP.mult, t, done["fg", i, j // 2], ffa_free[n % 2])
                done["fu", i, j // 2] = r
                k0 = 4 * i + j
                th = acp(pa(FH[:, k0:k0 + 2, :]), a_[:], r)
                tl = tt(pa(FL[:, k0:k0 + 2, :]), a_[:], pa(FH[:, k0:k0 + 2, :]).bitcast(F32), OP.subtract, th)
                ffa_free[n % 2] = [th, tl]
                for a in range(2):
                    ftok[k0 + a] = [th, tl]
                return r
            return f
        ffa_free, ftok = [[], []], {}
        for i in range(5):
            P.units(("fg", l, i), A["w_ffn_in_2"][l], 512 * i, [H], False, ev_g(i))
            P.units(("fu", l, i), A["w_ffn_in_2"][l], 2816 + 512 * i, [H], False, ev_u(i))
        P.want(("fl", l), [P.block(A["w_ffn_in_2"][l], 2560, n=256), P.block(A["w_ffn_in_2"][l], 5376, n=256, o=2048)])
        for u, ev, c0 in ((0, ev_g(5), 2560), (1, ev_u(5), 5376)):
            P.unit_at(("fl", l), 2048 * u, 256, [H], ev, c0, u == 1)
        acc = [B[4 + i] for i in range(4)]

        def ffn_out(k):
            def f(q):
                for j in range(8):
                    bk = acc[j // 2]
                    for w, v, wt in ((q.hi, FH, q.th), (q.hi, FL, q.th), (q.lo, FH, q.tl)):
                        t = mm(bk.t[:, 256 * (j % 2):256 * (j % 2) + 256], w[:, 0, 128 * j:128 * j + 128], v[:, k, :],
                               k == 0 and j % 2 == 0 and v is FH and w is q.hi, k == 21 and w is q.lo, wt, ftok[k],
                               bk.free if k == 0 else None)
                    if k == 21 and j % 2:
                        x2 = pa(x[:, j - 1:j + 1, :])
                        r = tt(x2, x2, bk.t[:], OP.add, t)
                        bk.free = [r]
                        P.x_tok[j - 1] = P.x_tok[j] = r
                if k == 21:
                    for j in range(0, KT, 2):
                        square(j, 2, [P.x_tok[j], t])
                return t
            return f
        for i in range(6):
            n = 4 if i < 5 else 2
            P.want(("fo", l, i), [P.block(A["w_ffn_out_2"][l], 0, n=1024, k0=4 * i, kt=n)])
            for k in range(n):
                P.quarter(("fo", l, i), 1, lambda s, k=k: s[:, 1024 * k:1024 * k + 1024].unsqueeze(1), k == n - 1,
                          ffn_out(4 * i + k))

    P.alog_free, P.maskb_free, P.sm_free = [], [], []
    for l in range(2):
        layer(l)
        P.run(1)
        P.drain()
    fin = []

    def store(k, t):
        if k % 4 == 3:
            fin.append(P.load(out[:, k - 3:k + 1, :], x[:, k - 3:k + 1, :], t))
    norm("norm_final_2", 0, store)
    return fin


def build(nc, A, out, stop=None):
    with ExitStack() as ctx:
        A = dict(A, kv1=nc.dram_tensor("kv1", (128, 4096), F32, kind="Internal").ap())
        P = Program(nc, A, ctx)
        phase_a(P)
        P.run(2)
        phase_b(P)
        P.run(2)
        P.drain()
        P.finish(phase_c(P, out), list(P.kv1_tok.values()))


def fm(a):
    return np.ascontiguousarray(a.T.reshape(-1, 128, a.shape[0]).transpose(1, 0, 2))


def layout(inp):
    g = {k: np.asarray(v) for k, v in inp.items()}
    d = {"xT": fm(g["x"][0]), "ctxT": fm(g["ctx"][0]), "cst": constants()}
    d["cols"] = np.ascontiguousarray(np.concatenate([g[n].reshape(-1, 128).T for n, _ in COLS], axis=1))
    d["w_mod"], d["w_in"] = g["w_mod"][0], g["w_in"][0]
    d["w_lr"] = np.ascontiguousarray(g["w_in"][0][:, 5120:5152].reshape(8, 128, 32).transpose(1, 0, 2))
    d["w_gate2"] = g["w_gate2"][0]
    d["sgu_wT"] = np.ascontiguousarray(g["sgu_w"][0].transpose(2, 0, 1))
    d["sgu_b"], d["sgu_ln_g"], d["sgu_ln_b"] = g["sgu_b"][0], g["sgu_ln_g"][0], g["sgu_ln_b"][0]
    d["memT"] = fm(g["mem_2"][0])
    d["w_mem_kv"], d["w_router"] = g["w_mem_kv_2"], np.ascontiguousarray(g["w_router"].reshape(8, 128, 16).transpose(1, 0, 2))
    d["b_router"] = g["b_router"].reshape(16, 1)
    d["w_eg"], d["w_eu"], d["w_ed"] = g["w_exp_gate"][0], g["w_exp_up"][0], g["w_exp_down"][0]
    d["cstc"] = constants_c()
    d["positions"] = g["positions_2"][0]
    d["w_in_2"] = w = g["w_in_2"]
    pk = lambda a: np.ascontiguousarray(a.reshape(8, 128, -1).transpose(1, 0, 2))
    d["w_small"] = np.stack([np.concatenate([pk(w[i][:, c:c + n]) for c, n in ((7696, 64), (4104, 8), (4096, 8), (7760, 8))], axis=2)
                             for i in range(2)])
    d["a_log"], d["dt_bias"] = g["a_log_2"].reshape(2, 8, 1), g["dt_bias_2"].reshape(2, 8, 1)
    d["w_branch_2"], d["w_out_2"] = g["w_branch_2"], g["w_out_2"]
    d["w_ffn_in_2"], d["w_ffn_out_2"] = g["w_ffn_in_2"], g["w_ffn_out_2"]
    d["w_a"], d["w_b"], d["w_o"] = g["w_branch_a"][0], g["w_branch_b"][0], g["w_out"][0]
    return d


def kernel(**inputs):
    import concourse.bacc as _bacc
    from concourse.bass_utils import run_bass_kernel_spmd as _run

    nc = _bacc.Bacc("TRN2", target_bir_lowering=False, num_devices=1)
    arrays, aps = {}, {}
    for name, a in layout(inputs).items():
        arrays[f"in_{name}_dram"] = a = np.ascontiguousarray(a)
        aps[name] = nc.dram_tensor(f"in_{name}_dram", a.shape, mybir.dt.from_np(a.dtype), kind="ExternalInput").ap()
    out = nc.dram_tensor("out_0_dram", (128, KT, T), F32, kind="ExternalOutput").ap()
    build(nc, aps, out)
    r = _run(nc, [arrays], core_ids=[0])
    o = r.results[0]["out_0_dram"]
    return np.ascontiguousarray(o.transpose(2, 1, 0)).reshape(1, T, 1024)
```

```python
import numpy as np
import concourse.bass as bass
from concourse import mybir
from contextlib import ExitStack

F32 = mybir.dt.float32
F32R = mybir.dt.float32r
I32 = mybir.dt.int32
AF = mybir.ActivationFunctionType
OP = mybir.AluOpType
AX = mybir.AxisListType

ACT_SETS = [{AF.Exp, AF.Tanh}, {AF.Tanh, AF.Sigmoid}, {AF.Tanh, AF.Silu, AF.Sin}, {AF.Tanh, AF.Gelu_apprx_tanh}, {AF.Ln}, {AF.Sqrt}]
ANY_SET = {AF.Copy, AF.Identity, AF.Square, AF.Abs, AF.Relu}

T = 256
KT = 8
BASE = 16512

COLS = [("c", 8), ("c_ctx", 8), ("b_mod", 48), ("g_norm1", 8), ("g_norm2", 8), ("b_gate2", 8),
        ("gla_norm_g", 8), ("sgu_ln_g", 8), ("sgu_ln_b", 8), ("b_branch", 16), ("g_final", 8),
        ("norm_mix_2", 16), ("norm_mem_2", 16), ("b_gate_2", 48), ("conv_w_2", 192), ("dn_norm_2", 2),
        ("norm_ffn_2", 16), ("norm_final_2", 8)]
COL = {}
for _n, _c in COLS:
    COL[_n] = sum(c for _, c in COLS[:len(COL)])
NCOL = sum(c for _, c in COLS)

MASKS = ["one", "eye", "le", "ge"]


def constants():
    p, f = np.meshgrid(np.arange(128), np.arange(128), indexing="ij")
    m = {"one": p >= 0, "eye": p == f, "le": p <= f, "ge": p >= f}
    small = np.zeros((128, 128), np.float32)
    small[:, 0] = 1e-6
    small[:, 1] = np.pi / 2
    small[:, 2] = 1e-12
    small[:, 16:32] = np.tri(4, k=-1).ravel()
    small[:, 32:36] = 4.0 - np.arange(4)
    small[:, 36:40] = 64.0 * np.arange(4)
    small[:, 40:56] = np.tri(4, k=-1).T.ravel()
    small[:, 64:128] = 1.0 + np.arange(64)
    return np.concatenate([m[n].astype(np.float32) for n in MASKS] + [small], axis=1)


class Tok:

    def __init__(self, sem=None, count=0):
        self.sem, self.count, self.used, self.at = sem, count, False, 0


def flat(waits):
    for w in waits:
        if isinstance(w, Tok):
            yield w
        elif w is not None:
            yield from flat(w)


def latest(waits):
    return max((w.at for w in flat([waits])), default=0)


class Stream:

    def __init__(self, sem, hop):
        self.sem, self.hop, self.q, self.at = sem, hop, [], 0

    def do(self, fn, *waits, tok=None, ns=100):
        t, ws = tok or Tok(), list(flat(waits))
        for w in ws:
            w.used = True
        self.q.append((fn, ws, t))
        t.at = self.at = max(self.at, latest(ws) + self.hop) + ns
        self.last = t
        return t

    def count(self):
        n = 0
        for _, _, t in self.q:
            if t.used and t.sem is None:
                n += 1
                t.sem, t.count = self.sem, n

    def emit(self, e):
        seen = {}
        for fn, ws, t in self.q:
            for w in ws:
                if seen.get(w.sem.name, 0) < w.count:
                    e.wait_ge(w.sem, w.count)
                    seen[w.sem.name] = w.count
            i = fn(e)
            if t.sem is self.sem:
                i.then_inc(self.sem, 1)


class Bank:

    def __init__(self, t):
        self.t, self.free = t, []


class Part:

    def __init__(self, hi, lo):
        self.hi, self.lo, self.tok = hi, lo, {}


class Slot:

    def __init__(self, t, r, sem, i, once=False):
        self.t, self.r, self.sem, self.n, self.i, self.once = t, r, sem, 0, i, once


class Quarter:

    def __init__(self, hi, lo, th, tl, b):
        self.hi, self.lo, self.th, self.tl, self.b = hi, lo, th, tl, b


class Lane:

    def __init__(self, *parts):
        self.parts, self.pending = list(parts), None

    def step(self):
        while self.parts:
            self.pending = next(self.parts[0], "end")
            if self.pending != "end":
                return
            self.parts.pop(0)

    def due(self):
        if callable(self.pending):
            return 0 if self.pending() else None
        return latest(self.pending)


class Program:
    NB = 6
    MOST = 5
    often = 4
    crowd = 8000
    SLOT = 2048

    def __init__(self, nc, A, ctx):
        self.nc, self.A, self.ctx = nc, A, ctx
        self.pe, self.act, self.dve, self.pool, self.sp = (
            Stream(self.sem("done_" + n), hop) for n, hop in (("pe", 240), ("act", 160), ("dve", 160), ("pool", 160), ("sp", 160)))
        self.nload, self.bus, self.sets = 0, 0, []
        ctx.enter_context(nc.sbuf_tensor("arena", [128, 53200], F32))
        self.banks = [Bank(ctx.enter_context(nc.psum_tensor(f"bank{i}", [128, 512], F32))) for i in range(8)]

        self.pf = self.at("pf", 0, [NCOL])
        self.cst = self.at("cst", 448, [128 * (len(MASKS) + 1)])
        self.x = self.at("x", 1536, [KT, T])
        self.small = self.at("small", 3584, [512])
        hl = 4096
        self.hib = [self.at(f"hib{i}", hl + 1024 * i, [1024], F32R) for i in range(self.NB)]
        self.R0 = hl + 1024 * self.NB
        self.Z = self.R0 + 6 * self.SLOT
        self.mask = {n: self.cst[:, 128 * i:128 * i + 128] for i, n in enumerate(MASKS)}
        self.ONE, self.EYE = self.mask["one"], self.mask["eye"]
        self.sm = self.cst[:, 128 * len(MASKS):128 * len(MASKS) + 128]
        self.EPS = self.sm[:, 0:1]

        self.early, self.want_, self.held, self.idle = [], [], {}, []
        self.todo, self.nq, self.ahead, self.most, self.rot = [], 0, 0, self.MOST, 0
        self.pe_read = [[] for _ in range(self.NB)]
        self.lanes = []

    def sem(self, n):
        return self.ctx.enter_context(self.nc.semaphore(n))

    def at(self, name, off, shape, dt=F32):
        return self.nc.alloc_sbuf_tensor_at(name, [128] + shape, dt, offset=BASE + 4 * off)

    def col(self, n, i=0, k=1):
        return self.pf[:, COL[n] + i:COL[n] + i + k]

    def mm(self, out, l, r, start, stop, *w, beside=1):
        k = 1 if l.dtype == F32R else 4
        return self.pe.do(lambda e: e.matmul(out, l, r, start=start, stop=stop, skip_group_check=True), *w,
                          ns=max(k * r.free_size(), (k + 1) // 2 * l.free_size()) / 2.4 / beside)

    def tp(self, out, i, *w):
        k = i.shape[0]
        return self.pe.do(lambda e: e.transpose(out, i, self.EYE[0:k, 0:k]), *w, ns=k)

    def af(self, out, i, func, *w, bias=0.0, scale=1.0, accum=None):
        ns = 93 * (1 + (not isinstance(scale, float)) + (not isinstance(bias, float))) + 0.83 * i.free_size()
        if func not in ANY_SET:
            if not any(func in s for s in self.sets):
                self.sets, ns = [s for s in ACT_SETS if func in s], ns + 1283
            self.sets = [s for s in self.sets if func in s]
        return self.act.do(lambda e: e.activation(out, i, func, bias=bias, scale=scale, accum_out=accum), *w, ns=ns)

    def acp(self, out, i, *w):
        return self.act.do(lambda e: e.copy(out, i), *w, ns=80 + 0.83 * i.free_size())

    def tt(self, out, a, b, op, *w, on=None):
        s = on or self.dve
        return s.do(lambda e: e.tensor_tensor(out, a, b, op), *w, ns=70 + 1.04 * out.free_size() * (1 if s is self.dve else 2))

    def ts(self, out, a, s1, s2, o1, o2, *w, on=None):
        s = on or self.dve
        if s2 is None:
            return s.do(lambda e: e.tensor_scalar(out, a, s1, None, o1), *w, ns=130 + 0.8 * out.free_size())
        return s.do(lambda e: e.tensor_scalar(out, a, s1, s2, o1, o2), *w, ns=130 + 0.8 * out.free_size())

    def stt(self, out, a, s, b, o1, o2, *w, rev1=False):
        return self.dve.do(lambda e: e.scalar_tensor_tensor(
            out=out, in0=a, scalar=s, in1=b, op0=o1, op1=o2, reverse1=rev1), *w, ns=130 + 1.04 * out.free_size())

    def cp(self, out, i, *w, on=None):
        return (on or self.dve).do(lambda e: e.tensor_copy(out, i), *w, ns=70 + 0.52 * out.free_size())

    def rcp(self, out, i, *w):
        return self.dve.do(lambda e: e.reciprocal(out, i), *w, ns=70 + 6.3 * out.free_size())

    def red(self, out, i, op, *w):
        return self.dve.do(lambda e: e.tensor_reduce(out, i, AX.X, op), *w, ns=70 + 1.04 * i.free_size())

    def fill(self, out, v, *w, on=None):
        return (on or self.dve).do(lambda e: e.memset(out, v), *w)

    def raw(self, stream, fn, *w):
        stream.do(fn, *w)

    def dma(self, q, out, src, sem, count, *w):
        t = q.do(lambda e: e.dma_start(out, src).then_inc(sem, 16), *w, tok=Tok(sem, count), ns=60)
        t.at = self.bus = max(self.bus, t.at + 1500) + out.free_size() * out.shape[0] * 4 / 360
        return t

    def load(self, out, src, *w, q=None):
        self.nload += 1
        return self.dma(q or self.sp, out, src, self.sem(f"load{self.nload}"), 16, *w)

    def add_slot(self, i, off, *free, n=2, h=0, once=False):
        for h in range(h, h + n):
            name, o = f"slot{2 * i + h}", off + self.SLOT * h
            s = Slot(self.at(name, o, [self.SLOT]), self.at(name + "r", o, [self.SLOT], F32R), self.sem(name), i, once)
            self.idle.append((s, list(flat(free))))
        self.pump()

    def pump(self):
        for q, low in ((self.want_, 0), (self.early, 3)):
            while q:
                key, parts, zone = q[0]
                fit = [(latest(free), j) for j, (s, free) in enumerate(self.idle) if low <= s.i < zone]
                if not fit:
                    break
                s, free = self.idle.pop(min(fit)[1])
                q.pop(0)
                for view, src in parts:
                    s.n += 16
                    t = self.dma(self.sp, view(s.t), src, s.sem, s.n, free)
                self.held[key] = (s, t)

    def want(self, key, parts, zone=3, early=False):
        (self.early if early else self.want_).append((key, parts, zone))
        self.pump()

    def release(self, key, *read):
        s, _ = self.held.pop(key)
        if not s.once:
            self.idle.append((s, list(flat(read))))
        self.pump()

    @staticmethod
    def block(w, c0, n=512, k0=0, kt=8, o=0):
        return (lambda t: t[:, o:o + kt * n].rearrange("p (k n) -> p k n", k=kt),
                w[128 * k0:128 * (k0 + kt), c0:c0 + n].rearrange("(k p) n -> p k n", p=128))

    def split_w(self, src, lo, k, ld):
        b = self.nq % self.NB
        self.nq += 1
        n = src.shape[-1]
        hi = self.hib[b][:].rearrange("p (k n) -> p k n", k=k)[:, :, 0:n]
        th = self.acp(hi, src, ld, self.pe_read[b])
        tl = self.tt(lo, src, hi.bitcast(F32), OP.subtract, ld, th)
        return Quarter(hi, lo, th, tl, b)

    def split_x(self, part, k, src, *w):
        th = self.acp(part.hi[:, k, :], src, *w)
        tl = self.tt(part.lo[:, k, :], src, part.hi[:, k, :].bitcast(F32), OP.subtract, th, *w)
        part.tok[k] = [th, tl]

    def staggered(self, part, src, scaled, *w):
        th = {}
        for k in range(KT + 1):
            if k < KT:
                t = scaled(k)
                th[k] = [t, self.acp(part.hi[:, k, :], src[:, k, :], t, *w)]
            if k:
                t, h = th[k - 1]
                part.tok[k - 1] = [h, self.tt(part.lo[:, k - 1, :], src[:, k - 1, :], part.hi[:, k - 1, :].bitcast(F32), OP.subtract,
                                         t, h, *w)]

    def bank(self):
        self.rot += 1
        return self.banks[self.rot % 3]

    def plain(self, key, fn):
        self.todo.append(("plain", key, fn))

    def call(self, fn, back=0):
        self.todo.insert(len(self.todo) - back, ("call", fn))

    def source(self, key, src, lo, ld, k, fn):
        self.held[key] = (Slot(src, lo, None, None), ld)
        self.todo.append(["quarter", key, k, lambda s: s, False, fn, None])

    def ready(self, q, fn):
        self.todo.append(("call", lambda: fn(q())))

    def quarter(self, key, k, view, last, fn):
        self.todo.append(["quarter", key, k, view, last, fn, None])

    def step(self):
        for t in self.todo:
            if self.ahead >= self.most:
                break
            if t[0] != "quarter" or t[6] is not None:
                continue
            if t[1] not in self.held:
                break
            s, ld = self.held[t[1]]
            if self.ahead and latest([ld]) > self.act.at:
                break
            t[6] = self.split_w(t[3](s.t), t[3](s.r), t[2], ld)
            self.ahead += 1
        t = self.todo.pop(0)
        if t[0] == "call":
            t[1]()
        elif t[0] == "plain":
            s, ld = self.held[t[1]]
            self.release(t[1], t[2](s.t, ld))
        else:
            self.ahead, self.most = self.ahead - 1, min(self.MOST, self.most + 2)
            self.pe_read[t[6].b] = [t[5](t[6])]
            if t[4]:
                self.release(t[1], self.pe_read[t[6].b])

    def unit(self, key, xs, tm, evac):
        st = {}

        def part(h):
            def f(q):
                if h == 0:
                    st["b"] = [self.bank() for _ in xs]
                t = None
                for xp, bk in zip(xs, st["b"]):
                    first = h == 0
                    for g in range(2):
                        gs = slice(128 * g, 128 * g + 128)
                        for k in range(4):
                            kk = 4 * h + k
                            for w, v, wt in ((q.hi, xp.hi, q.th), (q.hi, xp.lo, q.th), (q.lo, xp.hi, q.tl)):
                                l, r = (v[:, kk, gs], w[:, k, :]) if tm else (w[:, k, gs], v[:, kk, :])
                                t = self.mm(bk.t[:, 256 * g:256 * g + 256], l, r, first,
                                            h == 1 and k == 3, wt, xp.tok[kk], bk.free if first else None)
                                first = False
                            if k % self.often == self.often - 1 and (k < 3 or g == 0):
                                self.side_step(self.pe.at)
                    if h == 1:
                        bk.free = list(flat([evac(xp, bk.t, t)]))
                return t
            return f

        for h in range(2):
            self.quarter(key, 4, lambda s, h=h: s[:].rearrange("p (k n) -> p k n", k=8)[:, 4 * h:4 * h + 4, :], h == 1, part(h))

    def mixed(self, *loads, load=True):
        for u in range(2):
            for key, w, c0, xs, tm, evac in loads:
                if load:
                    self.columns((key, u), w, c0 + 256 * u)
                self.unit((key, u), xs, tm, lambda xp, b, t, c=c0 + 256 * u, evac=evac: evac(xp, b, c, t))

    def units(self, *load):
        self.mixed(load)

    def columns(self, key, w, c0, zone=3):
        self.want(key, [self.block(w, c0, 256)], zone)

    def later(self, toks, fn):
        def f():
            yield toks
            fn()
        lane = Lane(f())
        lane.step()
        self.lanes.insert(0, lane)

        def now():
            if lane.parts:
                lane.step()
        return now

    def side_step(self, now=None):
        self.lanes = [l for l in self.lanes if l.parts]
        ready = sorted((l for l in self.lanes if l.due() is not None), key=lambda l: l.due())
        if now is not None and max(self.act.at, self.dve.at) > now + self.crowd:
            return True
        for lane in ready[:1] if now is None else [l for l in self.lanes if l in ready and l.due() <= now]:
            lane.step()
        return bool(ready)

    def run(self, ratio=1):
        while self.todo:
            self.step()
            for _ in range(ratio):
                self.side_step(self.pe.at)

    @staticmethod
    def need(done, *keys):
        ready = lambda: all(k in done for k in keys)
        if not ready():
            yield ready

    def until(self, done, *keys):
        def f():
            while any(k not in done for k in keys):
                assert self.side_step(), keys
        self.call(f)

    def drain(self):
        while self.side_step():
            pass

    def finish(self, *last):
        self.sp.do(lambda e: e.nop(), *last)
        streams = dict(sync=self.sp, tensor=self.pe, scalar=self.act, vector=self.dve, gpsimd=self.pool)
        for s in streams.values():
            s.count()
        with self.nc.Block() as block:
            block.sync(lambda e: self.sp.emit(e))
            block.tensor(lambda e: self.pe.emit(e))
            block.scalar(lambda e: self.act.emit(e))
            block.vector(lambda e: self.dve.emit(e))
            block.gpsimd(lambda e: self.pool.emit(e))


def bc(a, n, axis):
    a = a.unsqueeze(axis)
    s = list(a.shape)
    s[axis] = n
    return a.to_broadcast(s)


def phase_a(P):
    A, Z = P.A, P.Z
    mm, tp, af, acp, tt, ts, stt, cp, rcp, fill = P.mm, P.tp, P.af, P.acp, P.tt, P.ts, P.stt, P.cp, P.rcp, P.fill
    col, ONE, EPS, x = P.col, P.ONE, P.EPS, P.x
    LE, GE = P.mask["le"], P.mask["ge"]
    B = P.banks

    off = [Z]

    def new(name, shape, dt=F32):
        n = int(np.prod(shape))
        off[0] += n
        assert off[0] <= 53200, name
        return P.at(name, off[0] - n, shape, dt), off[0] - n

    hx_hi = new("hx_hi", [KT, T], F32R)[0]
    hx = Part(hx_hi, new("hx_lo", [KT, T], F32R)[0])
    hc_hi, HC = new("hc_hi", [KT, T], F32R)
    hc = Part(hc_hi, new("hc_lo", [KT, T], F32R)[0])
    ctx, CX = new("ctx", [KT, T])
    kx, QK = new("kx", [4, T])
    qx = new("qx", [4, T])[0]
    vx, VX = new("vx", [2, 1024])
    kc = new("kc", [4, T])[0]
    vc, VC = new("vc", [2, 1024])
    la, LA = new("la", [2, 4, T])
    lc, LC = new("lc", [2, 4, T])
    zv, ZV = new("zv", [8, 2, 128])
    u, UU = new("u", [KT, T])
    wg2, GL = new("wg2", [512])
    wlr, WLR = new("wlr", [KT, 128])
    wlr_lo = P.at("wlr_lo", WLR, [KT, 128], F32R)
    lr, LR = new("lr", [2, T])
    gl1 = new("gl1", [8, T])[0]
    gls = [P.at("gl0", GL, [8, T]), gl1]
    cs = new("cs", [KT, 32])[0]
    md0 = new("md0", [16, 32])[0]
    mod = P.small[:, 0:64]
    sqx, nx = P.at("sqx", UU, [KT, T]), P.at("nx", UU, [KT, T])
    sqc, ncx = P.at("sqc", ZV, [KT, T]), P.at("ncx", ZV, [KT, T])
    rsx, rsc = P.at("rsx", LR, [T]), P.at("rsc", LR + T, [T])
    gates = P.at("gates", HC, [16, T])
    bb, rr = P.at("bb", CX, [2, 4, T]), P.at("rr", CX, [KT, T])
    gtmp = P.at("gtmp", UU, [2, 4, T])
    mix = P.small[:, 256:512]
    sguw, sgub = P.at("sguw", LA, [8, 128]), P.at("sgub", LA + 1024, [8, 128])
    sgu = Part(P.at("sgu_hi", ZV, [KT, T], F32R), P.at("sgu_lo", UU, [KT, T], F32R))
    o = P.at("o", VC, [4, 2, T])
    ob = Part(P.at("ob_hi", VX, [KT, T], F32R), P.at("ob_lo", VC, [KT, T], F32R))
    m = P.at("m", LC, [KT, T])
    mp = Part(P.at("m_hi", QK, [KT, T], F32R), P.at("m_lo", LC, [KT, T], F32R))

    l_pf = P.load(P.pf[:], A["cols"])
    l_cst = P.load(P.cst[:], A["cst"])
    w_mod = lambda g, k: [(lambda t: t[:], A["w_mod"][128 * k:128 * k + 128, 2048 * g:2048 * g + 2048])]
    P.most = 0
    P.add_slot(21, QK)
    P.add_slot(22, HC)
    for i in range(3):
        P.add_slot(i, P.R0 + 2 * P.SLOT * i)
    l_x = P.load(x[:], A["xT"])
    for k in range(KT):
        P.want(("mod", 0, k), w_mod(0, k), 30)
    for u_ in range(2):
        P.columns(("q", u_), A["w_in"], 2048 + 256 * u_, 30)
    l_ctx = P.load(ctx[:], A["ctxT"])
    f_lr = fill(wlr[:], 0.0, on=P.pool)
    f_g2 = fill(wg2[0:64, :], 0.0, on=P.pool)
    f_cs = fill(cs[:], 0.0, on=P.pool)
    l_lr = [P.load(wlr[:, :, 32 * d:32 * d + 16], A["w_lr"][:, :, 16 * d:16 * d + 16], f_lr) for d in range(2)]
    l_g2 = [P.load(wg2[32 * d:32 * d + 16, :], A["w_gate2"][d], f_g2) for d in range(2)]

    c0 = af(cs[:, :, 0], col("c", 0, 8), AF.Silu, l_pf, f_cs)
    c1 = af(cs[:, :, 1], col("c_ctx", 0, 8), AF.Silu, l_pf, f_cs)
    bank_mod = B[3]

    def mod_part(g, k):
        def f(s, ld):
            w = s[:].rearrange("p (t j n) -> p t j n", t=16, j=4)
            for j in range(4):
                t = mm(bank_mod.t[32 * j:32 * j + 32, :].rearrange("p (t n) -> p t n", t=16), cs[:, k, :], w[:, :, j, :], k == 0, k == 7,
                       ld, c1, c0, bank_mod.free if k == 0 else None, beside=4)
            mods[g] = t
            return t
        return f

    def mod_done(g, *w):
        t = P.dve.do(lambda e: e.transpose(md0[:].rearrange("p t n -> p (t n)"), bank_mod.t[:, :]), mods[g], *w)
        bank_mod.free = [t]
        return t

    mods = {}
    done, modcol = {}, {}
    P.sc2 = P.small[:, 40:56].rearrange("p (a k) -> p a k", a=2)
    hbr = P.small[:, 68:84]
    t_hbr = ts(hbr, col("b_branch", 0, 16), 0.5, None, OP.mult, None, l_pf)

    norms = {}

    def norm_in(r):
        src, sq, rs, n, bank, ld = ((x, sqx, rsx, nx, B[4], l_x), (ctx, sqc, rsc, ncx, B[5], l_ctx))[r]
        t = af(sq[:], src[:], AF.Square, ld)
        yield
        for k in range(KT):
            t2 = mm(bank.t[:, 0:T], ONE, sq[:, k, :], k == 0, k == KT - 1, t, l_cst, bank.free)
        t = af(rs[:], bank.t[:, 0:T], AF.Sqrt, t2, bias=EPS, scale=1.0 / 1024)
        bank.free = [t]
        t = rcp(rs[:], rs[:], t)
        norms[r] = tt(n[:], src[:], bc(rs[:], KT, 1), OP.mult, t)
        yield

    nin = [norm_in(0), norm_in(1)]
    sc = mod.rearrange("p (a k r) -> p a k r", a=4, k=8)[:, 0:2]

    def mod0():
        done["start"] = mods[0]
        t = mod_done(0)
        t1 = tt(sc[:, 1], md0[:, 0:8, 0:2], bc(col("b_mod", 0, 8), 2, 2), OP.add, t)
        t0 = tt(sc[:, 0], md0[:, 8:16, 0:2], bc(col("b_mod", 8, 8), 2, 2), OP.add, t)
        t0 = stt(sc[:, 0], sc[:, 0], 1.0, bc(col("g_norm1", 0, 8), 2, 2), OP.add, OP.mult, t0)
        modcol["1"] = [t0, t1]
        P.most = 2

    def h_in(r):
        src, part = ((nx, hx), (ncx, hc))[r]
        P.staggered(part, src, lambda k: ts(src[:, k, :], src[:, k, :], sc[:, 0, k, r:r + 1], sc[:, 1, k, r:r + 1],
                                      OP.mult, OP.add, norms[r], modcol["1"]), done["start"])

    P.call(lambda: next(nin[0]))
    P.call(lambda: next(nin[0]))
    for k in range(KT):
        P.plain(("mod", 0, k), mod_part(0, k))
    P.call(mod0)
    P.call(lambda: h_in(0))
    P.call(lambda: next(nin[1]))

    w_in = A["w_in"]
    pa = lambda a: a.rearrange("p a t -> p (a t)")

    def ev_k(xp, b, c, t):
        j = (c - 2560) // 128
        done["k", xp is hx, j // 2] = r = acp(pa((kx if xp is hx else kc)[:, j:j + 2, :]), b[:], t, done["start"])
        return r

    def ev_v(xp, b, c, t):
        c -= 3072
        done["v", xp is hx, c // 256] = r = cp((vx if xp is hx else vc)[:, :, c:c + 256],
                                              b[:].rearrange("p (a n) -> p a n", a=2), t, done["start"])
        return r

    def ev_q(xp, b, c, t):
        j = (c - 2048) // 128
        done["q", j // 2] = r = af(pa(qx[:, j:j + 2, :]), b[:], AF.Copy, t, done["start"], scale=128 ** -0.5)
        return r

    def ev_zv(xp, b, c, t):
        j = (c - 1024) // 128
        done["zv", j // 2] = r = af(zv[:, j:j + 2].rearrange("p g a c -> p a g c"), b[:].rearrange("p (a g c) -> p a g c", a=2, g=2),
                                    AF.Gelu_apprx_tanh, t, hc.tok.values())
        return r

    def ev_u(xp, b, c, t):
        done["u", c // 256] = r = af(pa(u[:, c // 128:c // 128 + 2, :]), b[:], AF.Gelu_apprx_tanh, t, done["decay"])
        return r

    def ev_r(xp, b, c, t):
        j = (c - 4096) // 128
        done["r", j // 2] = r = af(pa(rr[:, j:j + 2, :]), b[:], AF.Silu, t, done["gla"])
        return r

    def ev_g(xp, b, c, t):
        j = (c - 5152) // 128
        for a in range(2):
            r = af(gates[:, j + a, :], b[:, 256 * a:256 * a + 256], AF.Tanh, t, t_hbr, bias=hbr[:, j + a:j + a + 1], scale=0.5)
        done["g", j // 2] = r
        return r

    need = lambda *ks: P.need(done, *ks)

    def lr_part(q):
        t = None
        for r, (xp, bk) in enumerate(((hx, P.bank()), (hc, P.bank()))):
            for k in range(KT):
                for w, v, wt in ((q.hi, xp.hi, q.th), (q.hi, xp.lo, q.th), (q.lo, xp.hi, q.tl)):
                    t = mm(bk.t[:, 0:T], w[:, k, :], v[:, k, :], k == 0 and w is q.hi and v is xp.hi,
                           k == KT - 1 and w is q.lo, wt, xp.tok[k], bk.free)
            done["lr", r] = acp(lr[0:64, r, :], bk.t[0:64, 0:T], t, norms.values())
            bk.free = [done["lr", r]]
        return t

    S16 = 1.0 / 16

    def decays(r, dst, w):
        for d in range(2):
            tmp = gtmp[:, d]
            ta, tn = [], []
            for g in range(2):
                bk = B[4 + 2 * d + g]
                for a in range(2):
                    h = 2 * g + a
                    t = mm(bk.t[:, 256 * a:256 * a + 256], wg2[32 * d:32 * d + 32, 128 * h:128 * h + 128],
                           lr[32 * d:32 * d + 32, r, :], a == 0, a == 1, done["lr", r], l_g2, bk.free if a == 0 else None)
                for a in range(2):
                    h = 2 * g + a
                    src = bk.t[:, 256 * a:256 * a + 256]
                    ta.append(af(tmp[:, h, :], src, AF.Abs, t, w, bias=col("b_gate2", 4 * d + h)))
                for a in range(2):
                    h = 2 * g + a
                    src = bk.t[:, 256 * a:256 * a + 256]
                    tn.append(ts(dst[:, d, h, :], src, col("b_gate2", 4 * d + h), 0.0, OP.add, OP.min, ta[-1], w))
                bk.free = [tn[-1]]
            t = af(tmp, tmp, AF.Exp, ta, scale=-1.0)
            t = af(tmp, tmp, AF.Ln, t, bias=ONE[:, 0:1])
            done["la", r, d] = tt(dst[:, d], dst[:, d], tmp, OP.subtract, t, tn)
            yield done["la", r, d]
            w = [w, done["la", r, d]]

    def ctx_state(d, h, i):
        e, kt = gls[0][:, 2 * i, :], gls[0][:, 2 * i + 1, :].rearrange("p (a n) -> p a n", a=2)
        L = lc[:, d, h, :]
        w = done["la", 1, d]
        t = P.dve.do(lambda s: s.tensor_tensor_scan(e, L, L, 0.0, OP.add, OP.bypass), w, gfree[i], ns=340)
        if d == 0:
            t = ts(P.small[:, 64 + i:65 + i], e[:, T - 1:T], S16, None, OP.mult, None, t, gfree[i])
            t = af(e, e, AF.Exp, t, bias=P.small[:, 64 + i:65 + i], scale=-S16)
        else:
            t = tt(e, e, L, OP.subtract, t)
            t = af(e, e, AF.Exp, t, scale=S16)
        t = tt(e, e, kc[:, h, :], OP.mult, t, done["k", False, h // 2])
        bk = B[4 + i % 4]
        yield t, bk.free
        for a in range(2):
            t2 = tp(bk.t[:, 128 * a:128 * a + 128], e[:, 128 * a:128 * a + 128], t, bk.free, l_cst)
        t = acp(kt, bk.t[:, 0:256].rearrange("p (a n) -> p a n", a=2), t2, gfree[i])
        yield t
        for a in range(2):
            t2 = mm(bk.t[:, 256:512], kt[:, a, :], vc[:, a, 256 * h:256 * h + 256], a == 0, a == 1, t, bk.free,
                    done["v", False, h])
        done["s", d, h] = cp(L, bk.t[:, 256:512], t2)
        bk.free = [done["s", d, h]]
        gfree[i] = [done["s", d, h]]

    gfree = [[] for _ in range(4)]
    xfree = [[], []]

    def x_head(h):
        gl, tm_, fr = (gls[h % 2], {}, xfree[h % 2])
        q, k = qx[:, h, :], kx[:, h, :]
        c2 = lambda a: a.rearrange("p (c n) -> p c n", c=2)
        qm, km, qi = ([gl[:, 3 * d + i, :] for d in range(2)] for i in range(3))
        kst = [gl[:, 6, 128 * d:128 * d + 128] for d in range(2)]
        att = gl[:, 7, :]
        wk, wq = done["k", True, h // 2], done["q", h // 2]
        mq, mk, mi, ms = [], [], [], []
        for d in range(2):
            tq, tk = [], []
            for c in range(2):
                b = bb[:, d, h, 128 * c:128 * c + 128]
                cc = slice(128 * c, 128 * c + 128)
                nm, pm = (sc_mid[i][:, d, h, c:c + 1] for i in range(2))
                tq.append(af(qm[d][:, cc], b, AF.Exp, done["bb"], fr, bias=nm, scale=S16))
                tk.append(af(km[d][:, cc], b, AF.Exp, done["bb"], fr, bias=pm, scale=-S16))
            ti = af(qi[d], bb[:, d, h, :], AF.Exp, done["bb"], fr, scale=S16)
            tst = af(kst[d], bb[:, d, h, 128 * d:128 * d + 128], AF.Exp, done["bb"], fr,
                     bias=sc_tot[:, d, h, d:d + 1], scale=-S16)
            yield tst
            mq.append(tt(qm[d], qm[d], q, OP.mult, tq, wq))
            mk.append(tt(km[d], km[d], k, OP.mult, tk, wk))
            ms.append(tt(kst[d], kst[d], k[:, 128 * d:128 * d + 128], OP.mult, tst, wk))
            mi.append(tt(qi[d], qi[d], q, OP.mult, ti, wq))
        b4, b5, b6, b7 = B[4], B[5], B[6], B[7]
        yield mq, mk, ms, b4.free, b5.free
        for d in range(2):
            for c in range(2):
                cc = slice(128 * c, 128 * c + 128)
                t = mm(b4.t[:, 256 * d + 128 * c:256 * d + 128 * c + 128], km[d][:, cc], qm[d][:, cc], d == 0 and c == 0,
                       d == 1 and c == 1, mq[d], mk[d], b4.free)
        for d in range(2):
            t2 = tp(b5.t[:, 128 * d:128 * d + 128], kst[d], ms[d], b5.free)
        t_kt = acp(gl[:, 6, :], b5.t[:, 0:256], t2)
        b5.free = [t_kt]
        t1 = tt(c2(att), b4.t[:, 0:256].rearrange("p (c n) -> p c n", c=2), bc(LE, 2, 1), OP.mult, t, fr)
        t3 = tt(c2(km[0]), b4.t[:, 256:512].rearrange("p (c n) -> p c n", c=2), bc(GE, 2, 1), OP.mult, t)
        t_att = tt(att, att, km[0], OP.add, t1, t3)
        b4.free = [t1, t3]
        yield t_kt, t_att, mi
        for d in range(2):
            t = mm(b5.t[:, 256:512] if d == 0 else b6.t[:, 0:256], kst[d], vx[:, d, 256 * h:256 * h + 256], True, True,
                   t_kt, (b5, b6)[d].free, done["v", True, h])
            S1 = km[1] if d == 0 else qm[1]
            t = stt(S1, lc[:, d, h, :], sc_dec[:, d, h, d:d + 1], b5.t[:, 256:512] if d == 0 else b6.t[:, 0:256],
                    OP.mult, OP.add, t, done["s", d, h], t1, t3)
            (b5 if d == 0 else b6).free = [t, t_kt]
            tm_[d] = t
        yield tm_[0], tm_[1], b7.free
        for j in range(2):
            js = slice(128 * j, 128 * j + 128)
            for c in range(2):
                cc = slice(128 * c, 128 * c + 128)
                out = b7.t[:, 256 * j + 128 * c:256 * j + 128 * c + 128]
                mm(out, vx[:, c, 256 * h + 128 * j:256 * h + 128 * j + 128], att[:, cc], j == 0 and c == 0, False, t_att, b7.free)
                mm(out, lc[:, c, h, js], qi[c][:, cc], False, False, mi[c], done["s", c, h])
                S1 = km[1] if c == 1 else qm[1]
                t = mm(out, S1[:, js], qi[1 - c][:, cc], False, j == 1 and c == 1, mi[1 - c], tm_[0], tm_[1])
        t_o = acp(pa(o[:, h]), b7.t[:], t, done["ctx"])
        sq = [km[0], qm[0]]
        for j in range(2):
            t_s = af(sq[j], b7.t[:, 256 * j:256 * j + 256], AF.Square, t)
        b7.free = [t_s]
        yield t_s
        for j in range(2):
            t = mm(b4.t[:, 0:T], ONE, sq[j], j == 0, j == 1, t_s, b4.free)
        rs = qi[0]
        t = af(rs, b4.t[:, 0:T], AF.Ln, t, bias=EPS, scale=1.0 / 256)
        b4.free = [t]
        t = af(rs, rs, AF.Exp, t, scale=-0.5)
        for j in range(2):
            t = stt(o[:, h, j, :], o[:, h, j, :], col("gla_norm_g", 2 * h + j), rs, OP.mult, OP.mult, t, t_o)
        done["o", h] = t
        xfree[h % 2] = [t]

    sc_mid = [P.small[:, 128 + 16 * i:144 + 16 * i].rearrange("p (d h c) -> p d h c", d=2, h=4) for i in range(2)]
    sc_tot = P.small[:, 160:176].rearrange("p (d h c) -> p d h c", d=2, h=4)
    sc_dec = P.small[:, 176:192].rearrange("p (d h c) -> p d h c", d=2, h=4)

    def gla():
        yield from need(("lr", 1), ("lr", 0))
        yield from decays(1, lc, [hc.tok[KT - 1]])
        yield from decays(0, la, [hc.tok[KT - 1]])
        done["decay"] = [done["la", r, d] for r in range(2) for d in range(2)]
        t = None
        tb = []
        for d in range(2):
            for h in range(4):
                for c in range(2):
                    cc = slice(128 * c, 128 * c + 128)
                    L = la[:, d, h, cc]
                    t = P.dve.do(lambda s, a=bb[:, d, h, cc], L=L: s.tensor_tensor_scan(a, L, L, 0.0, OP.add, OP.bypass),
                                 done["la", 0, d], ns=200)
                    if d == 1:
                        t = ts(P.small[:, 192 + 2 * h + c:193 + 2 * h + c], bb[:, d, h, 128 * c + 127:128 * c + 128], 1.0,
                               None, OP.mult, None, t)
                        t = stt(bb[:, d, h, cc], bb[:, d, h, cc], P.small[:, 192 + 2 * h + c:193 + 2 * h + c], L,
                                OP.subtract, OP.subtract, t, rev1=True)
                    tb.append(t)
                yield
        yield tb
        b5 = bb[:].rearrange("p d h (c n) -> p d h c n", c=2)
        for d in range(2):
            mid, end = (63, 127) if d == 0 else (64, 0)
            ts(sc_mid[0][:, d], b5[:, d, :, :, mid], -S16, None, OP.mult, None, tb)
            ts(sc_mid[1][:, d], b5[:, d, :, :, mid], S16, None, OP.mult, None, tb)
            t = ts(sc_tot[:, d], b5[:, d, :, :, end], S16, None, OP.mult, None, tb)
        done["bb"] = af(sc_dec[:], sc_tot[:], AF.Exp, t)
        yield

    def heads(r):
        yield from need("bb")
        for h in (r, r + 2):
            yield from need(("k", False, h // 2), ("v", False, h))
            gs = [ctx_state(d, h, 2 * (h % 2) + d) for d in range(2)]
            while gs:
                w = [next(g, "end") for g in gs]
                gs = [g for g, t in zip(gs, w) if t != "end"]
                if gs:
                    yield w
        done["ctx", r] = [done["s", d, h] for d in range(2) for h in (r, r + 2)]
        yield from need(("ctx", 1 - r))
        done["ctx"] = [done["ctx", 0], done["ctx", 1]]
        if r == 0:
            xfree[0] = [done["ctx"], gfree]
        for h in (r, r + 2):
            yield from need(("k", True, h // 2), ("q", h // 2), ("v", True, h))
            yield from x_head(h)
        done["gla", r] = [done["o", r], done["o", r + 2]]
        yield from need(("gla", 1 - r))
        done["gla"] = [done["o", h] for h in range(4)]
        for h in (r, r + 2):
            yield from need(("r", h))
            t = tt(pa(o[:, h]), pa(o[:, h]), pa(rr[:, 2 * h:2 * h + 2, :]), OP.mult, done["r", h], done["o", h])
            for j in range(2):
                P.split_x(ob, 2 * h + j, o[:, h, j, :], t, done["gla"])
            yield

    def sgu_side():
        yield from need("bb")
        l_sgu = [P.load(sguw[:], A["sgu_wT"], done["bb"], q=P.pool), P.load(sgub[:], A["sgu_b"].partition_broadcast(128), done["bb"], q=P.pool)]
        yield from need(*[("zv", i) for i in range(4)])
        st = P.small[:, 208:232].rearrange("p (a b s) -> p a b s", a=2, b=2)
        mv = P.small[:, 232:236].rearrange("p (a s) -> p a s", a=2)
        wz = [done["zv", i] for i in range(4)]
        yield wz
        t1 = []
        for a in range(2):
            t = [P.dve.do(lambda e, a=a, b=b: e.bn_stats(st[:, a, b, :], zv[:, 4 * b:4 * b + 4, a, :]), wz, ns=600) for b in range(2)]
            t = P.dve.do(lambda e, a=a: e.bn_aggr(mv[:, a, :], st[:, a].rearrange("p b s -> p (b s)")), t)
            t1.append(t)
            yield t
        t = af(mv[:, :, 1], mv[:, :, 1], AF.Sqrt, t1, bias=EPS)
        yield t
        t = rcp(mv[:, :, 1], mv[:, :, 1], t)
        tz = [ts(zv[:, :, a, :], zv[:, :, a, :], mv[:, a, 0:1], mv[:, a, 1:2], OP.subtract, OP.mult, t) for a in range(2)]
        done["ln"] = tz
        tb = []
        for i in range(2):
            bk = B[4 + i]
            yield l_sgu, bk.free
            t = mm(bk.t[:], ONE, sguw[:, 4 * i:4 * i + 4, :], True, True, l_sgu, bk.free)
            for g in range(4):
                tb.append(stt(sgub[:, 4 * i + g, :], bk.t[:, 128 * g:128 * g + 128], col("sgu_ln_b", 4 * i + g), sgub[:, 4 * i + g, :],
                              OP.mult, OP.add, t, l_sgu))
            bk.free = tb[-1:]
        for i in range(4):
            yield from need(("u", i))
            bk = B[4 + i]
            yield tz, done["u", i], bk.free
            for g in range(2):
                for n in range(2):
                    t = mm(bk.t[:, 256 * g + 128 * n:256 * g + 128 * n + 128], zv[:, 2 * i + g, n, :], sguw[:, 2 * i + g, :],
                           g == 0 and n == 0, g == 1 and n == 1, tz, bk.free)
            r2 = []
            for g in range(2):
                ug = u[:, 2 * i + g, :]
                r = stt(mix.rearrange("p (n t) -> p n t", n=2), bk.t[:, 256 * g:256 * g + 256].rearrange("p (n t) -> p n t", n=2),
                        col("sgu_ln_g", 2 * i + g), bc(sgub[:, 2 * i + g, :], 2, 1), OP.mult, OP.add, t, tb[2 * i + g], done.get("sgu"))
                r2.append(tt(ug, ug, mix, OP.mult, r, done["u", i]))
                done["sgu"] = r2[g]
            bk.free = [r]
            yield r2
            for g in range(2):
                P.split_x(sgu, 2 * i + g, u[:, 2 * i + g, :], r2[g], t)

    P.lanes = [Lane(gla()), Lane(heads(0)), Lane(heads(1)), Lane(sgu_side())]
    P.mixed(("q", w_in, 2048, [hx], False, ev_q), load=False)
    P.call(lambda: next(nin[1]), back=2)
    P.units("zv0", w_in, 1024, [hx], True, ev_zv)
    P.call(lambda: h_in(1), back=4)
    P.source("lr", wlr[:], wlr_lo[:], l_lr, 8, lr_part)
    P.modcol = modcol
    gt1 = P.small[:, 32:40]
    gt2 = P.small[:, 56:64]
    sc2 = P.sc2

    mod_i = iter([(g, k) for g in (1, 2) for k in range(KT)])

    def mod_more(n=1):
        for _ in range(n):
            g, k = next(mod_i)
            P.want(("mod", g, k), w_mod(g, k))
            P.plain(("mod", g, k), mod_part(g, k))
            if k == KT - 1:
                P.call((mod1, mod2)[g - 1])

    def mod1():
        t = mod_done(1, modcol["1"])
        t1 = tt(gt1, md0[:, 0:8, 0], col("b_mod", 16, 8), OP.add, t)
        modcol["gt1"] = ts(gt1, gt1, 0.5, None, OP.mult, None, t1)
        modcol["sh2"] = tt(sc2[:, 1], md0[:, 8:16, 0], col("b_mod", 24, 8), OP.add, t)

    def mod2():
        t = mod_done(2, modcol["gt1"], modcol["sh2"])
        t2 = tt(sc2[:, 0], md0[:, 0:8, 0], col("b_mod", 32, 8), OP.add, t)
        modcol["sc2"] = stt(sc2[:, 0], sc2[:, 0], 1.0, col("g_norm2", 0, 8), OP.add, OP.mult, t2)
        modcol["gt2"] = tt(gt2, md0[:, 8:16, 0], col("b_mod", 40, 8), OP.add, t)

    P.units("k", w_in, 2560, [hx, hc], False, ev_k)
    mod_more(2)
    for i in range(2):
        P.units(f"v{i}", w_in, 3072 + 512 * i, [hx, hc], True, ev_v)
        mod_more()
    P.units("zv1", w_in, 1536, [hx], True, ev_zv)
    mod_more(2)
    P.until(done, "decay")
    for i in range(2):
        P.units(f"u{i}", w_in, 512 * i, [hx], False, ev_u)
        mod_more(2)
    P.call(lambda: router_loads())
    for i in range(4):
        P.units(f"g{i}", w_in, 5152 + 512 * i, [hx], False, ev_g)
        mod_more(1)
    P.until(done, "gla")
    for i in range(2):
        P.units(f"r{i}", w_in, 4096 + 512 * i, [hx], False, ev_r)
        mod_more(1)

    def ev_a(xp, b, c, t):
        j = c // 128
        done["m", j] = r = stt(pa(m[:, j:j + 2, :]), pa(gates[:, j:j + 2, :]), 1.0, b[:], OP.add, OP.mult, t, done["g", j // 2], done["gla"])
        return r

    def ev_b(xp, b, c, t):
        j = c // 128
        gb = pa(gates[:, 8 + j:10 + j, :])
        r = stt(gb, gb, 1.0, b[:], OP.add, OP.mult, t, done["g", 4 + j // 2])
        t = tt(pa(m[:, j:j + 2, :]), pa(m[:, j:j + 2, :]), gb, OP.add, r, done["m", j])
        for a in range(2):
            P.split_x(mp, j + a, m[:, j + a, :], t, done["gla"])
        done["mp"] = t
        return r

    def ev_o(xp, b, c, t):
        j = c // 128
        for a in range(2):
            r = stt(x[:, j + a, :], b[:, 256 * a:256 * a + 256], gt1[:, j + a:j + a + 1], x[:, j + a, :], OP.mult, OP.add, t,
                    modcol["gt1"], norms[0])
            P.x_tok[j + a] = r
        P.sq_tok[j // 2] = af(pa(P.sqx2[:, j:j + 2, :]), pa(x[:, j:j + 2, :]), AF.Square, r)
        for a in range(2):
            P.u_tok[j + a] = ts(P.u2[:, j + a, :], x[:, j + a, :], sc2[:, 0, j + a:j + a + 1], None, OP.mult, None, r, modcol["sc2"])
        return r

    P.x_tok, P.sq_tok, P.u_tok = {}, {}, {}
    P.u2, P.sqx2 = P.at("u2", Z + 8192, [KT, T]), P.at("sqx2", Z + 16384, [KT, T])
    wr, brow = P.at("wr", 1344, [KT, 16]), P.at("brow", 1472, [16])
    P.crow = P.at("crow", 1488, [16])
    l_wr = []

    def router_loads():
        l_wr.append(P.load(wr[:], A["w_router"], q=P.pool))
        l_wr.append(P.load(brow[:], A["b_router"].partition_broadcast(128), q=P.pool))

    def router_const():
        for k in range(KT):
            t = mm(B[5].t[:, 0:16], bc(sc2[:, 1, k:k + 1].squeeze(1), 128, 1), wr[:, k, :], k == 0, k == KT - 1, l_wr, modcol["sh2"],
                   B[5].free)
        t = tt(P.crow[:], B[5].t[:, 0:16], brow[:], OP.add, t, l_wr)
        B[5].free = [t]
        P.crow_tok = [t, af(P.small[:, 240:241], EPS, AF.Sqrt, t)]

    def router(p):
        for k in (2 * p, 2 * p + 1):
            for a in range(2):
                w = [P.u_tok[k], P.sq_tok[p], l_wr, B[4].free if k == 0 else None]
                mm(B[4].t[:, 16 * a:16 * a + 16], P.u2[:, k, 128 * a:128 * a + 128], wr[:, k, :], k == 0 and a == 0, k == KT - 1, w)
                t = mm(B[4].t[:, 32 + a:33 + a], P.sqx2[:, k, 128 * a:128 * a + 128], ONE[:, 0:1], False, k == KT - 1)
        P.router_tok = t
    P.router = router

    def slots(n):
        if n == 0:
            P.add_slot(3, Z, done["r", 3])
            P.add_slot(8, Z + 26576, [done["gla"], done["sgu"], modcol.values()])
            expert_loads(P, 0)
        elif n == 1:
            P.add_slot(11, Z + 21888, [done["m", j] for j in range(0, KT, 2)], once=True)
        else:
            P.add_slot(5, Z + 4096, [done["mp"]])
            P.add_slot(7, Z + 10240, [done["mp"]], n=1, h=1)
            P.add_slot(10, Z + 14336, [done["mp"]], n=1, once=True)

    P.call(P.drain)
    P.call(lambda: slots(0))
    for i in range(2):
        P.units(f"wa{i}", A["w_a"], 512 * i, [sgu], False, ev_a)
    P.call(lambda: slots(1))
    for i in range(2):
        P.units(f"wb{i}", A["w_b"], 512 * i, [ob], False, ev_b)
    P.call(lambda: slots(2))
    assert next(mod_i, None) is None
    P.call(router_const)
    for i in range(2):
        P.units(f"wo{i}", A["w_o"], 512 * i, [mp], False, ev_o)
    for p in range(3):
        P.call(lambda p=p: router(p), back=5 - 2 * p)

    P.gt2, P.modcol, P.doneB = gt2, modcol, {}


def zone(e):
    return 11 if e == 0 else 10 if e == 1 else 9 if e < 6 else 8 if e < 11 else 6


def expert_loads(P, e):
    A = P.A
    for n, w, c in (("g0", "w_eg", 0), ("g1", "w_eg", 512), ("u0", "w_eu", 0), ("u1", "w_eu", 512),
                    ("g2", "w_eg", 1024), ("u2", "w_eu", 1024)):
        for h in range(2):
            P.want((n, e, h), [P.block(A[w][e], c, k0=4 * h, kt=4)], 12 if e == 0 and n[1] != "2" else zone(e), e == 0)
    for j in range(3):
        for h in range(2):
            P.want((f"d{j}", e, h), [P.block(A["w_ed"][e], 0, n=1024, k0=4 * j + 2 * h, kt=2)], zone(e), e == 0)


def phase_b(P):
    A, Z = P.A, P.Z
    mm, tp, af, acp, tt, ts, stt, cp, rcp, red = P.mm, P.tp, P.af, P.acp, P.tt, P.ts, P.stt, P.cp, P.rcp, P.red
    col, sm, ONE, EPS, x, B = P.col, P.sm, P.ONE, P.EPS, P.x, P.banks
    LE = P.mask["le"]
    pa = lambda a: a.rearrange("p a t -> p (a t)")

    for s in (P.pe, P.act, P.dve, P.pool, P.sp):
        s.hop = 80
    P.m_free = [P.x_tok[k] for k in range(KT)]
    P.modcol = list(P.modcol.values())
    h2 = P.u2
    h2t = P.at("h2t", 8192, [2, 1024])
    yacc = P.at("yacc", Z + 14336, [KT, T])
    xe = P.at("xe", Z + 16384, [KT, T])
    mem, memg, rsm = P.at("mem", Z + 8192, [KT, T]), P.at("memg", Z + 18432, [KT, T]), P.small[:, 256:512]
    sel = P.at("sel", Z + 20480, [2, 4, 64])
    selw = P.at("selw", Z + 20992, [2, 2, 64])
    selT = [P.at(f"selT{i}", Z + 21248 + 256 * i, [T]) for i in range(2)]
    diff = P.at("diff", Z + 21760, [8, 4, 4])
    hid = [P.at(f"hid{i}", Z + 21888 + 768 * i, [768]) for i in range(2)]
    hidT = [P.at(f"hidT{i}", Z + 23424 + 768 * i, [6, 2, 64]) for i in range(2)]
    y = [P.at(f"y{i}", Z + 24960 + 512 * i, [512]) for i in range(2)]
    rt = P.at("rt", Z + 25984, [512])
    P.mkv = P.at("mkv", Z + Layout2.MK, [4096])
    P.mk = P.mkv[:, 0:2048].rearrange("p (k t) -> p k t", k=KT)
    P.mv = P.mkv[:, 2048:4096].rearrange("p (a n) -> p a n", a=2)
    rs2 = P.small[:, 236:238]
    done = P.doneB

    assert not P.want_
    P.want_, P.early = P.early, []
    P.add_slot(4, 4096, P.pe_read)
    P.add_slot(7, Z + 10240, P.pe_read, n=1)
    P.add_slot(9, Z + 18432, list(P.x_tok.values()), n=1, once=True)

    r_ = lambda o, *s: rt[:, o:o + int(np.prod(s))].rearrange(
        "p (a b) -> p a b", a=s[0]) if len(s) == 2 else rt[:, o:o + s[0]]
    prob, am, wt, posm = (r_(32 * i, 2, 16) for i in range(4))
    beats = rt[:, 128:384].rearrange("p (b i k) -> p b i k", b=8, i=4)
    hi_, lo_ = r_(384, 8, 2), r_(400, 8, 2)
    t1_, t2_, gs_, gsel, gw = (r_(416 + 8 * i, 2, 4) for i in range(5))
    m_ = [r_(456 + 2 * i, 2) for i in range(8)]
    cnt, cnt1 = r_(472, 16), r_(488, 1)
    counts = P.nc.alloc_sbuf_tensor_at("counts", [128, 32], I32, offset=BASE + 4 * (Z + 26496))
    most = {}
    streams = {"act": P.act, "pe": P.pe, "dve": P.dve}
    b16, b4 = lambda a: bc(a, 16, 2), lambda a: bc(a, 4, 2)

    def route():
        P.router(3)
        L = B[4].t
        t = af(rs2, L[:, 32:34], AF.Sqrt, P.router_tok, P.crow_tok, bias=EPS, scale=1.0 / 1024)
        th = af(P.small[:, 240:241], EPS, AF.Exp, P.crow_tok)
        tr = t = rcp(rs2, rs2, t)
        t = [stt(prob[:, a, :], L[:, 16 * a:16 * a + 16], rs2[:, a:a + 1], P.crow[:], OP.mult, OP.add, t, P.crow_tok)
             for a in range(2)]
        B[4].free = t
        t = red(m_[0], prob, OP.max, t)
        t = tt(prob, prob, b16(m_[0]), OP.subtract, t)
        t = af(prob, prob, AF.Exp, t, th)
        for a in range(2):
            for g in range(2):
                bk = B[(3, 7, 0, 1)[2 * a + g]]
                for j in range(4):
                    k = 4 * g + j
                    t3 = tp(bk.t[:, 128 * j:128 * j + 128], h2[:, k, 128 * a:128 * a + 128], P.u_tok[k], bk.free)
                done["h2t", a, g] = af(h2t[:, a, 512 * g:512 * g + 512], bk.t[:], AF.Copy, t3, tr, P.m_free, scale=rs2[:, a:a + 1])
                bk.free = [done["h2t", a, g]]
        P.add_slot(9, Z + 8192 - P.SLOT, [done["h2t", a, g] for a in range(2) for g in range(2)], n=1, h=1, once=True)
        p3 = prob.rearrange("p a (g i) -> p (a g) i", g=4)
        p2 = prob.rearrange("p a (g j i) -> p (a g) j i", g=4, j=2)
        f8 = lambda a: a.rearrange("p a b -> p (a b)")
        four = lambda a: bc(a.rearrange("p (i j) -> p i j", i=4), 8, 1)
        ta = tt(hi_, p2[:, :, :, 0], p2[:, :, :, 1], OP.max, t)
        tb = tt(lo_, p2[:, :, :, 0], p2[:, :, :, 1], OP.min, t)
        tx = tt(diff[:], bc(p3, 4, 2), bc(p3, 4, 3), OP.subtract, t)
        tc = tt(f8(t1_), hi_[:, :, 0], hi_[:, :, 1], OP.max, ta)
        td = tt(f8(t2_), hi_[:, :, 0], hi_[:, :, 1], OP.min, ta)
        te = tt(f8(gs_), lo_[:, :, 0], lo_[:, :, 1], OP.max, tb)
        t1 = stt(beats[:, :, :, 0:4], diff[:], 0.0, four(sm[:, 16:32]), OP.is_ge, OP.mult, tx)
        t = tt(t2_, t2_, gs_, OP.max, td, te)
        t2 = stt(beats[:, :, :, 4:8], diff[:], 0.0, four(sm[:, 40:56]), OP.is_gt, OP.mult, tx)
        t = tt(gs_, t1_, t2_, OP.add, t, tc)
        a3 = am.rearrange("p a (g i) -> p (a g) i", g=4)
        tn = red(a3, beats, OP.add, t1, t2)
        t = red(m_[2], gs_, OP.max, t)
        t = tt(gw, gs_, b4(m_[2]), OP.is_equal, t)
        t = tt(gw, gw, bc(sm[:, 32:36], 2, 1), OP.mult, t)
        t = red(m_[3], gw, OP.max, t)
        t = tt(gsel, gw, b4(m_[3]), OP.is_equal, t)
        ta = stt(a3, a3, 1.5, bc(f8(gsel), 4, 2), OP.is_lt, OP.mult, tn, t)
        t = tt(wt, prob, am, OP.mult, ta)
        t = red(m_[4], wt, OP.add, t)
        t = rcp(m_[5], m_[4], t)
        done["wt"] = tt(wt, wt, b16(m_[5]), OP.mult, t)
        pb, pc = B[5].t, B[6].t
        mm(pb[:, 0:16], LE, am[:, 0, :], True, True, ta, B[5].free)
        mm(pb[:, 16:32], LE, am[:, 1, :], False, False)
        t2 = mm(pb[:, 16:32], ONE, am[:, 0, :], False, True)
        mm(pc[:, 0:16], ONE, am[:, 0, :], True, False, B[6].free)
        t = mm(pc[:, 0:16], ONE, am[:, 1, :], False, True)
        done["pos"] = tt(posm, pb[:, 0:32].rearrange("p (a b) -> p a b", a=2), am, OP.mult, t2)
        B[5].free = [done["pos"]]
        done["counts"] = t

    def count():
        t = cp(cnt, B[6].t[:, 0:16], done["counts"])
        B[6].free = [t]
        tm = red(cnt1, cnt, OP.max, t)
        done["cnt"] = cp(counts[:, 0:17], rt[:, 472:489], t, tm)
        for n in ("act", "pe", "dve"):
            P.raw(streams[n], lambda e, n=n: most.__setitem__(n, e.value_load(counts[0:1, 16:17])), done["cnt"])

    IOTA = sm[:, 64:128]
    xe_read = []

    SH2 = lambda k: P.sc2[:, 1, k:k + 1]

    def gather(q, e0=0, e1=4):
        c0, n = 64 * e0, 64 * (e1 - e0)
        t = [tt(sel[:, a, e0:e1], bc(IOTA, e1 - e0, 1), bc(posm[:, a, 4 * q + e0:4 * q + e1], 64, 2), OP.is_equal, done["pos"],
                done.get("gather")) for a in range(2)]
        for g in range(4):
            bk = B[3 + g % 2]
            for j in range(2):
                k = 2 * g + j
                for a in range(2):
                    r = mm(bk.t[:, 256 * j:256 * j + n], h2t[:, a, 128 * k:128 * k + 128],
                           sel[:, a].rearrange("p e s -> p (e s)")[:, c0:c0 + n], j == 0 and a == 0, a == 1, t,
                           done["h2t", a, k // 4], bk.free)
            bk.free = []
            for j in range(2):
                k = 2 * g + j
                dst, src = xe[:, k, c0:c0 + n], bk.t[:, 256 * j:256 * j + n]
                if g % 2:
                    tx = ts(dst, src, SH2(k), None, OP.add, None, r, xe_read, P.modcol)
                else:
                    tx = af(dst, src, AF.Identity, r, xe_read, P.modcol, bias=SH2(k))
                bk.free.append(tx)
            for e in range(e0, e1):
                done["xe", 4 * q + e, g] = bk.free
        done["gather"] = r

    def xs(e, k):
        return xe[:, k, 64 * (e % 4):64 * (e % 4) + 64]

    def up(n, e, dst, j, first, last):
        def f(kh):
            def g(s, ld):
                w = s[:].rearrange("p (k n) -> p k n", k=4)
                bk = dst
                for k in range(4 * kh, 4 * kh + 4):
                    for h in range(2):
                        t = mm(bk.t[64 * h:64 * h + 64, 256 * j:256 * j + 256], xs(e, k), w[:, k - 4 * kh, 256 * h:256 * h + 256],
                               first and k == 0, last and k == KT - 1, ld, done["xe", e, k // 2], bk.free if first else None, beside=2)
                done["up"] = t
                return t
            return g
        for kh in range(2):
            P.plain((n, e, kh), f(kh))

    def hidden(e, part):
        i = e % 2
        n = 512 if part == 0 else 256
        g_, u_ = (B[0].t[:], B[1].t[:]) if part == 0 else (B[2].t[:, 0:256], B[2].t[:, 256:512])
        h = hid[i][:, 512 * part:512 * part + n]
        t = af(h, g_, AF.Silu, done["up"], done.get(("hT", e - 2, part)))
        t = tt(h, h, u_, OP.mult, t)
        if part == 0:
            B[0].free = [t]
            B[1].free = [t]
        else:
            B[2].free = [t]
        bk = B[3 + part]
        for j in range(n // 128):
            t2 = tp(bk.t[:, 128 * j:128 * j + 128], h[:, 128 * j:128 * j + 128], t, bk.free)
        r = acp(hidT[i][:, 4 * part:4 * part + n // 128].rearrange("p a b c -> p (a b c)"), bk.t[:, 0:n], t2,
                done.get(("down", e - 2)))
        bk.free = [r]
        done["hT", e, part] = r

    def down(e, j):
        def f(h):
            def g(s, ld):
                w = s[:].rearrange("p (u n) -> p u n", u=2)
                bk = B[5]
                for u in range(2):
                    for c in range(2):
                        t = mm(bk.t[64 * c:64 * c + 64, :], hidT[e % 2][:, 2 * j + u, h, :], w[:, u, 512 * c:512 * c + 512],
                               j == 0 and h == 0 and u == 0, j == 2 and h == 1 and u == 1, ld, done["hT", e, j // 2],
                               bk.free if j == 0 else None, beside=2)
                done["down", e] = t
                return t
            return g
        for h in range(2):
            P.plain((f"d{j}", e, h), f(h))

    def weigh(e):
        i = e % 2
        t = [ts(selw[:, a], bc(IOTA, 2, 1), posm[:, a, e:e + 1], wt[:, a, e:e + 1], OP.is_equal, OP.mult,
                done["pos"], done["wt"], done.get("weigh")) for a in range(2)]
        bk = B[6]
        for a in range(2):
            t2 = tp(bk.t[:, 128 * a:128 * a + 128], selw[:, a].rearrange("p a b -> p (a b)"), t, bk.free)
        done["weigh"] = t2
        done["selT", e] = acp(selT[i][:], bk.t[:, 0:256], t2, done.get(("comb", e - 2)))
        bk.free = [done["selT", e]]

    def combine(e):
        i = e % 2
        t = acp(y[i][:], B[5].t[:], done["down", e], done.get(("comb", e - 2)), P.kv_done[i])
        B[5].free = [t]
        for g in range(4):
            bk = B[6 + g % 2]
            c = g // 2
            for j in range(2):
                f = 2 * (g % 2) + j
                r = mm(bk.t[:, 256 * j:256 * j + 256], y[i][64 * c:64 * c + 64, 128 * f:128 * f + 128],
                       selT[i][64 * c:64 * c + 64, :], j == 0, j == 1, t, done["selT", e], bk.free)
            dst = pa(yacc[:, 4 * c + 2 * (g % 2):4 * c + 2 * (g % 2) + 2, :])
            if e == 0:
                bk.free = [cp(dst, bk.t[:], r, P.m_free)]
            elif e < 15:
                bk.free = [tt(dst, dst, bk.t[:], OP.add, r, done["y", g])]
            else:
                for j in range(2):
                    k = 2 * g + j
                    P.x_tok[k] = stt(x[:, k, :], bk.t[:, 256 * j:256 * j + 256], P.gt2[:, k:k + 1], x[:, k, :], OP.mult, OP.add, r,
                                     P.x_tok[k])
                bk.free = [P.x_tok[k]]
            done["y", g] = bk.free
        done["comb", e] = r

    def add_others():
        for k in range(KT):
            P.x_tok[k] = stt(x[:, k, :], yacc[:, k, :], P.gt2[:, k:k + 1], x[:, k, :], OP.mult, OP.add, done["y", k // 2],
                             P.modcol, done["gather"])

    P.stage, P.kv_done, P.kv_tok, stages = [P.sem("stage0"), P.sem("stage1")], [None, None], [], [0]

    def mem_side():
        yield from P.need(done, ("down", 1))
        free = done["down", 1]
        ld = P.load(mem[:], A["memT"], free, q=P.pool)
        yield ld
        t = af(memg[:], mem[:], AF.Square, ld, free)
        yield t, B[4].free
        for k in range(KT):
            t2 = mm(B[4].t[:, 0:T], ONE, memg[:, k, :], k == 0, k == KT - 1, t, B[4].free)
        t = af(rsm, B[4].t[:, 0:T], AF.Sqrt, t2, bias=EPS, scale=1.0 / 1024)
        B[4].free = [t]
        yield t
        t = rcp(rsm, rsm, t)
        tm = tt(mem[:], mem[:], bc(rsm, KT, 1), OP.mult, t)
        for l in (1, 0):
            done["memg", l] = [ts(memg[:, k, :], mem[:, k, :], col("norm_mem_2", 8 * l + k), None, OP.mult, None, tm, t2, done.get("kv1"))
                               for k in range(KT)]
            yield from P.need(done, "kv1")

    def kv_at(n):
        return 2 + n * 12 // 16

    def kv_unit(n):
        l, i = 1 - n // 8, n % 8
        P.want(("kv", n), [P.block(A["w_mem_kv"][l], 256 * i, 256)], zone(kv_at(n)))
        P.until(done, ("memg", l))

        def f(s, ld):
            w, bk = s[:].rearrange("p (k n) -> p k n", k=8), B[4]
            for g in range(2):
                gs = slice(128 * g, 128 * g + 128)
                for k in range(KT):
                    a, b = (w[:, k, gs], memg[:, k, :]) if i < 4 else (memg[:, k, gs], w[:, k, :])
                    t = mm(bk.t[:, 256 * g:256 * g + 256], a, b, g == 0 and k == 0, g == 1 and k == KT - 1, ld, done["memg", l], bk.free)
            two = lambda a: a.rearrange("p (a n) -> p a n", a=2)
            if l == 1:
                j = stages[0] % 2
                stages[0] += 1
                r = acp(y[j][:], bk.t[:], t, P.kv_done[j], [done.get(("comb", e)) for e in range(16)])
                if i < 4:
                    dst, src = A["kv"][:, 512 * i:512 * i + 512], y[j][:]
                else:
                    dst, src = two(A["kv"][:, 2048:4096])[:, :, 256 * (i - 4):256 * (i - 4) + 256], two(y[j][:])
                P.kv_done[j] = P.dma(P.pool, dst, src, P.stage[j], 16 * ((stages[0] + 1) // 2), r)
            else:
                dst, src = (pa(P.mk[:, 2 * i:2 * i + 2, :]), bk.t[:]) if i < 4 else (P.mv[:, :, 256 * (i - 4):256 * (i - 4) + 256], two(bk.t[:]))
                r = acp(dst, src, t, done["down", 5])
                P.kv_tok.append(r)
            bk.free = [r]
            if n == 7:
                done["kv1"] = t
            return t
        P.plain(("kv", n), f)

    P.lanes.append(Lane(mem_side()))
    P.call(route)
    for e in range(16):
        if e % 4 == 0:
            P.call(lambda e=e: gather(e // 4, 0, 1 if e == 0 else 4))
        if e:
            expert_loads(P, e)
        up("g0", e, B[0], 0, True, False)
        if e == 0:
            P.call(count)
        up("g1", e, B[0], 1, False, True)
        up("u0", e, B[1], 0, True, False)
        up("u1", e, B[1], 1, False, True)
        P.call(lambda e=e: hidden(e, 0))
        up("g2", e, B[2], 0, True, False)
        up("u2", e, B[2], 1, False, True)

        def mark(e=e):
            xe_read[:] = [done["up"]]
            hidden(e, 1)
            weigh(e)
            if e == 15:
                add_others()
        P.call(mark)
        for j in range(3):
            down(e, j)
        if e < 2:
            P.call(lambda e=e: gather(0, 1 + e, 2 + 2 * e))
        P.call(lambda e=e: combine(e))
        for n in range(16):
            if kv_at(n) == e:
                kv_unit(n)
        if e == 11:
            P.call(lambda: last_scales())
        if e == 12:
            P.call(lambda: prepare_c(P, [done["h2t", a, g] for a in range(2) for g in range(2)], done["pos"], done["down", 11]))

    class Loop:

        def __init__(self):
            self.q = {n: [] for n in streams}
            self.n = {n: 0 for n in ("act", "pe", "dve", "dma")}
            self.sem = {n: P.sem("more_" + n) for n in self.n}

        def do(self, n, fn, *w, dma=False):
            s = "dma" if dma else n
            self.n[s] += 16 if dma else 1
            self.q[n].append((fn, [x for x in w if x], s, 16 if dma else 1))
            return s, self.n[s]

        def emit(self, n, e, before):
            reg = {s: e.alloc_register(f"more_{n}_{s}") for s in self.n}
            tmp = e.alloc_register(f"more_{n}_tmp")
            with e.If(most[n] > 64):
                for t in before:
                    e.wait_ge(t.sem, t.count)
                for r in reg.values():
                    e.reg_mov(r, 0)
                with e.Fori(1, 4) as blk:
                    with e.Fori(0, 16) as ex:
                        c = e.value_load(counts[0:1, bass.ds(ex, 1)])
                        with e.If(c - blk * 64 > 0):
                            for fn, waits, s, k in self.q[n]:
                                for ws, wc in waits:
                                    e.reg_add(tmp, reg[ws], wc)
                                    e.wait_ge(self.sem[ws], tmp)
                                fn(e, ex, blk).then_inc(self.sem[s], k)
                            for s in self.n:
                                if n == "pe":
                                    e.reg_add(tmp, reg[s], self.whole[s])
                                    e.wait_ge(self.sem[s], tmp)
                            for s in self.n:
                                e.reg_add(reg[s], reg[s], self.n[s])

    def more():
        lp = Loop()
        W = P.at("more_w", Z, [4096])
        pc, wc, base = rt[:, 400:402], rt[:, 402:404], rt[:, 404:405]
        last = [None]

        def lmm(out, l, r, start, stop, *w):
            last[0] = lp.do("pe", lambda e, ex, blk: e.matmul(out, l, r, start=start, stop=stop, skip_group_check=True), *w)
            return last[0]

        def copy(out, i, *w):
            return lp.do("act", lambda e, ex, blk: e.copy(out, i), *w)

        def weights(w, view, *waits):
            return lp.do("act", lambda e, ex, blk: e.dma_start(view, w(ex)), *waits, dma=True)

        t = lp.do("dve", lambda e, ex, blk: e.tensor_copy(base, sm[:, 36:40][:, bass.ds(blk, 1)]))
        tp_ = None
        for a in range(2):
            tp_ = lp.do("dve", lambda e, ex, blk, a=a: e.tensor_copy(pc[:, a:a + 1], posm[:, a, bass.ds(ex, 1)]))
            tw = lp.do("dve", lambda e, ex, blk, a=a: e.tensor_copy(wc[:, a:a + 1], wt[:, a, bass.ds(ex, 1)]))
        t = lp.do("dve", lambda e, ex, blk: e.tensor_scalar(pc, pc, base, None, OP.subtract), t, tp_, tw)
        for a in range(2):
            ts_ = lp.do("dve", lambda e, ex, blk, a=a: e.tensor_scalar(sel[:, a, 0, :], IOTA, pc[:, a:a + 1], None, OP.is_equal), t)
            tw = lp.do("dve", lambda e, ex, blk, a=a: e.tensor_scalar(
                selw[:, a], bc(IOTA, 2, 1), pc[:, a:a + 1], wc[:, a:a + 1], OP.is_equal, OP.mult), t)
        for k in range(KT):
            for a in range(2):
                t = lmm(B[3].t[:, 64 * k:64 * k + 64], h2t[:, a, 128 * k:128 * k + 128], sel[:, a, 0, :], k == 0 and a == 0,
                        a == 1, ts_)
        x64 = xe[:, 0:2, :].rearrange("p a t -> p (a t)")
        for k in range(KT):
            tx = lp.do("act", lambda e, ex, blk, k=k: e.activation(x64[:, 64 * k:64 * k + 64], B[3].t[:, 64 * k:64 * k + 64],
                                                                  AF.Identity, bias=SH2(k)), t)
        for a in range(2):
            t = lp.do("pe", lambda e, ex, blk, a=a: e.transpose(B[6].t[:, 128 * a:128 * a + 128],
                                                             selw[:, a].rearrange("p a b -> p (a b)"), P.EYE), tw)
        tT = copy(selT[0][:], B[6].t[:, 0:256], t)
        tw = None
        for n, w, j, bk, o, st in (("g", "w_eg", 0, 0, 0, True), ("g", "w_eg", 1, 0, 256, False), ("u", "w_eu", 0, 1, 0, True),
                                   ("u", "w_eu", 1, 1, 256, False), ("g", "w_eg", 2, 2, 0, True), ("u", "w_eu", 2, 2, 256, False)):
            w3 = W[:].rearrange("p (k n) -> p k n", k=8)
            ld = weights(lambda ex, w=w, j=j: A[w][bass.ds(ex, 1), :, 512 * j:512 * j + 512].rearrange(
                "o (k p) n -> p (o k) n", p=128), w3, tw)
            for k in range(KT):
                for h in range(2):
                    tw = lmm(B[bk].t[64 * h:64 * h + 64, o:o + 256], x64[:, 64 * k:64 * k + 64], w3[:, k, 256 * h:256 * h + 256],
                             st and k == 0, k == KT - 1, ld, tx)
        for part, (g_, u_) in enumerate(((B[0].t[:], B[1].t[:]), (B[2].t[:, 0:256], B[2].t[:, 256:512]))):
            n = 512 if part == 0 else 256
            h = hid[0][:, 512 * part:512 * part + n]
            t = lp.do("act", lambda e, ex, blk, h=h, g_=g_: e.activation(h, g_, AF.Silu), tw)
            t = lp.do("dve", lambda e, ex, blk, h=h, u_=u_: e.tensor_tensor(h, h, u_, OP.mult), t)
            for j in range(n // 128):
                t2 = lp.do("pe", lambda e, ex, blk, j=j, h=h, part=part: e.transpose(
                    B[3 + part].t[:, 128 * j:128 * j + 128], h[:, 128 * j:128 * j + 128], P.EYE), t, tx)
            th = copy(hidT[0][:, 4 * part:4 * part + n // 128].rearrange("p a b c -> p (a b c)"), B[3 + part].t[:, 0:n], t2)
        for j in range(3):
            w3 = W[:].rearrange("p (k n) -> p k n", k=4)
            ld = weights(lambda ex, j=j: A["w_ed"][bass.ds(ex, 1), 512 * j:512 * j + 512, :].rearrange(
                "o (k p) n -> p (o k) n", p=128), w3, tw)
            for h in range(2):
                for u in range(2):
                    for c in range(2):
                        tw = lmm(B[5].t[64 * c:64 * c + 64, :], hidT[0][:, 2 * j + u, h, :], w3[:, 2 * h + u, 512 * c:512 * c + 512],
                                 j == 0 and h == 0 and u == 0, j == 2 and h == 1 and u == 1, ld, th)
        ty = copy(y[0][:], B[5].t[:], tw)
        rd = [tT, None]
        for g in range(4):
            bk, c = B[6 + g % 2], g // 2
            for j in range(2):
                f = 2 * (g % 2) + j
                t = lmm(bk.t[:, 256 * j:256 * j + 256], y[0][64 * c:64 * c + 64, 128 * f:128 * f + 128],
                        selT[0][64 * c:64 * c + 64, :], j == 0, j == 1, ty, tT, rd[g % 2])
            for j in range(2):
                k = 2 * g + j
                rd[g % 2] = lp.do("dve", lambda e, ex, blk, k=k, i=bk.t[:, 256 * j:256 * j + 256]: e.scalar_tensor_tensor(
                    out=x[:, k, :], in0=i, scalar=P.gt2[:, k:k + 1], in1=x[:, k, :], op0=OP.mult, op1=OP.add), t)
        lp.whole = dict(lp.n)
        lp.do("act", lambda e, ex, blk: e.copy(rt[:, 406:407], sm[:, 0:1]), *lp.whole.items())
        lp.do("dve", lambda e, ex, blk: e.tensor_copy(rt[:, 407:408], sm[:, 0:1]), *lp.whole.items())
        before = list(flat([done["comb", 15], [P.x_tok[k] for k in range(KT)], done["selT", 15]]))
        for t in before:
            t.used = True
        for n in streams:
            P.raw(streams[n], lambda e, n=n: lp.emit(n, e, before))
    P.call(more)

    P.sqg, P.sqx = P.at("sqg", Z + 16384, [KT, T]), P.at("sqx_", Z + 19200, [KT, T])
    P.last, P.root, gg = P.at("last", Z + 18944, [T]), P.small[:, 500:508], P.small[:, 492:500]
    root = P.root

    def last_scales():
        t = af(root, col("g_final", 0, 8), AF.Square)
        done["root"] = [af(root, root, AF.Sqrt, t, bias=EPS), tt(gg, col("g_final", 0, 8), col("norm_mix_2", 0, 8), OP.mult)]


C_MASKS = ["level4", "level5", "level6", "last", "dup", "sixteen", "same"]
C_SMALL = ["freq_sa", "sign_sa", "freq_ix", "sign_ix", "eps_q"]
N_CC = 128 * len(C_MASKS) + 32
TURN = 2 * np.pi
TURN1 = 6.28125
TURN2 = float(np.floor((TURN - TURN1) * 2.0 ** 20) / 2.0 ** 20)
TURN3 = float(np.float32(TURN - TURN1 - TURN2))
HALF_TURN = 3.1415925
BIG = -1e30
TAKEN = -3e38


def constants_c():
    p, f = np.meshgrid(np.arange(128), np.arange(128), indexing="ij")
    m = {f"level{i}": (p >> (i + 1) == f >> (i + 1)) & (p >> i > f >> i) for i in (4, 5, 6)}
    m["last"] = p == 127
    m["dup"] = p == f % 64
    m["sixteen"] = p // 16 == f // 16
    m["same"] = np.where(f // 64 <= p // 64, 0.0, BIG)
    sm = np.zeros((128, 32), np.float32)
    for c, (head, half) in ((0, (128, 16)), (2, (64, 8))):
        rd = 2 * half
        freq = np.float32(500000.0) ** -(np.arange(half, dtype=np.float32) * np.float32(2.0) / np.float32(rd))
        for r in range(128):
            k = r % head
            if k < rd:
                sm[r, c] = freq[k % half]
                sm[r, c + 1] = -1.0 if k < half else 1.0
    sm[:, 4] = 1.28e-10
    sm[:, 16:32] = np.arange(128)[:, None] % 16 == np.arange(16)
    return np.concatenate([m[n].astype(np.float32) for n in C_MASKS] + [sm], axis=1)


class Layout2:
    KQ, V = (4096, 10240), (6144, 12288)
    CC, ROPE = 8192, 9152
    D, G, U, TT = 13312, 14848, 17920, 18944
    ODN, XQ = 19968, 22016
    IQ, SMT, IK, SCORE, RELU = 24064, 25088, 25344, 25600, 25984
    MK, MV = 26576, 28624
    RS = 21504
    WSM, TURNS = (13312, 22016), 12288
    Y = 7168


def small_weights(P, l, *w):
    A, Z = P.A, P.Z
    o = Z + Layout2.WSM[l]
    t = P.at(f"wsm{l}", o, [KT, 128])
    z = P.fill(t[:], 0.0, *w, on=P.pool)
    ld = [P.load(t[:, :, c:c + n], A["w_small"][l, :, :, s:s + n], z, q=P.pool)
          for c, s, n in ((0, 0, 64), (64, 64, 8), (96, 72, 16))]
    hi, lo = P.at(f"wsm{l}_hi", Z + (Layout2.IQ if l else Layout2.KQ[1]), [KT, 128], F32R), P.at(f"wsm{l}_lo", o, [KT, 128], F32R)

    def split():
        yield ld
        th = P.acp(hi[:], t[:], ld, *w)
        P.wsm = Quarter(hi, lo, th, P.tt(lo[:], t[:], hi[:].bitcast(F32), OP.subtract, ld, th), None)
    return split()


def prepare_c(P, *w):
    A, Z, L = P.A, P.Z, Layout2
    ts, stt, cp, af = P.ts, P.stt, P.cp, P.af
    cc = P.at("cc", Z + L.CC, [N_CC])
    rope = P.rope = P.at("rope", Z + L.ROPE, [4, T])
    P.cm = {n: cc[:, 128 * i:128 * i + 128] for i, n in enumerate(C_MASKS)}
    o = 128 * len(C_MASKS)
    cs = P.ccol = {n: cc[:, o + i:o + i + 1] for i, n in enumerate(C_SMALL)}
    P.e16 = cc[:, o + 16:o + 32]
    P.l_cc = l_cc = P.load(cc[:], A["cstc"], *w, q=P.pool)
    posi = P.nc.alloc_sbuf_tensor_at("posi", [128, T], I32, offset=BASE + 4 * (Z + L.TURNS))
    l_pos = P.load(posi[:], A["positions"].partition_broadcast(128), *w, q=P.pool)
    P.lanes.append(Lane(small_weights(P, 0, *w)))
    P.hb = P.small[:, 376:424]
    P.hb_tok = ts(P.hb, P.col("b_gate_2", 0, 48), 0.5, None, OP.mult, None)

    def tables():
        a0, a1, a2 = (P.at(f"rp{i}", Z + L.TURNS + 256 + 256 * i, [T])[:] for i in range(3))
        t = cp(a2, posi[:], l_pos)
        for i, n in enumerate(("sa", "ix")):
            f, sg = cs["freq_" + n], cs["sign_" + n]
            for j in range(2):
                t = ts(a0, a2, f, None, OP.mult, None, t, l_cc)
                t = ts(a1, a0, 1.0 / TURN, 0.25 * (1 - j), OP.mult, OP.add, t)
                t = ts(a1, a1, 12582912.0, -12582912.0, OP.add, OP.add, t)
                for c in (TURN1, TURN2, TURN3):
                    t = stt(a0, a1, -c, a0, OP.mult, OP.add, t)
                if j == 0:
                    t = ts(a0, a0, TURN / 4, None, OP.add, None, t)
                t = ts(a0, a0, HALF_TURN, -HALF_TURN, OP.min, OP.max, t)
                t = af(rope[:, 2 * i + j, :], a0, AF.Sin, t, *w)
                if j == 1:
                    t = ts(rope[:, 2 * i + 1, :], rope[:, 2 * i + 1, :], sg, None, OP.mult, None, t)
                yield
        P.rope_tok = [t]
    P.lanes.append(Lane(tables()))


def phase_c(P, out):
    A, Z, L = P.A, P.Z, Layout2
    mm, tp, af, acp, tt, ts, stt, cp, rcp, red = P.mm, P.tp, P.af, P.acp, P.tt, P.ts, P.stt, P.cp, P.rcp, P.red
    col, sm, ONE, EYE, EPS, x, B = P.col, P.sm, P.ONE, P.EYE, P.EPS, P.x, P.banks
    LE, cm, l_cc, rope, hb = P.mask["le"], P.cm, P.l_cc, P.rope, P.hb
    pa = lambda a: a.rearrange("p a t -> p (a t)")
    at = lambda n, o, s, dt=F32: P.at(n, Z + o, s, dt)

    H = Part(at("h_hi", 0, [KT, T], F32R), at("h_lo", 2048, [KT, T], F32R))
    KQ = [at(f"kq{g}", L.KQ[g], [4, 2, 2, 128]) for g in range(2)]
    V = [at(f"v{g}", L.V[g], [4, 2, 128]) for g in range(2)]
    D, G = at("dd", L.D, [4, 3, 128]), at("gg", L.G, [24, 128])
    U, Tm = at("uu", L.U, [8, 128]), at("tt", L.TT, [8, 128])
    sys_u, sys_t, sys_m = at("su", L.D, [8, 16]), at("st", L.D + 128, [8, 16]), at("sm_", L.D + 256, [8, 16])
    Q = at("qq", L.D + 512, [8, 128])
    rows = at("rows", L.U, [16, 128])
    odn, xq = at("odn", L.ODN, [KT, T]), at("xq", L.XQ, [KT, T])
    iq, ik, smT = at("iq", L.IQ, [4, T]), at("ik", L.IK, [T]), at("smT", L.SMT, [T])
    score, relu = at("score", L.SCORE, [384]), at("relu", L.RELU, [512])
    Y = [at(f"y_{i}", L.Y + 512 * i, [2, T]) for i in range(2)]
    PM = [at(f"pm{i}", L.ODN + 512 * i, [512]) for i in range(4)]
    PC = [at(f"pc{i}", L.V[0] + 512 * i, [512]) for i in range(4)]
    mk, mv = P.mk, P.mv
    mg = at("mg", L.MK, [KT, T])
    sq_, sk_, sv_ = at("sq_", L.XQ, [KT, T]), at("sk_", L.KQ[0], [KT, T]), at("sv_", L.MV, [2, 1024])
    gate = at("gate", L.IQ, [4, T])
    XA = Part(at("xa_hi", L.MV, [KT, T], F32R), at("xa_lo", L.XQ, [KT, T], F32R))
    SA = Part(at("sa_hi", L.KQ[0], [KT, T], F32R), at("sa_lo", L.XQ, [KT, T], F32R))
    DN = Part(at("dn_hi", L.D, [KT, T], F32R), at("dn_lo", L.ODN, [KT, T], F32R))
    MG = Part(at("m_hi2", L.U, [KT, T], F32R), at("m_lo2", L.MK, [KT, T], F32R))
    zt = [at(f"zt{i}", L.KQ[1] + 512 * i, [2, T]) for i in range(2)]
    hsq, hn, xg = at("hsq", 0, [KT, T]), at("hn", L.G + 2048, [KT, T]), at("xg", 2048, [KT, T])
    rs = at("rs_", L.RS, [T])
    HM = Part(at("hm_hi", L.KQ[0], [KT, T], F32R), at("hm_lo", L.V[0], [KT, T], F32R))
    HF = Part(at("hf_hi", L.KQ[1], [KT, T], F32R), at("hf_lo", L.V[1], [KT, T], F32R))
    FH, FL = at("f_hi", L.KQ[1], [22, T], F32R), at("f_lo", L.KQ[1] + 5632, [22, T], F32R)
    fg = [at(f"fg{i}", L.KQ[0] + 1024 * i, [4, T]) for i in range(2)]
    fa = [at(f"fa{i}", L.V[0] + 512 * i, [512]) for i in range(2)]
    tokm = P.small[:, 240:336].rearrange("p (c n) -> p c n", c=2)
    ekd = P.small[:, 336:344]
    ss, r8, bp, s8 = (P.small[:, 344 + 8 * i:352 + 8 * i] for i in range(4))
    alog = P.small[64:72, 424:428]
    mx, nmx, sums = P.small[:, 428:444], P.small[:, 444:460], P.small[:, 460:476]
    top8, gg = P.small[:, 476:492], P.small[:, 492:500]
    for i in range(P.NB):
        P.pe_read[i] = [P.pe_read[i], P.doneB["down", 15]]

    SW16 = list(range(16, 32)) + list(range(16))
    SW8 = list(range(8, 16)) + list(range(8)) + list(range(16, 32))

    def rotate(a, n, ci, tmp, mask_, *w):
        p = a.shape[0]
        cos, sin = (bc(rope[0:p, 2 * ci + j, :], n, 1) for j in range(2))
        t0 = P.dve.do(lambda e: e.stream_shuffle(tmp, a, mask_), *w)
        t1 = tt(tmp, tmp, sin, OP.mult, t0, P.rope_tok)
        t2 = tt(a, a, cos, OP.mult, t0, P.rope_tok)
        return tt(a, a, tmp, OP.add, t1, t2)

    units, mixed = P.units, P.mixed

    sqt, fin = {}, []

    def square(j, n, t):
        t = af(pa(hsq[:, j:j + n, :]), pa(x[:, j:j + n, :]), AF.Square, t)
        for k in range(j, j + n):
            sqt[k] = t

    def scaled(part, k, g, *w):
        h = af(part.hi[:, k, :], x[:, k, :], AF.Copy, P.x_tok[k], *w, scale=g)
        part.tok[k] = [h, stt(part.lo[:, k, :], x[:, k, :], g, part.hi[:, k, :].bitcast(F32), OP.mult, OP.subtract, h)]

    def total(bk, sq, t):
        return [mm(bk.t[:, 0:T], ONE, sq[:, k, :], k == 0, k == KT - 1, t[k], bk.free) for k in range(KT)][-1]

    def root(t, bias):
        t = af(rs[:], B[7].t[:, 0:T], AF.Ln, t, bias=bias, scale=1.0 / 1024)
        B[7].free = [t]
        P.rs_tok = af(rs[:], rs[:], AF.Exp, t, scale=-0.5)

    def normed(g, *w):
        P.staggered(H, hn, lambda k: stt(hn[:, k, :], x[:, k, :], g(k), rs[:], OP.mult, OP.mult, P.rs_tok, P.x_tok[k], *w))

    def times_root(out, i, *w):
        return tt(out, i, bc(rs[:], 2, 1), OP.mult, P.rs_tok, *w)

    def last_norm():
        for j in range(0, KT, 2):
            square(j, 2, P.x_tok[j])
        for k in range(KT):
            P.x_tok[k] = af(xg[:, k, :], x[:, k, :], AF.Copy, P.x_tok[k], scale=col("norm_final_2", k))
        root(total(B[7], hsq, sqt), EPS)
        for j in range(0, KT, 2):
            t = times_root(x[:, j:j + 2, :], xg[:, j:j + 2, :], P.x_tok[j], P.x_tok[j + 1], sqt[j])
            fin.append(P.load(out[:, j:j + 2, :], x[:, j:j + 2, :], t))

    def last_x(done):
        yield from P.need(done, "last")
        yield P.last_tok
        t = af(P.last[:], P.last[:], AF.Exp, P.last_tok, scale=-0.5)
        yield t, HM.tok.values(), H.tok.values()
        for k in range(KT):
            P.x_tok[k] = stt(x[:, k, :], x[:, k, :], col("g_final", k), P.last[:], OP.mult, OP.mult, HM.tok[k], H.tok[k], t)
            yield

    def layer(l):
        done = {}
        w_in = A["w_in_2"][l]
        need = lambda *ks: P.need(done, *ks)
        l_al = [P.load(alog[:, 0:1], A["a_log"][l], P.alog_free, q=P.pool),
                P.load(alog[:, 1:2], A["dt_bias"][l], P.alog_free, q=P.pool)]

        def mix_scaled():
            for k in range(KT):
                scaled(HM, k, *gmix(k))
            if l == 0:
                for k in range(KT):
                    sqt[k] = af(P.sqg[:, k, :], x[:, k, :], AF.Square, P.x_tok[k], P.doneB["root"], scale=P.root[:, k:k + 1])
                P.most = min(4, P.MOST)
            else:
                for j in range(0, KT, 2):
                    square(j, 2, P.x_tok[j])

        def gmix(k):
            return (gg[:, k:k + 1], P.doneB["root"]) if l == 0 else (col("norm_mix_2", 8 + k),)

        def narrow(q):
            bk = P.bank()
            for k in range(KT):
                for w, v, wt in ((q.hi, HM.hi, q.th), (q.hi, HM.lo, q.th), (q.lo, HM.hi, q.tl)):
                    t = mm(bk.t[:, 0:T], w[:, k, :], v[:, k, :], k == 0 and v is HM.hi and w is q.hi,
                           k == KT - 1 and w is q.lo, wt, HM.tok[k], bk.free)
            P.narrow_read = t
            root(total(B[7], hsq if l else P.sqg, sqt), EPS if l else sm[:, 2:3])
            done["small"] = tt(smT[:], bk.t[:, 0:T], rs[:], OP.mult, t, P.rs_tok)
            bk.free = [done["small"]]

        tx = {}

        def strengths():
            yield from need("small")
            if l == 0:
                for k in range(0, KT, 2):
                    tx[k] = tx[k + 1] = af(pa(P.sqx[:, k:k + 2, :]), pa(x[:, k:k + 2, :]), AF.Square, P.x_tok[k], P.x_tok[k + 1])
                yield tx.values(), B[5].free
                last_sum = total(B[5], P.sqx, tx)
            w = done["small"]
            z, tmp, be = smT[64:72, :], relu[64:72, 0:256], smT[96:104, :]
            t = af(alog[:, 2:3], alog[:, 0:1], AF.Exp, l_al)
            t0 = ts(alog[:, 2:3], alog[:, 2:3], -1.0, None, OP.mult, None, t)
            t = af(tmp, z, AF.Abs, w, l_al, bias=alog[:, 1:2])
            t = af(tmp, tmp, AF.Exp, t, scale=-1.0)
            t3 = af(be, be, AF.Tanh, w, scale=0.5)
            t1 = af(tmp, tmp, AF.Ln, t, bias=ONE[64:72, 0:1])
            if l == 0:
                P.last_tok = af(P.last[:], B[5].t[:, 0:T], AF.Ln, last_sum, bias=EPS, scale=1.0 / 1024)
                B[5].free = [P.last_tok]
            t3 = ts(be, be, 0.5, 0.5, OP.mult, OP.add, t3)
            t = ts(z, z, alog[:, 1:2], 0.0, OP.add, OP.max, t1)
            t = tt(z, z, tmp, OP.add, t)
            t = ts(z, z, alog[:, 2:3], None, OP.mult, None, t, t0)
            P.alog_free = [t]
            done["last"] = True
            for c in range(2):
                s_ = smT[64:72, 128 * c:128 * c + 128]
                t2 = P.dve.do(lambda e, s_=s_: e.tensor_tensor_scan(s_, s_, s_, 0.0, OP.add, OP.bypass), t)
            done["gcT"] = t2
            yield t2, t3, B[7].free
            bk = B[7]
            for c in range(2):
                t4 = tp(bk.t[:, 128 * c:128 * c + 128], smT[:, 128 * c:128 * c + 128], t2, t3, bk.free)
            t = cp(tokm[:], bk.t[:, 0:256].rearrange("p (c n) -> p c n", c=2)[:, :, 64:112], t4)
            bk.free = [t]
            done["tokm"] = t = ts(tokm[:, :, 40:48], tokm[:, :, 40:48], 512 ** -0.5, None, OP.mult, None, t)
            yield t
            t5 = mm(bk.t[:, 0:8], cm["last"], tokm[:, 0, 0:8], True, True, t, bk.free, l_cc)
            done["ekd"] = tt(ekd, bk.t[:, 0:8], tokm[:, 0, 0:8], OP.subtract, t5)
            bk.free = [done["ekd"]]

        def index():
            yield from need("small")
            yield done["small"], B[3].free
            bk = B[3]
            t = mm(bk.t[:, 0:T], cm["dup"][0:64, :], smT[0:64, :], True, True, done["small"], bk.free, l_cc)
            t = acp(ik[:], bk.t[:, 0:T], t)
            bk.free = [t]
            yield from need("tokm", ("iq", 0), ("iq", 1))
            tmp = PM[0][:].rearrange("p (n t) -> p n t", n=2)
            tk = rotate(ik[:].unsqueeze(1), 1, 1, tmp[:, 0:1], SW8, t)
            ti = rotate(iq[:, 0:2, :], 2, 1, tmp, SW8, done["iq", 0], tk)
            yield ti
            ti = rotate(iq[:, 2:4, :], 2, 1, tmp, SW8, done["iq", 1], ti)
            yield ti
            ta = [None, None]
            for h in range(8):
                ps = slice(64 * (h % 2), 64 * (h % 2) + 64)
                bk = B[3 + h % 2]
                for b in range(2):
                    n = 128 * (b + 1)
                    t = mm(bk.t[:, 128 * b:128 * b + n], iq[ps, h // 2, 128 * b:128 * b + 128], ik[ps, 0:n], b == 0, b == 1,
                           ti, tk, bk.free)
                t = af(relu[:, 0:384], bk.t[:, 0:384], AF.Relu, t, ta, done["tokm"])
                bk.free = [t]
                if h == 0:
                    for b in range(2):
                        t2 = stt(score[:, 256 * b:256 * b + 128], relu[:, 256 * b:256 * b + 128], tokm[:, b, 40:41], cm["same"],
                                 OP.mult, OP.add, t, P.maskb_free, l_cc)
                    ta = [ts(score[:, 128:256], relu[:, 128:256], tokm[:, 1, 40:41], None, OP.mult, None, t), t2]
                else:
                    ta = [stt(score[:, o_:o_ + n], relu[:, o_:o_ + n], tokm[:, b, 40 + h:41 + h], score[:, o_:o_ + n],
                              OP.mult, OP.add, t, ta[b]) for b, o_, n in ((0, 0, 128), (1, 128, 256))]
                yield B[3 + (h + 1) % 2].free
            done["score"] = ta

        def best():
            yield from need("score")
            ta = list(done["score"])
            for r in range(8):
                t = []
                for b, o_, n in ((0, 0, 128), (1, 128, 256)):
                    t.append(P.dve.do(lambda e, b=b, o_=o_, n=n: e.max(top8[:, 8 * b:8 * b + 8], score[:, o_:o_ + n]), ta[b]))
                for b, o_, n in ((0, 0, 128), (1, 128, 256)):
                    ta[b] = P.dve.do(lambda e, b=b, o_=o_, n=n: e.match_replace(
                        score[:, o_:o_ + n], top8[:, 8 * b:8 * b + 8], score[:, o_:o_ + n], TAKEN), t[b])
                yield ta
            done["maskb"] = ts(score[:], score[:], 0.5 * TAKEN, BIG, OP.is_gt, OP.mult, ta)

        nr, y_free, y_late = [0], [[], []], [lambda: None] * 2

        def conv_in(kind, g):
            def f(xp, b, c, t):
                n = nr[0]
                nr[0] += 1
                y_ = Y[n % 2]
                h = 2 * ((c % 512) // 256)
                y_late[n % 2]()
                w = lambda j, a: col("conv_w_2", 96 * l + 24 * j + 8 * kind + 4 * g + h + a)
                src = [b[:, 256 * a:256 * a + 256] for a in range(2)]
                ty = [af(y_[:, a, :], src[a], AF.Copy, t, y_free[n % 2], scale=w(3, a)) for a in range(2)]
                ty = [ty, ty]
                for j in (2, 1, 0):
                    s = 3 - j
                    ty = [stt(y_[:, a, s:], src[a][:, 0:T - s], w(j, a), y_[:, a, s:], OP.mult, OP.add, ty[a]) for a in range(2)]
                dst = V[g][:, h:h + 2] if kind == 2 else KQ[g][:, h:h + 2, :, 1 - kind, :]

                def silu():
                    r = af(dst, y_[:].rearrange("p a (c n) -> p a c n", c=2), AF.Silu, ty)
                    y_free[n % 2] = [r]
                    done["qkv"[kind], g, h] = r
                y_late[n % 2] = P.later(ty, silu)
                return ty
            return f

        def delta(g):
            kq, v = KQ[g], V[g]
            bank = [B[5], B[6], B[7]]
            g8 = lambda i: G[:, 8 * i:8 * i + 8, :]
            gcol = lambda c, h: tokm[:, c, 4 * g + h:4 * g + h + 1]
            M = g8(0)
            MA = G[:].rearrange("p (k b) n -> p k b n", k=3)
            KA = G[:, 16:24, :].rearrange("p (k h) n -> p k h n", k=2)
            yield from need("ekd")
            if g:
                yield from need(("dn", 0))
            yield [b.free for b in bank[:2]], done["tokm"], done["ekd"]
            for p in range(2):
                bk = bank[p]
                for a in range(2):
                    h = 2 * p + a
                    t = mm(bk.t[:, 256 * a:256 * a + 256], bc(EYE[64:96, 64 + 4 * g + h:65 + 4 * g + h].squeeze(1), 128, 1),
                           smT[64:96, :], a == 0, a == 1, done["gcT"], bk.free)
                for a in range(2):
                    h = 2 * p + a
                    s0, s1 = bk.t[:, 256 * a:256 * a + 128], bk.t[:, 256 * a + 128:256 * a + 256]
                    ts(D[:, h, 0, :], s0, gcol(0, h), 0.0, OP.subtract, OP.min, t, done["tokm"])
                    ts(D[:, h, 1, :], s1, ekd[:, 4 * g + h:4 * g + h + 1], 0.0, OP.add, OP.min, done["ekd"])
                    td = ts(D[:, h, 2, :], s1, gcol(1, h), 0.0, OP.subtract, OP.min)
                bk.free = [td]
            yield td
            tD = af(D[:], D[:], AF.Exp, td)
            yield from need(*[(n, g, h) for n in "kq" for h in (0, 2)])
            for p in range(2):
                yield [b.free for b in bank], [done[n, g, 2 * p] for n in "kq"]
                bw = bank[2]
                inp = [done[n, g, 2 * p] for n in "kq"]
                tm = []
                for a in range(2):
                    h = 2 * p + a
                    bk = bank[a]
                    t = mm(bk.t[:], kq[:, h, 0, 0, :], kq[:, h].rearrange("p c a n -> p (c a n)"), True, True, inp, bk.free)
                    t2 = mm(bw.t[:, 256 * a:256 * a + 256], kq[:, h, 1, 0, :], kq[:, h, 1].rearrange("p a n -> p (a n)"), a == 0,
                            a == 1, bw.free)
                    tm.append((t, t2))
                for a in range(2):
                    h = 2 * p + a
                    bk = bank[a]
                    b2 = lambda o: bk.t[:, o:o + 256].rearrange("p (a n) -> p a n", a=2)
                    tt(MA[:, 0:2, 2 * h, :], b2(0), bc(D[:, h, 0, :], 2, 1), OP.mult, tm[a][0], tD)
                    tG = tt(KA[:, :, h, :], b2(256), bc(D[:, h, 1, :], 2, 1), OP.mult)
                    bk.free = [tG]
                for a in range(2):
                    h = 2 * p + a
                    tG = tt(MA[:, 0:2, 2 * h + 1, :], bw.t[:, 256 * a:256 * a + 256].rearrange("p (a n) -> p a n", a=2),
                            bc(D[:, h, 2, :], 2, 1), OP.mult, tm[1][1], tD)
                bw.free = [tG]
            t = tt(U[:], M, bc(cm["sixteen"], 8, 1), OP.mult, tG, l_cc)
            t = tr = red(sys_m[:], U[:].rearrange("p s (b i) -> p s i b", b=8), OP.add, t)
            t2 = tt(sys_t[:], sys_m[:], bc(P.e16, 8, 1), OP.mult, t)
            t2 = red(ss, sys_t[:], OP.add, t2)
            t2 = ts(ss, ss, 1e-6, None, OP.add, None, t2)
            tss = t2
            t2 = rcp(r8, ss, t2)
            tb = tt(bp.rearrange("p (h c) -> p h c", h=4), r8.rearrange("p (h c) -> p h c", h=4),
                    tokm[:, :, 32 + 4 * g:36 + 4 * g].rearrange("p c h -> p h c"), OP.mult, t2)
            t = tt(sys_m[:], sys_m[:], bc(bp, 16, 2), OP.mult, tb)
            tu = cp(sys_u[:], bc(P.e16, 8, 1))
            yield t
            ts8 = af(s8, ss, AF.Sqrt, tss)
            md = sys_m[:].rearrange("p s i -> p (s i)")
            tj = []

            def rows_of(i):
                n = 4 if i < 3 else 3
                return [af(rows[:, j, :], md, AF.Copy, t, tr, scale=P.e16[:, j:j + 1]) for j in range(4 * i, 4 * i + n)]

            def spread(i):
                n = len(te[i])
                tj.append(mm(bank[i % 3].t[:, 0:128 * n], cm["sixteen"], rows[:, 4 * i:4 * i + n, :].rearrange("p j n -> p (j n)"),
                             True, True, te[i], bank[i % 3].free))
            te = [rows_of(0)]
            for i in range(3):
                te.append(rows_of(i + 1))
                yield te[i], bank[i].free
                spread(i)
            tM = tt(M, M, bc(bp, 128, 2), OP.mult, tb)
            tA = tt(g8(1), g8(1), bc(LE, 8, 1), OP.mult, tG)
            for j in range(15):
                if j == 4:
                    spread(3)
                bk = bank[j // 4 % 3]
                mj = bk.t[:, 128 * (j % 4):128 * (j % 4) + 128].rearrange("p (s i) -> p s i", s=8)[:, :, j + 1:]
                tu = tt(sys_t[:, :, j + 1:], mj, bc(sys_u[:, :, j:j + 1].squeeze(2), 15 - j, 2), OP.mult, tu, tj[j // 4])
                tu = tt(sys_u[:, :, j + 1:], sys_u[:, :, j + 1:], sys_t[:, :, j + 1:], OP.subtract, tu)
                if j % 4 == 3 or j == 14:
                    bk.free = [tu]
                    yield tu
            tU = tt(U[:].rearrange("p s (b i) -> p s b i", b=8), bc(sys_u[:], 8, 2),
                    bc(cm["sixteen"].rearrange("p (b i) -> p b i", b=8), 8, 1), OP.mult, tu)
            yield from need(("v", g, 0), ("v", g, 2))
            yield tu, done["v", g, 0], done["v", g, 2]
            tvs = []
            for p in range(2):
                bk = bank[p]
                for i in range(4):
                    t = tp(bk.t[:, 128 * i:128 * i + 128], v[:, 2 * p + i // 2, i % 2, :], done["v", g, 2 * p], bk.free)
                tv = [af(v[:, 2 * p + i // 2, i % 2, :], bk.t[:, 128 * i:128 * i + 128], AF.Copy, t, ts8,
                         scale=s8[:, 4 * p + i:4 * p + i + 1]) for i in range(4)]
                bk.free = tv[-1:]
                tvs += tv
            yield tU
            tT = []
            for p in range(2):
                bk = bank[(2 + p) % 3]
                for i in range(4):
                    t = tp(bk.t[:, 128 * i:128 * i + 128], U[:, 4 * p + i, :], tU, bk.free)
                r = acp(Tm[:, 4 * p:4 * p + 4, :], bk.t[:].rearrange("p (s n) -> p s n", s=4), t)
                bk.free = [r]
                tT.append(r)
            tU, tQf = [tU, tU], [None, None]
            b4 = lambda bk: bk.t[:].rearrange("p (s n) -> p s n", s=4)
            for lv in (4, 5, 6):
                yield tT, tU, tM, bank[0].free, bank[1].free
                tQ = []
                for p in range(2):
                    bk = bank[p]
                    for i in range(4):
                        s = 4 * p + i
                        t = mm(bk.t[:, 128 * i:128 * i + 128], M[:, s, :], Tm[:, s, :], i == 0, i == 3, tM, tT[p], bk.free)
                    t = tt(Q[:, 4 * p:4 * p + 4, :], b4(bk), bc(cm[f"level{lv}"], 4, 1), OP.mult, t, tQf[p])
                    bk.free = [t]
                    tQ.append(t)
                yield tQ
                bt, to = bank[2], list(tU)

                def times(p, bk, a, b):
                    for i in range(4):
                        s = 4 * p + i
                        t = mm(bk.t[:, 128 * i:128 * i + 128], a[:, s, :], b[:, s, :], i == 0, i == 3, tQ[p], to[p], bk.free)
                    return t

                def less(a, p, bk, t):
                    a = a[:, 4 * p:4 * p + 4, :]
                    t = tt(a, a, b4(bk), OP.subtract, t)
                    bk.free = [t]
                    return t
                tq = times(0, bt, U, Q) if lv < 6 else None
                tQf = [times(p, bank[p], Q, U) for p in range(2)]
                if lv < 6:
                    tT[0] = less(Tm, 0, bt, tq)
                    yield tT[0]
                    tq = times(1, bt, U, Q)
                    tT[1] = less(Tm, 1, bt, tq)
                tU = [less(U, p, bank[p], [tQf[p], tq]) for p in range(2)]
                tQf = [[t, tq] for t in tQf]
            yield tU, tvs
            X, Y_, W = bank
            sl = lambda h: slice(128 * h, 128 * h + 128)
            h4 = lambda bk: bk.t[:].rearrange("p (h n) -> p h n", h=4)

            def strong(c, t):
                r = [af(v[:, h, c, :], Y_.t[:, sl(h)], AF.Copy, t, scale=bp[:, 2 * h + c:2 * h + c + 1]) for h in range(4)]
                Y_.free = r[-1:]
                return r
            for h in range(4):
                t = mm(Y_.t[:, sl(h)], U[:, 2 * h, :], v[:, h, 0, :], h == 0, h == 3, tU, tvs, Y_.free)
            t0 = strong(0, t)
            tq = af(Tm[:].rearrange("p (h c) n -> p h c n", h=4), kq[:, :, :, 1, :], AF.Square, tT, tQf, scale=0.128)
            yield t0
            for h in range(4):
                t = mm(Y_.t[:, sl(h)], KA[:, 0, h, :], v[:, h, 0, :], h == 0, h == 3, t0, Y_.free)
            t1 = tt(v[:, :, 1, :], v[:, :, 1, :], h4(Y_), OP.subtract, t)
            Y_.free = [t1]
            for h in range(4):
                bk, o_ = (X, W)[h // 2], 256 * (h % 2)
                mm(bk.t[:, o_:o_ + 128], v[:, h, 0, :], MA[:, 1, 2 * h, :], h % 2 == 0, False, t0, tA, bk.free)
                mm(bk.t[:, o_ + 128:o_ + 256], v[:, h, 0, :], KA[:, 1, h, :], False, False)
            yield t1
            for h in range(4):
                t = mm(Y_.t[:, sl(h)], U[:, 2 * h + 1, :], v[:, h, 1, :], h == 0, h == 3, t1, Y_.free)
            t1 = strong(1, t)
            yield t1
            to = []
            for h in range(4):
                bk, o_ = (X, W)[h // 2], 256 * (h % 2)
                t = mm(bk.t[:, o_ + 128:o_ + 256], v[:, h, 1, :], MA[:, 1, 2 * h + 1, :], False, h % 2 == 1, t1)
                if h % 2:
                    to.append(t)
            sqd = Q[:].rearrange("p (h c) n -> p h (c n)", h=4)
            q2 = Tm[:].rearrange("p (h c) n -> p h (c n)", h=4)
            tc, ts_ = [], []
            for p, bk in enumerate((X, W)):
                i = bk.t[:].rearrange("p (h n) -> p h n", h=2)
                t = af(sqd[:, 2 * p:2 * p + 2, :], i, AF.Square, to[p], tQf)
                r = acp(odn[:, 4 * g + 2 * p:4 * g + 2 * p + 2, :], i, to[p], xa_done())
                bk.free = [t, r]
                tc.append(r)
                ts_.append(tt(sqd[:, 2 * p:2 * p + 2, :], sqd[:, 2 * p:2 * p + 2, :], q2[:, 2 * p:2 * p + 2, :], OP.add, t, tq))
            yield ts_
            rn = U[:].rearrange("p (h c) n -> p h (c n)", h=4)
            for p in range(2):
                bk = (Y_, X)[p]
                for a in range(2):
                    t = mm(bk.t[:, 256 * a:256 * a + 256], ONE, sqd[:, 2 * p + a, :], a == 0, a == 1, ts_[p], bk.free)
                r = af(pa(rn[:, 2 * p:2 * p + 2, :]), bk.t[:], AF.Ln, t, bias=P.ccol["eps_q"], scale=1.0 / 128)
                bk.free = [r]
            t = af(rn, rn, AF.Exp, r, scale=-0.5)
            o4 = odn[:, 4 * g:4 * g + 4, :]
            done["dn", g] = stt(o4, o4, col("dn_norm_2", l), rn, OP.mult, OP.mult, t, tc)

        def memory(h):
            bk = B[3 + h % 2]
            yield from need(("xq", h), "score")
            yield done["xq", h], bk.free
            w = [done["xq", h], P.kv_tok]
            for b in range(2):
                for k in range(2):
                    t = mm(bk.t[:, 256 * b:256 * b + 256], xq[:, 2 * h + k, 128 * b:128 * b + 128], mk[:, 2 * h + k, :],
                           b == 0 and k == 0, b == 1 and k == 1, w, bk.free)
            m2, n2, s2 = mx[:, 2 * h:2 * h + 2], nmx[:, 2 * h:2 * h + 2], sums[:, 2 * h:2 * h + 2]
            p_, pt = PM[h % 2], PM[2 + h % 2]
            t = red(m2, bk.t[:].rearrange("p (b n) -> p b n", b=2), OP.max, t, P.sm_free)
            t = ts(n2, m2, -1.0 / 16, None, OP.mult, None, t)
            yield t
            for b in range(2):
                t2 = af(p_[:, 256 * b:256 * b + 256], bk.t[:, 256 * b:256 * b + 256], AF.Exp, t, pt_free[h % 2], done["tokm"],
                        bias=n2[:, b:b + 1], scale=1.0 / 16, accum=s2[:, b:b + 1])
            t = rcp(s2, s2, t2)
            p3 = p_[:].rearrange("p (b n) -> p b n", b=2)
            t = [af(p3[:, b, :], p3[:, b, :], AF.Copy, t, scale=s2[:, b:b + 1]) for b in range(2)]
            yield t
            for k in range(2):
                for b in range(2):
                    t2 = tp(bk.t[:, 256 * k + 128 * b:256 * k + 128 * b + 128], p_[:, 256 * b + 128 * k:256 * b + 128 * k + 128], t)
            t = acp(pt[:], bk.t[:], t2, pt_free[2 + h % 2])
            pt_free[h % 2] = [t2]
            yield t
            for j in range(2):
                for k in range(2):
                    t2 = mm(bk.t[:, 256 * j:256 * j + 256], mv[:, k, 256 * h + 128 * j:256 * h + 128 * j + 128],
                            pt[:, 256 * k:256 * k + 256], j == 0 and k == 0, j == 1 and k == 1, t)
            pt_free[2 + h % 2] = [t2]
            r = acp(pa(xq[:, 2 * h:2 * h + 2, :]), bk.t[:], t2)
            bk.free = [r]
            done["xa", h] = r
            if all(("xa", i) in done for i in range(4)):
                done["xa"] = xa_done()
                split_o(XA, xq, "xa")

        pt_free = [[], [], [], []]

        def chosen(h):
            bk = B[3 + h % 2]
            yield from need("maskb", "xa", ("dn", 0), ("rk", h // 2), ("sv_", h // 2))
            yield done["rq", h // 2], done["rk", h // 2], bk.free
            S = 128 ** -0.5
            w = [done["rq", h // 2], done["rk", h // 2]]
            for b in range(2):
                n = 128 * (b + 1)
                t = mm(bk.t[:, 128 * b:128 * b + n], sq_[:, h, 128 * b:128 * b + 128], sk_[:, h, 0:n], b == 0, b == 1, w, bk.free)
            m2, n2, s2 = mx[:, 2 * h:2 * h + 2], nmx[:, 2 * h:2 * h + 2], sums[:, 2 * h:2 * h + 2]
            p_, pt = PC[h % 2], PC[2 + h % 2]
            tb = []
            for b in range(2):
                o_, n = 128 * b, 128 * (b + 1)
                tb.append(P.dve.do(lambda e, b=b, o_=o_, n=n: e.tensor_tensor_reduce(
                    out=p_[:, o_:o_ + n], in0=bk.t[:, o_:o_ + n], in1=score[:, o_:o_ + n], op0=OP.add, op1=OP.max, scale=S,
                    scalar=-3e38, accum_out=m2[:, b:b + 1]), t, done["maskb"], pt_free[h % 2], done["dn", 0], done["xa"]))
            t = ts(n2, m2, -1.0, None, OP.mult, None, tb)
            yield t
            for b in range(2):
                o_, n = 128 * b, 128 * (b + 1)
                t2 = af(p_[:, o_:o_ + n], p_[:, o_:o_ + n], AF.Exp, t, bias=n2[:, b:b + 1], accum=s2[:, b:b + 1])
            t = rcp(s2, s2, t2)
            for b in range(2):
                o_, n = 128 * b, 128 * (b + 1)
                t3 = ts(p_[:, o_:o_ + n], p_[:, o_:o_ + n], s2[:, b:b + 1], None, OP.mult, None, t)
            yield t3
            for i in range(3):
                t2 = tp(bk.t[:, 128 * i:128 * i + 128], p_[:, 128 * i:128 * i + 128], t3, tb)
            t = acp(pt[:, 0:384], bk.t[:, 0:384], t2, pt_free[2 + h % 2], done["dn", 0])
            pt_free[h % 2] = [t2]
            yield t
            mm(bk.t[:, 0:256], sv_[:, 0, 128 * h:128 * h + 128], pt[:, 0:256], True, False, t, done["sv_", h // 2])
            t2 = mm(bk.t[:, 128:256], sv_[:, 1, 128 * h:128 * h + 128], pt[:, 256:384], False, True)
            pt_free[2 + h % 2] = [t2]
            r = acp(sq_[:, h, :], bk.t[:, 0:256], t2)
            bk.free = [r]
            done["sa", h] = r
            if all(("sa", i) in done for i in range(8)):
                done["sa"] = P.maskb_free = [done["sa", i] for i in range(8)]
                split_o(SA, sq_, "sa")

        xa_done = lambda: [done["xa", h] for h in range(4)]

        def ev_copy(name, dst, base, *w):
            def f(xp, b, c, t):
                j = (c - base) // 128
                done[name, j // 2] = r = acp(pa(dst[:, j:j + 2, :]), b[:], t, *[u() for u in w])
                return r
            return f

        rtmp = relu[0:32, :].rearrange("p (n t) -> p n t", n=2)

        def ev_rope(name, dst, base, *w):
            def f(xp, b, c, t):
                j = (c - base) // 128
                r = acp(pa(dst[:, j:j + 2, :]), b[:], t, *[u() for u in w])
                done["r" + name, j // 2] = done["rtmp"] = rotate(dst[0:32, j:j + 2, :], 2, 0, rtmp, SW16, r, done["maskb"],
                                                               done.get("rtmp"))
                return r
            return f

        def ev_tm(name, dst, base, *w):
            def f(xp, b, c, t):
                j = c - base
                done[name, j // 256] = r = acp(dst[:, :, j:j + 256], b[:].rearrange("p (a n) -> p a n", a=2), t, *[u() for u in w])
                return r
            return f

        def ev_z(xp, b, c, t):
            j = (c - 3072) // 128
            z = zt[(j // 2) % 2]
            t = af(pa(z[:]), b[:], AF.Silu, t, done["dn", 1], done.get(("z", j // 2 - 2)))
            o_ = pa(odn[:, j:j + 2, :])
            done["z", j // 2] = r = tt(o_, o_, pa(z[:]), OP.mult, t, done["dn", 0], done["dn", 1])
            split2(DN, j, o_, r)
            return t

        def split2(part, j, src, *w):
            hi, lo = pa(part.hi[:, j:j + 2, :]), pa(part.lo[:, j:j + 2, :])
            th = acp(hi, src, *w)
            tl = tt(lo, src, hi.bitcast(F32), OP.subtract, th, *w)
            part.tok[j] = part.tok[j + 1] = [th, tl]

        def ev_gl(br):
            def f(xp, b, c, t):
                j = (c - 8792 - 1024 * br) // 128
                for a in range(2):
                    k = 24 * l + 8 * br + j + a
                    r = af(gate[:, (j + a) % 4, :], b[:, 256 * a:256 * a + 256], AF.Tanh, t, done.get(("gm", j % 4)), done["score"],
                           P.hb_tok, bias=hb[:, k:k + 1], scale=0.5)
                done["g", j % 4] = r
                return r
            return f

        def ev_br(br, first, last):
            def f(xp, b, c, t):
                j = c // 128
                g2, m2 = pa(gate[:, j % 4:j % 4 + 2, :]), pa(mg[:, j:j + 2, :])
                if first:
                    done["gm", j % 4] = done["m", j] = r = stt(m2, g2, 1.0, b[:], OP.add, OP.mult, t, done["g", j % 4], done["xa"])
                    return r
                r = stt(g2, g2, 1.0, b[:], OP.add, OP.mult, t, done["g", j % 4])
                done["gm", j % 4] = done["m", j] = t = tt(m2, m2, g2, OP.add, r, done["m", j])
                if last:
                    split2(MG, j, m2, t)
                return r
            return f

        def gl(br, i):
            return (f"gl{br}", l, i), w_in, 8792 + 1024 * br + 512 * i, [H], False, ev_gl(br)

        def wb(br, i, part, first=False, last=False):
            return (f"wb{br}", l, i), A["w_branch_2"][l, br], 512 * i, [part], False, ev_br(br, first, last)

        def split_o(part, o_, key):
            for j in range(0, KT, 2):
                split2(part, j, pa(o_[:, j:j + 2, :]), done[key])

        if l == 0:
            P.most = 0
        P.call(mix_scaled)
        P.lanes += [Lane(strengths(), delta(0), delta(1)),
                   Lane(index(), memory(0), memory(2), chosen(0), chosen(2), chosen(4), chosen(6)),
                   Lane(*([last_x(done)] if l == 0 else []), memory(1), memory(3), best(), chosen(1), chosen(3), chosen(5), chosen(7))]
        P.ready(lambda: P.wsm, narrow)
        def inp(name, c0, i, evac, tm=False):
            return (name, l, i), w_in, c0 + 512 * i, [H], tm, evac
        dk, dq, dv = (lambda g, n=n, c0=c0, kind=kind: inp(n, c0, g, conv_in(kind, g))
                      for n, c0, kind in (("dk", 1024, 1), ("dq", 0, 0), ("dv", 2048, 2)))
        e_xq, e_sv = ev_copy("xq", xq, 7768), ev_tm("sv_", sv_, 6160)
        e_sq, e_sk = ev_rope("q", sq_, 4112), ev_rope("k", sk_, 5136, lambda: [done["dn", 0]])

        def ev_iq(xp, b, c, t):
            j = (c - 7184) // 128
            done["iq", j // 2] = r = times_root(iq[:, j:j + 2, :], b[:].rearrange("p (a t) -> p a t", a=2), t, P.narrow_read)
            return r
        units(("iq", l, 0), w_in, 7184, [HM], False, ev_iq)
        P.call(lambda: normed(lambda k: gmix(k)[0], *gmix(0)[1:]), back=4)
        units(*dk(0))
        units(*dq(0))
        mixed(inp("xq", 7768, 0, e_xq), dv(0))
        units(*inp("xq", 7768, 1, e_xq))
        P.until(done, "score")
        mixed(dk(1), gl(2, 0))
        mixed(dq(1), dv(1))
        P.until(done, "xa")
        units(*wb(2, 0, XA, first=True))
        units(*gl(2, 1))
        units(*wb(2, 1, XA, first=True))
        mixed(inp("sv", 6160, 0, e_sv, True), inp("sq", 4112, 0, e_sq))
        P.until(done, ("dn", 0))
        mixed(inp("sv", 6160, 1, e_sv, True), inp("sk", 5136, 0, e_sk))
        units(*inp("sq", 4112, 1, e_sq))
        units(*inp("sk", 5136, 1, e_sk))
        units(*gl(1, 0))
        P.until(done, ("dn", 1))
        for i in range(2):
            units(*inp("dz", 3072, i, ev_z))
        P.until(done, "sa")
        units(*wb(1, 0, SA))
        units(*gl(1, 1))
        units(*wb(1, 1, SA))
        for i in range(2):
            units(*gl(0, i))
            units(*wb(0, i, DN, last=True))

        def ev_o(xp, b, c, t):
            j = c // 128
            x2 = pa(x[:, j:j + 2, :])
            P.x_tok[j] = P.x_tok[j + 1] = r = stt(x2, b[:], 0.5, x2, OP.mult, OP.add, t)
            for k in (j, j + 1):
                scaled(HF, k, col("norm_ffn_2", 8 * l + k))
            square(j, 2, r)
            return r
        P.call(lambda: af(P.small[:, 476:477], EPS, AF.Ln))
        for i in range(2):
            units(("wo", l, i), A["w_out_2"][l], 512 * i, [MG], False, ev_o)

        def next_loads():
            w = [P.x_tok[k] for k in range(KT)]
            P.lanes.append(Lane(small_weights(P, 1, w)))
            P.kv_tok = P.load(P.mkv[:], A["kv"], w, P.kv_done, q=P.pool)

        def ffn_norm():
            root(total(B[7], hsq, sqt), EPS)
            normed(lambda k: col("norm_ffn_2", 8 * l + k))
        if l == 0:
            P.call(next_loads)

        def ev_g(i):
            def f(xp, b, c, t):
                j = c // 128 - 4 * i
                o_ = fg[i % 2][:, j:j + 2, :]
                if i == 0:
                    r = times_root(o_, b[:, 0:512].rearrange("p (a t) -> p a t", a=2), t)
                    done["fg", i, j // 2] = af(o_, o_, AF.Silu, r)
                else:
                    done["fg", i, j // 2] = r = af(pa(o_), b[:, 0:512], AF.Silu, t, done.get(("fu", i - 2, j // 2)))
                return r
            return f

        def ev_u(i):
            def f(xp, b, c, t):
                j = (c - 2816) // 128 - 4 * i
                n = done.get("nf", 0)
                done["nf"] = n + 1
                a_ = fa[n % 2]
                r = tt(a_[:], b[:, 0:512], pa(fg[i % 2][:, j:j + 2, :]), OP.mult, t, done["fg", i, j // 2], ffa_free[n % 2])
                done["fu", i, j // 2] = r
                k0 = 4 * i + j
                th = acp(pa(FH[:, k0:k0 + 2, :]), a_[:], r)
                tl = tt(pa(FL[:, k0:k0 + 2, :]), a_[:], pa(FH[:, k0:k0 + 2, :]).bitcast(F32), OP.subtract, th)
                ffa_free[n % 2] = [th, tl]
                for a in range(2):
                    ftok[k0 + a] = [th, tl]
                return r
            return f
        ffa_free, ftok = [[], []], {}
        for i in range(5):
            units(("fg", l, i), A["w_ffn_in_2"][l], 512 * i, [H] if i else [HF], False, ev_g(i))
            if i == 0:
                P.call(ffn_norm, back=3)
            units(("fu", l, i), A["w_ffn_in_2"][l], 2816 + 512 * i, [H], False, ev_u(i))
        for n, ev, c0 in (("fg", ev_g(5), 2560), ("fu", ev_u(5), 5376)):
            P.columns((n, l, 5), A["w_ffn_in_2"][l], c0)
            P.unit((n, l, 5), [H], False, lambda xp, b, t, c=c0, ev=ev: ev(xp, b, c, t))
        acc = [B[4 + i] for i in range(4)]

        def ffn_out(k):
            def f(q):
                for j in range(8):
                    bk = acc[j // 2]
                    for w, v, wt in ((q.hi, FH, q.th), (q.hi, FL, q.th), (q.lo, FH, q.tl)):
                        t = mm(bk.t[:, 256 * (j % 2):256 * (j % 2) + 256], w[:, 0, 128 * j:128 * j + 128], v[:, k, :],
                               k == 0 and j % 2 == 0 and v is FH and w is q.hi, k == 21 and w is q.lo, wt, ftok[k],
                               bk.free if k == 0 else None)
                    if k == 21 and j % 2:
                        x2 = pa(x[:, j - 1:j + 1, :])
                        r = tt(x2, x2, bk.t[:], OP.add, t)
                        bk.free = [r]
                        P.x_tok[j - 1] = P.x_tok[j] = r
                return t
            return f
        P.call(lambda: af(P.small[:, 476:477], EPS, AF.Ln))
        if l == 0:
            P.call(lambda: layer(1))
        for i in range(11):
            P.want(("fo", l, i), [P.block(A["w_ffn_out_2"][l], 0, n=1024, k0=2 * i, kt=2)])
            for k in range(2):
                P.quarter(("fo", l, i), 1, lambda s, k=k: s[:, 1024 * k:1024 * k + 1024].unsqueeze(1), k == 1, ffn_out(2 * i + k))

    P.alog_free, P.maskb_free, P.sm_free = [], [], []
    layer(0)
    P.run(1)
    P.drain()
    last_norm()
    return fin


def build(nc, A, out):
    with ExitStack() as ctx:
        A = dict(A, kv=nc.dram_tensor("kv", (128, 4096), F32, kind="Internal").ap())
        P = Program(nc, A, ctx)
        phase_a(P)
        P.run(2)
        phase_b(P)
        P.run(2)
        P.drain()
        P.finish(phase_c(P, out), P.kv_done)


def fm(a):
    return np.ascontiguousarray(a.T.reshape(-1, 128, a.shape[0]).transpose(1, 0, 2))


def layout(inp):
    g = {k: np.asarray(v) for k, v in inp.items()}
    d = {"xT": fm(g["x"][0]), "ctxT": fm(g["ctx"][0]), "cst": constants()}
    d["cols"] = np.ascontiguousarray(np.concatenate([g[n].reshape(-1, 128).T for n, _ in COLS], axis=1))
    d["w_mod"], d["w_in"] = g["w_mod"][0], g["w_in"][0]
    d["w_lr"] = np.ascontiguousarray(g["w_in"][0][:, 5120:5152].reshape(8, 128, 32).transpose(1, 0, 2))
    d["w_gate2"] = g["w_gate2"][0]
    d["sgu_wT"] = np.ascontiguousarray(g["sgu_w"][0].transpose(2, 0, 1))
    d["sgu_b"] = g["sgu_b"][0]
    d["memT"] = fm(g["mem_2"][0])
    d["w_mem_kv"], d["w_router"] = g["w_mem_kv_2"], np.ascontiguousarray(g["w_router"].reshape(8, 128, 16).transpose(1, 0, 2))
    d["b_router"] = g["b_router"]
    d["w_eg"], d["w_eu"], d["w_ed"] = g["w_exp_gate"][0], g["w_exp_up"][0], g["w_exp_down"][0]
    d["cstc"] = constants_c()
    d["positions"] = g["positions_2"][0]
    d["w_in_2"] = w = g["w_in_2"]
    pk = lambda a: np.ascontiguousarray(a.reshape(8, 128, -1).transpose(1, 0, 2))
    d["w_small"] = np.stack([np.concatenate([pk(w[i][:, c:c + n]) for c, n in ((7696, 64), (4104, 8), (4096, 8), (7760, 8))], axis=2)
                             for i in range(2)])
    d["a_log"], d["dt_bias"] = g["a_log_2"].reshape(2, 8, 1), g["dt_bias_2"].reshape(2, 8, 1)
    d["w_branch_2"], d["w_out_2"] = g["w_branch_2"], g["w_out_2"]
    d["w_ffn_in_2"], d["w_ffn_out_2"] = g["w_ffn_in_2"], g["w_ffn_out_2"]
    d["w_a"], d["w_b"], d["w_o"] = g["w_branch_a"][0], g["w_branch_b"][0], g["w_out"][0]
    return d


def kernel(**inputs):
    import concourse.bacc as _bacc
    from concourse.bass_utils import run_bass_kernel_spmd as _run

    nc = _bacc.Bacc("TRN2", target_bir_lowering=False, num_devices=1)
    arrays, aps = {}, {}
    for name, a in layout(inputs).items():
        arrays[f"in_{name}_dram"] = a = np.ascontiguousarray(a)
        aps[name] = nc.dram_tensor(f"in_{name}_dram", a.shape, mybir.dt.from_np(a.dtype), kind="ExternalInput").ap()
    out = nc.dram_tensor("out_0_dram", (128, KT, T), F32, kind="ExternalOutput").ap()
    build(nc, aps, out)
    r = _run(nc, [arrays], core_ids=[0])
    o = r.results[0]["out_0_dram"]
    return np.ascontiguousarray(o.transpose(2, 1, 0)).reshape(1, T, 1024)
```
